# Optimizing a Trainium2 kernel written in Bass

```python
import jax, jax.numpy as jnp
from jax import lax
import numpy as np

D_MODEL = 2048
BATCH = 1
SEQ = 256
DEPTH = 1

CHUNK = 64
HEAD_DIM = 64
N_Q_HEADS = 16
N_KV_HEADS = 4
Q_PER_KV = N_Q_HEADS // N_KV_HEADS
ATTN_WINDOW = 128
WIN_CHUNKS = ATTN_WINDOW // CHUNK
ATTN_WIDTH = N_Q_HEADS * HEAD_DIM
KV_WIDTH = N_KV_HEADS * HEAD_DIM
SGU_BLOCK = 128
SGU_GROUPS = 8
SGU_GROUP_DIM = 128
SGU_WIDTH = SGU_GROUPS * SGU_GROUP_DIM
SGU_OFFSET = ATTN_WIDTH + 2 * KV_WIDTH
IN_WIDTH = SGU_OFFSET + 2 * SGU_WIDTH
N_BRANCHES = 2
N_GROUPS = 4
EXPERTS_PER_GROUP = 8
N_EXPERTS = N_GROUPS * EXPERTS_PER_GROUP
TOP_K_IN_GROUP = 2
EXPERT_FF = 256
NORM_EPS = 1e-6
NEG_INF = -1e30

kernel_name = "hybrid_swa_sink_sgu_hmoe_block"

def rms_norm(x, g):
    xf = x.astype(jnp.float32)
    y = xf * lax.rsqrt(jnp.mean(xf * xf, axis=-1, keepdims=True) + NORM_EPS)
    return (y * g.astype(jnp.float32)).astype(x.dtype)

def sliding_window_sink_attention(q, k, v, sinks):
    b, s = q.shape[:2]
    nc = s // CHUNK
    qc = q.reshape(b, nc, CHUNK, N_KV_HEADS, Q_PER_KV, HEAD_DIM)
    kc = k.reshape(b, nc, CHUNK, N_KV_HEADS, HEAD_DIM)
    vc = v.reshape(b, nc, CHUNK, N_KV_HEADS, HEAD_DIM)

    def band(t):
        padded = jnp.pad(t, ((0, 0), (WIN_CHUNKS - 1, 0), (0, 0), (0, 0), (0, 0)))
        return jnp.concatenate([padded[:, o:o + nc] for o in range(WIN_CHUNKS)], axis=2)

    kb, vb = band(kc), band(vc)
    key_chunk = (jnp.arange(nc)[:, None] - (WIN_CHUNKS - 1)
                 + jnp.arange(WIN_CHUNKS * CHUNK)[None, :] // CHUNK)
    valid = key_chunk >= 0
    scores = jnp.einsum('bcqkgd,bcjkd->bckgqj', qc.astype(jnp.float32),
                        kb.astype(jnp.float32)) * (HEAD_DIM ** -0.5)
    scores = jnp.where(valid[None, :, None, None, None, :], scores, NEG_INF)
    sink = sinks.astype(jnp.float32).reshape(N_KV_HEADS, Q_PER_KV)[None, None, :, :, None, None]
    m = jnp.maximum(jnp.max(scores, axis=-1, keepdims=True), sink)
    p = jnp.exp(scores - m)
    denom = jnp.sum(p, axis=-1, keepdims=True) + jnp.exp(sink - m)
    out = jnp.einsum('bckgqj,bcjkd->bcqkgd', p / denom, vb.astype(jnp.float32))
    return out.reshape(b, s, ATTN_WIDTH).astype(q.dtype)

def chunked_spatial_gating(u, v, norm_v_g, w_spatial, b_spatial):
    b, s = u.shape[:2]
    nb = s // SGU_BLOCK
    vn = rms_norm(v, norm_v_g).reshape(b, nb, SGU_BLOCK, SGU_GROUPS, SGU_GROUP_DIM)
    pos = jnp.arange(SGU_BLOCK)
    mask = (pos[:, None] // CHUNK) >= (pos[None, :] // CHUNK)
    w = jnp.where(mask[None], w_spatial, 0)
    mixed = jnp.einsum('gij,bcjgd->bcigd', w, vn) + b_spatial.T[None, None, :, :, None]
    return u * mixed.reshape(b, s, SGU_WIDTH)

def hierarchical_moe(xn, w_router_group, b_router_group, w_router_expert, b_router_expert,
                     w_e_gate, w_e_up, w_e_down):
    b, s, d = xn.shape
    t = xn.reshape(b * s, d)
    group_prob = jax.nn.softmax((t @ w_router_group + b_router_group).astype(jnp.float32), axis=-1)
    g_val, g_idx = lax.top_k(group_prob, 1)
    exp_logits = (t @ w_router_expert + b_router_expert).astype(jnp.float32)
    exp_logits = exp_logits.reshape(-1, N_GROUPS, EXPERTS_PER_GROUP)
    in_group = jnp.take_along_axis(exp_logits, g_idx[:, :, None], axis=1)[:, 0]
    e_val, e_idx = lax.top_k(in_group, TOP_K_IN_GROUP)
    e_w = jax.nn.softmax(e_val, axis=-1) * g_val
    global_idx = g_idx * EXPERTS_PER_GROUP + e_idx
    combine = jnp.einsum('nk,nke->ne', e_w,
                         jax.nn.one_hot(global_idx, N_EXPERTS, dtype=jnp.float32)).astype(t.dtype)
    out = jnp.zeros_like(t)
    for grp in range(N_GROUPS):
        sl = slice(grp * EXPERTS_PER_GROUP, (grp + 1) * EXPERTS_PER_GROUP)
        hid = (jax.nn.silu(jnp.einsum('nd,edf->nef', t, w_e_gate[sl]))
               * jnp.einsum('nd,edf->nef', t, w_e_up[sl]))
        out = out + jnp.einsum('nef,efd->nd', hid * combine[:, sl, None], w_e_down[sl])
    return out.reshape(b, s, d)

def setup_inputs(seed: int = 0) -> dict:
    key = jax.random.key(seed)
    ks = jax.random.split(key, 24)
    f32 = jnp.float32
    L, D = DEPTH, D_MODEL

    def nrm(k, shape, scale):
        return jax.random.normal(k, shape, f32) * scale

    return {
        "x": nrm(ks[0], (BATCH, SEQ, D), 1.0),
        "norm_mix_g": 1.0 + nrm(ks[1], (L, D), 0.02),
        "w_in": nrm(ks[2], (L, D, IN_WIDTH), D ** -0.5),
        "b_in": nrm(ks[3], (L, IN_WIDTH), 0.01),
        "attn_sinks": nrm(ks[4], (L, N_Q_HEADS), 0.5),
        "norm_v_g": 1.0 + nrm(ks[5], (L, SGU_WIDTH), 0.02),
        "w_spatial": nrm(ks[6], (L, SGU_GROUPS, SGU_BLOCK, SGU_BLOCK), SGU_BLOCK ** -0.5),
        "b_spatial": 1.0 + nrm(ks[7], (L, SGU_GROUPS, SGU_BLOCK), 0.1),
        "w_gate": nrm(ks[8], (L, D, N_BRANCHES * D), D ** -0.5),
        "b_gate": nrm(ks[9], (L, N_BRANCHES * D), 0.01),
        "w_branch_a": nrm(ks[10], (L, ATTN_WIDTH, D), ATTN_WIDTH ** -0.5),
        "w_branch_b": nrm(ks[11], (L, SGU_WIDTH, D), SGU_WIDTH ** -0.5),
        "w_out": nrm(ks[12], (L, D, D), D ** -0.5),
        "norm_ffn_g": 1.0 + nrm(ks[13], (L, D), 0.02),
        "w_router_group": nrm(ks[14], (L, D, N_GROUPS), D ** -0.5),
        "b_router_group": nrm(ks[15], (L, N_GROUPS), 0.01),
        "w_router_expert": nrm(ks[16], (L, D, N_EXPERTS), D ** -0.5),
        "b_router_expert": nrm(ks[17], (L, N_EXPERTS), 0.01),
        "w_e_gate": nrm(ks[18], (L, N_EXPERTS, D, EXPERT_FF), D ** -0.5),
        "w_e_up": nrm(ks[19], (L, N_EXPERTS, D, EXPERT_FF), D ** -0.5),
        "w_e_down": nrm(ks[20], (L, N_EXPERTS, EXPERT_FF, D), EXPERT_FF ** -0.5),
        "norm_final_g": 1.0 + nrm(ks[21], (D,), 0.02),
    }

def reference(x, norm_mix_g, w_in, b_in, attn_sinks, norm_v_g, w_spatial, b_spatial,
              w_gate, b_gate, w_branch_a, w_branch_b, w_out, norm_ffn_g,
              w_router_group, b_router_group, w_router_expert, b_router_expert,
              w_e_gate, w_e_up, w_e_down, norm_final_g):
    b, s, _ = x.shape
    h = x
    for l in range(DEPTH):
        xn = rms_norm(h, norm_mix_g[l])
        proj = xn @ w_in[l] + b_in[l]
        q = proj[..., :ATTN_WIDTH].reshape(b, s, N_Q_HEADS, HEAD_DIM)
        k = proj[..., ATTN_WIDTH:ATTN_WIDTH + KV_WIDTH].reshape(b, s, N_KV_HEADS, HEAD_DIM)
        v = proj[..., ATTN_WIDTH + KV_WIDTH:SGU_OFFSET].reshape(b, s, N_KV_HEADS, HEAD_DIM)
        sgu_in = jax.nn.gelu(proj[..., SGU_OFFSET:])
        u_sgu, v_sgu = sgu_in[..., :SGU_WIDTH], sgu_in[..., SGU_WIDTH:]

        y_a = sliding_window_sink_attention(q, k, v, attn_sinks[l])
        y_b = chunked_spatial_gating(u_sgu, v_sgu, norm_v_g[l], w_spatial[l], b_spatial[l])

        gates = jax.nn.sigmoid(xn @ w_gate[l] + b_gate[l])
        g_a, g_b = gates[..., :D_MODEL], gates[..., D_MODEL:]
        merged = g_a * (y_a @ w_branch_a[l]) + g_b * (y_b @ w_branch_b[l])
        h = h + merged @ w_out[l]

        xn2 = rms_norm(h, norm_ffn_g[l])
        h = h + hierarchical_moe(xn2, w_router_group[l], b_router_group[l],
                                 w_router_expert[l], b_router_expert[l],
                                 w_e_gate[l], w_e_up[l], w_e_down[l])
    return rms_norm(h, norm_final_g)


_drawn_inputs = setup_inputs


def setup_inputs(seed=0):
    import zlib

    import numpy as np

    out = dict(_drawn_inputs(seed))
    spreads = {}
    factors = {'attn_sinks': 8.0,
     'b_gate': 7.261,
     'b_router_group': 43.125,
     'norm_final_g': 7.633,
     'b_in': 3.54,
     'norm_v_g': 3.661,
     'b_router_expert': 3.764}
    for name, (base, spread) in spreads.items():
        noise = np.random.default_rng([zlib.crc32(name.encode()), seed]).standard_normal(out[name].shape)
        drawn = base * np.exp(spread * noise) if base else spread * noise
        out[name] = __import__('jax').numpy.asarray(drawn.astype(out[name].dtype))
    for name, factor in factors.items():
        out[name] = (out[name] * factor).astype(out[name].dtype)
    return out
```

```python
from contextlib import ExitStack

import concourse.bass as bass
from concourse import mybir

F32 = mybir.dt.float32
F32R = mybir.dt.float32r
I32 = mybir.dt.int32
U32 = mybir.dt.uint32
ALU = mybir.AluOpType
ACT = mybir.ActivationFunctionType
AX_X = mybir.AxisListType.X

P = 128
KB = 1024
CHUNK, HEAD, Q_PER_KV = 64, 64, 4
COLS = 512
PIECE = 2048
ROUND = 4
EPS = 1e-6
DENSE_RAW, DENSE_PARTS = 4, 2
EXP_RAW, EXP_PARTS = 6, 3
LOWEST = -3.0e38


class Chain:

    def __init__(self, eng, sem, base=0):
        self.eng, self.sem, self.base, self.n = eng, sem, base, 0

    def mark(self, ins):
        self.n += 1
        return ins.then_inc(self.sem, 1)

    def wait(self):
        self.eng.wait_ge(self.sem, self.base + self.n)

    def link(self, ins):
        self.mark(ins)
        self.wait()


def build_trunk(nc, a, out):
    T, D = a["x"].shape[1], a["x"].shape[2]
    TT, KT = T // P, D // P
    IN_W = a["w_in"].shape[2]
    SGU_W = a["norm_v_g"].shape[1]
    NH = a["attn_sinks"].shape[1]
    NKV = NH // Q_PER_KV
    ATT_W, KV_W = NH * HEAD, NKV * HEAD
    K_OFF, V_OFF = ATT_W, ATT_W + KV_W
    U_OFF, VS_OFF = ATT_W + 2 * KV_W, ATT_W + 2 * KV_W + SGU_W
    SG = a["w_spatial"].shape[1]
    KB2 = SGU_W // P
    NG = a["w_router_group"].shape[2]
    NE = a["w_router_expert"].shape[2]
    EPG = NE // NG
    FF = a["w_e_gate"].shape[3]
    NR = NG + NE
    A1, A2 = 3, IN_W // COLS - 3
    NC = D // COLS
    C_ROUND0 = A1 + A2
    D_ROUND0 = C_ROUND0 + 3 * NC
    DENSE = ROUND * (D_ROUND0 + NC)
    PER_G = 6 * EPG
    assert TT == 2 and KT == 16 and A2 == NKV == 4 and NC == 4 and KB2 == 8 and SG == 8 and FF == 256
    SCALE = float(HEAD) ** -0.5

    with ExitStack() as ctx:
        base = (nc.sbuf_base + 31) // 32 * 32
        room = (nc.sbuf_usable_end - base) // 32 * 32
        ctx.enter_context(nc.sbuf_tensor("arena", [P, room // 4], F32))

        def at(name, kb, shape, dt=F32):
            nbytes = 4
            for n in shape[1:]:
                nbytes *= n
            assert kb * KB + nbytes <= room, name
            return nc.alloc_sbuf_tensor_at(name, shape, dt, offset=base + int(kb * KB))

        def sem(name):
            return ctx.enter_context(nc.semaphore(name))

        bank = [ctx.enter_context(nc.psum_tensor(f"bank{i}", [P, COLS], F32)) for i in range(8)]

        resid = at("resid", 0, [P, TT, D])
        wsp = at("wsp", 0, [P, SG, P])
        yat = at("yat", 0, [P, 2, T])
        wspT = at("wspT", 4, [P, SG, P])
        gv = at("gv", 8, [P, SGU_W])
        probT = [at(f"probT{b}", 12 + 2 * b, [P, 4, P]) for b in range(2)]
        whi = at("whi", 16, [P, EXP_PARTS, PIECE], F32R)
        wlo = at("wlo", 40, [P, EXP_PARTS, PIECE], F32R)
        actT_hi = at("actT_hi", 64, [P, KT, T], F32R)
        actT_lo = at("actT_lo", 80, [P, KT, T], F32R)
        x2_hi = actT_hi[:].rearrange("p k t -> p (k t)").rearrange("p (t d) -> p t d", t=TT)
        x2_lo = actT_lo[:].rearrange("p k t -> p (k t)").rearrange("p (t d) -> p t d", t=TT)
        raw = at("raw", 96, [P, DENSE_RAW, PIECE])
        x2 = at("x2", 96, [P, TT, D])
        x2T = at("x2T", 112, [P, KT, T])
        xg_hi = at("xg_hi", 96, [P, KT, P], F32R)
        xg_lo = at("xg_lo", 104, [P, KT, P], F32R)
        o_hi = at("o_hi", 112, [P, D], F32R)
        o_lo = at("o_lo", 120, [P, D], F32R)
        y_out = at("y_out", 96, [P, TT, D])
        xraw = at("xraw", 128, [P, EXP_RAW, PIECE])
        x0 = at("x0", 128, [P, TT, D])
        xs0 = at("xs0", 144, [P, TT, D])
        g1 = at("g1", 160, [P, D])
        sq0 = at("sq0", 168, [P, D])
        proj = at("proj", 128, [P, TT, IN_W])
        merged = at("merged", 128, [P, TT, D])
        sga = at("sga", 144, [P, TT, COLS])
        sgb = at("sgb", 148, [P, TT, COLS])
        gyb = at("gyb", 152, [P, TT, COLS])
        yaT_hi = at("yaT_hi", 156, [P, KB2, T], F32R)
        yaT_lo = at("yaT_lo", 164, [P, KB2, T], F32R)
        ybT_hi = at("ybT_hi", 172, [P, KB2, T], F32R)
        ybT_lo = at("ybT_lo", 180, [P, KB2, T], F32R)
        sq_v = at("sq_v", 172, [P, SGU_W])
        s_act = at("s_act", 176, [P, FF])
        hid = at("hid", 177, [P, FF])
        hT_hi = at("hT_hi", 178, [P, 2, P], F32R)
        hT_lo = at("hT_lo", 179, [P, 2, P], F32R)
        sel = at("sel", 180, [P, TT, P], F32R)
        selT = at("selT", 181, [P, T], F32R)
        sq2 = at("sq2", 180, [P, D])
        bias_a = at("bias_a", 188, [P, COLS])
        bias_b = at("bias_b", 190, [P, COLS])
        ident = at("ident", 192, [P, P])
        ident_r = at("ident_r", 192.5, [P, P], F32R)
        before = at("before", 193, [P, P])
        ones = at("ones", 193.5, [P, P])
        slot_no = at("slot_no", 194, [P, P])
        qkv = at("qkv", 194.5, [P, TT, (Q_PER_KV + 2) * HEAD])
        qT = at("qT", 197.5, [HEAD, T // CHUNK, Q_PER_KV, CHUNK])
        kT = at("kT", 201.5, [HEAD, T])
        prob = [at(f"prob{b}", 202.5 + 2 * b, [P, 4, P]) for b in range(2)]
        gbig = at("gbig", 196.875, [P, D])
        wr = at("wr", 194.5, [P, KT, NR])
        small_at = [206.5]

        def small(name, shape, dt=F32):
            n = 4
            for s in shape[1:]:
                n *= s
            t = at(name, small_at[0], shape, dt)
            small_at[0] += (n + 31) // 32 * 32 / KB
            return t

        ssq = small("ssq", [P, TT])
        ms = small("ms", [P, TT])
        rstd = small("rstd", [P, TT])
        credit = small("credit", [P, 8])
        bsT = small("bsT", [P, SG])
        sink_row = small("sink_row", [P, NH])
        sinkv = small("sinkv", [P, NKV, 2, 2])
        mx = small("mx", [P, 2, 4])
        nmx = small("nmx", [P, 2, 4])
        sdiff = small("sdiff", [P, 2, 4])
        rsum = small("rsum", [P, 2, 4])
        esink = small("esink", [P, 2, 4])
        rden = small("rden", [P, 2, 4])
        vmid = small("vmid", [P, HEAD])
        bs8 = at("bs8", 202.5, [SG, P])
        br = at("br", 188, [P, NR])

        def rsmall(name, shape, dt=F32):
            t = small(name, shape, dt)
            assert small_at[0] <= 192, name
            return t

        small_at[0] = 188.25
        lg = rsmall("lg", [P, TT, NR])
        gl8 = rsmall("gl8", [P, TT, 8])
        gm8 = rsmall("gm8", [P, TT, 8])
        gi8 = rsmall("gi8", [P, TT, 8], U32)
        gif = rsmall("gif", [P, TT, 8])
        ngm = rsmall("ngm", [P, TT])
        gexp = rsmall("gexp", [P, TT, NG])
        gsum = rsmall("gsum", [P, TT])
        gval = rsmall("gval", [P, TT])
        goh = rsmall("goh", [P, TT, NG])
        own = rsmall("own", [P, TT, NG, EPG])
        inl = rsmall("inl", [P, TT, EPG])
        em8 = rsmall("em8", [P, TT, 8])
        ei8 = rsmall("ei8", [P, TT, 8], U32)
        eif = rsmall("eif", [P, TT, 8])
        ed = rsmall("ed", [P, TT])
        ee = rsmall("ee", [P, TT])
        es1 = rsmall("es1", [P, TT])
        ew0 = rsmall("ew0", [P, TT])
        ew1 = rsmall("ew1", [P, TT])
        ca = rsmall("ca", [P, TT, EPG])
        cb = rsmall("cb", [P, TT, EPG])
        cw_hi = rsmall("cw_hi", [P, TT, EPG], F32R)
        cw_lo = rsmall("cw_lo", [P, TT, EPG], F32R)
        rkp = rsmall("rkp", [P, TT, NG])
        rank = rsmall("rank", [P, TT])
        fits = rsmall("fits", [P, TT])
        over = rsmall("over", [P, TT])
        rk1 = rsmall("rk1", [P, TT])
        rk2 = rsmall("rk2", [P, TT])
        pos = rsmall("pos", [P, TT, NG + 1])
        ovg = rsmall("ovg", [P, NG])
        ovn = rsmall("ovn", [P, NG])
        ctlf = rsmall("ctlf", [P, 2])
        ctl = rsmall("ctl", [P, 2], I32)
        cw = rsmall("cw", [P, EPG])

        x_in = [sem(f"x_in{t}") for t in range(TT)]
        g1_in, gv_in, wsp_in, bs_in, sink_in = (sem(n) for n in ("g1_in", "gv_in", "wsp_in", "bs_in", "sink_in"))
        raw_in = [sem(f"raw_in{s}") for s in range(DENSE_RAW)]
        xraw_in = [sem(f"xraw_in{s}") for s in range(EXP_RAW)]
        bias_a_in, bias_b_in = sem("bias_a_in"), sem("bias_b_in")
        resid_in, g2_in, wr_in, br_in, gf_in = (sem(n) for n in ("resid_in", "g2_in", "wr_in", "br_in", "gf_in"))
        out_done = sem("out_done")
        hi_made, lo_made, piece_used = sem("hi_made"), sem("lo_made"), sem("piece_used")
        consts, ident_r_made, small_made = sem("consts"), sem("ident_r_made"), sem("small_made")
        ssq_made, mean_made, ms_made, rstd_made = (sem(n) for n in ("ssq_made", "mean_made", "ms_made", "rstd_made"))
        xs_made, xT_full, xT_hi_made, xT_lo_made = sem("xs_made"), sem("xT_full"), sem("xT_hi_made"), sem("xT_lo_made")
        wspT_full, wspT_made = sem("wspT_full"), sem("wspT_made")
        acc_full, acc_free = sem("acc_full"), sem("acc_free")
        gb_full, gb_free = sem("gb_full"), sem("gb_free")
        ya_full, ya_free = sem("ya_full"), sem("ya_free")
        yb_full, yb_free = sem("yb_full"), sem("yb_free")
        ga_sig, gb_sig, gyb_made = sem("ga_sig"), sem("gb_sig"), sem("gyb_made")
        qkv_made, qkT_full, qkT_made, vmid_made = sem("qkv_made"), sem("qkT_full"), sem("qkT_made"), sem("vmid_made")
        sc_full, max_made, exp_made, prob_made = sem("sc_full"), sem("max_made"), sem("exp_made"), sem("prob_made")
        pT_full, pT_made, ya_t_full, yat_made = sem("pT_full"), sem("pT_made"), sem("ya_t_full"), sem("yat_made")
        yaT_hi_made, yaT_lo_made = sem("yaT_hi_made"), sem("yaT_lo_made")
        gelu_v, gelu_u, vn_made, mix_full, yb_made = (sem(n) for n in ("gelu_v", "gelu_u", "vn_made", "mix_full", "yb_made"))
        ybT_full, ybT_hi_made, ybT_lo_made = sem("ybT_full"), sem("ybT_hi_made"), sem("ybT_lo_made")
        mT_full, mT_hi_made, mT_lo_made = sem("mT_full"), sem("mT_hi_made"), sem("mT_lo_made")
        x2_made, x2T_full, x2T_a_made, x2T_v_made = sem("x2_made"), sem("x2T_full"), sem("x2T_a_made"), sem("x2T_v_made")
        x2_hi_made, x2_lo_made, lg_full = sem("x2_hi_made"), sem("x2_lo_made"), sem("lg_full")
        gmax_made, gexp_made, goh_made, rank_full = sem("gmax_made"), sem("gexp_made"), sem("goh_made"), sem("rank_full")
        ed_made, ee_made, cwparts_made, ctl_made = sem("ed_made"), sem("ee_made"), sem("cwparts_made"), sem("ctl_made")
        sel_made, selT_full, selT_made, cw_made = sem("sel_made"), sem("selT_full"), sem("selT_made"), sem("cw_made")
        xg_full, xg_hi_made, xg_lo_made = sem("xg_full"), sem("xg_hi_made"), sem("xg_lo_made")
        silu_made, hid_made = sem("silu_made"), sem("hid_made")
        hT_full, hT_hi_made, hT_lo_made = sem("hT_full"), sem("hT_hi_made"), sem("hT_lo_made")
        o_full, o_hi_made, o_lo_made = sem("o_full"), sem("o_hi_made"), sem("o_lo_made")
        scat_full, added = sem("scat_full"), sem("added")
        y_made = sem("y_made")
        v_order, v_att, v_c, pool_order = sem("v_order"), sem("v_att"), sem("v_c"), sem("pool_order")
        a_att = sem("a_att")

        block = ctx.enter_context(nc.Block())

        def await_used(eng, n):
            eng.wait_ge(piece_used, n + (DENSE_PARTS + 1))

        def await_chunk(eng, t, full, n, last_piece):
            if t == 0:
                eng.wait_ge(full, n + 1)
            else:
                await_used(eng, last_piece)

        x_v = a["x"].rearrange("b (t p) d -> p (b t) d", p=P)
        out_v = out.rearrange("b (t p) d -> p (b t) d", p=P)

        def chunked(w):
            return w[0].rearrange("(k p) (c n) -> p k c n", p=P, n=COLS)

        w_in_v, w_gate_v, w_out_v = chunked(a["w_in"]), chunked(a["w_gate"]), chunked(a["w_out"])
        w_a_v, w_b_v = chunked(a["w_branch_a"]), chunked(a["w_branch_b"])
        b_in_v = a["b_in"].rearrange("a (c n) -> a c n", n=COLS)
        b_gate_v = a["b_gate"].rearrange("a (c n) -> a c n", n=COLS)
        wg_v = a["w_e_gate"][0].rearrange("e (p k) f -> e p k f", p=P)
        wu_v = a["w_e_up"][0].rearrange("e (p k) f -> e p k f", p=P)
        wd_v = a["w_e_down"][0].rearrange("e (k p) d -> e p k d", p=P)

        def wide(row):
            return row.partition_broadcast(P).rearrange("p a n -> p (a n)")

        @block.sync
        def _(sp):
            def load_round(r, views):
                for k, (view, kt, c) in enumerate(views):
                    sp.wait_ge(lo_made, ROUND * r + k + 1)
                    for h in range(2):
                        sp.dma_start(raw[:, k, h * KB:(h + 1) * KB].rearrange("p (k n) -> p k n", n=COLS),
                                     view[:, kt + 2 * h:kt + 2 * h + 2, c, :]).then_inc(raw_in[k], 16)

            def full(view, c):
                return [(view, 4 * k, c) for k in range(4)]

            def load_bias(tile, row, arrived, freed, n):
                sp.wait_ge(freed, 2 * n + 2)
                sp.dma_start(tile[:], wide(row)).then_inc(arrived, 16)

            sp.dma_start(x0[:, 0, :], x_v[:, 0, :]).then_inc(x_in[0], 16)
            sp.dma_start(g1[:], wide(a["norm_mix_g"])).then_inc(g1_in, 16)
            sp.dma_start(x0[:, 1, :], x_v[:, 1, :]).then_inc(x_in[1], 16)
            sp.dma_start(wsp[:], a["w_spatial"][0].rearrange("g i j -> i g j")).then_inc(wsp_in, 16)
            sp.dma_start(bs8[:], a["b_spatial"][0]).then_inc(bs_in, 16)
            sp.dma_start(sink_row[:], wide(a["attn_sinks"])).then_inc(sink_in, 16)
            with sp.Fori(0, A1 + A2) as c:
                load_round(c, full(w_in_v, c))
                load_bias(bias_a, b_in_v[:, c, :], bias_a_in, acc_free, c)
            sp.dma_start(gv[:], wide(a["norm_v_g"])).then_inc(gv_in, 16)

            def load_c(n, extra=None):
                r = C_ROUND0 + 3 * n
                load_round(r, full(w_gate_v, n))
                load_bias(bias_a, b_gate_v[:, n, :], bias_a_in, acc_free, A1 + A2 + n)
                load_round(r + 1, full(w_gate_v, NC + n))
                load_bias(bias_b, b_gate_v[:, NC + n, :], bias_b_in, gb_free, n)
                load_round(r + 2, [(w_a_v, 0, n), (w_a_v, 4, n), (w_b_v, 0, n), (w_b_v, 4, n)])

            load_c(0)
            sp.wait_ge(ybT_lo_made, 4)
            for t in range(TT):
                sp.dma_start(resid[:, t, :], x_v[:, t, :]).then_inc(resid_in, 16)
            sp.wait_ge(yaT_lo_made, NKV)
            sp.dma_start(gbig[:], wide(a["norm_ffn_g"])).then_inc(g2_in, 16)
            sp.dma_start(wr[:, :, 0:NG], a["w_router_group"][0].rearrange("(p k) n -> p k n", p=P)).then_inc(wr_in, 16)
            sp.dma_start(wr[:, :, NG:NR], a["w_router_expert"][0].rearrange("(p k) n -> p k n", p=P)).then_inc(wr_in, 16)
            with sp.Fori(1, NC) as n:
                load_c(n)
            load_round(D_ROUND0, full(w_out_v, 0))

            def load_expert(i, e, m, kind, k):
                s, use = m % EXP_RAW, PER_G // EXP_RAW * i + m // EXP_RAW
                if kind == "gu":
                    for h, view in enumerate((wg_v, wu_v)):
                        sp.dma_start(xraw[:, s, h * KB:(h + 1) * KB].rearrange("p (k f) -> p k f", f=FF),
                                     view[e, :, 4 * k:4 * k + 4, :]).then_inc(xraw_in[s], 16)
                else:
                    for h in range(2):
                        sp.dma_start(xraw[:, s, h * KB:(h + 1) * KB],
                                     wd_v[e, :, k, h * KB:(h + 1) * KB]).then_inc(xraw_in[s], 16)

            def await_slot(i, m):
                sp.wait_ge(lo_made, DENSE_RAW + DENSE + PER_G * i + m - EXP_RAW + 1)

            sp.wait_ge(mT_lo_made, 2 * NC)
            for m in range(4):
                load_expert(0, 0, m, "gu", m)
            for k in range(2):
                load_expert(0, 1, 4 + k, "gu", k)
            with sp.Fori(1, NC) as n:
                load_round(D_ROUND0 + n, full(w_out_v, n))
            sp.wait_ge(acc_free, 2 * (A1 + A2 + 2 * NC) + 2)
            sp.dma_start(br[:, 0:NG], wide(a["b_router_group"])).then_inc(br_in, 16)
            sp.dma_start(br[:, NG:NR], wide(a["b_router_expert"])).then_inc(br_in, 16)
            sp.wait_ge(x2_made, TT)
            sp.dma_start(gbig[:], wide(a["norm_final_g"].rearrange("(a n) -> a n", a=1))).then_inc(gf_in, 16)

            def load_step(i, e, j, gu_from=0):
                for k in range(gu_from, 4):
                    await_slot(i, 6 * j - 2 + k)
                    load_at(i, e + j, j, k, "gu", k)
                for k in range(2):
                    await_slot(i, 6 * j + 2 + k)
                    load_at(i, e + j - 1, j, 4 + k, "down", k)

            def load_at(i, e, j, q, kind, k):
                s = (4 + q) % EXP_RAW
                if kind == "gu":
                    for h, view in enumerate((wg_v, wu_v)):
                        sp.dma_start(xraw[:, s, h * KB:(h + 1) * KB].rearrange("p (k f) -> p k f", f=FF),
                                     view[e, :, 4 * k:4 * k + 4, :]).then_inc(xraw_in[s], 16)
                else:
                    for h in range(2):
                        sp.dma_start(xraw[:, s, h * KB:(h + 1) * KB],
                                     wd_v[e, :, k, h * KB:(h + 1) * KB]).then_inc(xraw_in[s], 16)

            def load_tail(i, e):
                for k in range(2):
                    await_slot(i, PER_G - 2 + k)
                    load_expert(0, e + EPG - 1, PER_G - 2 + k, "down", k)

            def load_group(i, e):
                for k in range(4):
                    await_slot(i, k)
                    load_expert(0, e, k, "gu", k)
                with sp.Fori(1, EPG) as j:
                    load_step(i, e, j)
                load_tail(i, e)

            load_step(0, 0, 1, gu_from=2)
            with sp.Fori(2, EPG) as j:
                load_step(0, 0, j)
            load_tail(0, 0)
            with sp.Fori(1, NG) as i:
                load_group(i, i * EPG)
            sp.wait_ge(ctl_made, 1)
            more = sp.value_load(ctl[0:1, 0:1], min_val=0, max_val=1)
            group = sp.value_load(ctl[0:1, 1:2], min_val=0, max_val=NG - 1)
            with sp.If(more == 1):
                load_group(NG, group * EPG)
            for t in range(TT):
                sp.wait_ge(y_made, t + 1)
                sp.dma_start(out_v[:, t, :], y_out[:, t, :]).then_inc(out_done, 16)
            sp.wait_ge(out_done, 16 * TT)

        @block.gpsimd
        def _(pool):
            order = Chain(pool, pool_order)
            pool.memset(ident[:], 0.0).then_inc(pool_order, 1)
            pool.memset(before[:], 1.0).then_inc(pool_order, 1)
            pool.memset(ones[:], 1.0).then_inc(pool_order, 1)
            pool.iota(slot_no[:], [[1, P]], base=0, channel_multiplier=0,
                      allow_small_or_imprecise_dtypes=True).then_inc(pool_order, 1)
            pool.memset(wspT[:], 0.0).then_inc(pool_order, 1)
            order.n = 5
            order.wait()
            order.link(pool.affine_select(out=ident[:], in_=ident[:], compare_op=ALU.not_equal, fill=1.0,
                                          base=0, pattern=[[-1, P]], channel_multiplier=1))
            order.link(pool.affine_select(out=before[:], in_=before[:], compare_op=ALU.is_gt, fill=0.0,
                                          base=0, pattern=[[1, P]], channel_multiplier=-1))
            pool.memset(credit[:, 7:8], 0.0).then_inc(consts, 1)

        @block.scalar
        def _(act):
            def make_hi(slot, arrived, use, src):
                act.wait_ge(arrived, 32 * use + 32)
                return act.activation(whi[:, slot, :], src, ACT.Copy)

            def dense_hi(r, k):
                act.wait_ge(piece_used, ROUND * r + k + 1)
                make_hi(k % DENSE_PARTS, raw_in[k], r, raw[:, k, :]).then_inc(hi_made, 1)

            def sum_squares(src, junk, t):
                act.activation(junk, src, ACT.Square, accum_out=ssq[:, t:t + 1]).then_inc(ssq_made, 1)

            def root(n, t):
                act.wait_ge(ms_made, n + 1)
                act.activation(rstd[:, t:t + 1], ms[:, t:t + 1], ACT.Sqrt).then_inc(rstd_made, 1)

            for t in range(TT):
                act.wait_ge(x_in[t], 16)
                if t:
                    act.wait_ge(ssq_made, t)
                sum_squares(x0[:, t, :], sq0[:], t)
            for t in range(TT):
                root(t, t)
            act.wait_ge(consts, 1)
            act.activation(ident_r[:], ident[:], ACT.Copy).then_inc(ident_r_made, 1)
            for u in range(2 * 4):
                act.wait_ge(xT_full, u + 1)
                t, k4 = divmod(u, 4)
                act.activation(actT_hi[:, 4 * k4:4 * k4 + 4, t * P:(t + 1) * P],
                               bank[u][:].rearrange("p (k t) -> p k t", k=4), ACT.Copy).then_inc(xT_hi_made, 1)

            with act.Fori(0, A1) as c:
                for k in range(ROUND):
                    dense_hi(c, k)

            def evac_heads(g):
                act.wait_ge(ya_t_full, 2 * g + 2)
                for b in range(2):
                    for h2 in range(2):
                        ins = act.activation(
                            yat[h2 * HEAD:(h2 + 1) * HEAD, :, b * P:(b + 1) * P].rearrange("p r (c q) -> p c r q", c=2),
                            bank[3 + b][0:HEAD, :].rearrange("p (c r h q) -> p c r h q", c=2, r=2, h=2)[:, :, :, h2, :],
                            ACT.Copy)
                        ins.then_inc(yat_made, 1)
                act.wait_ge(yat_made, 4 * g + 4)
                act.activation(yaT_hi[:, bass.ds(2 * g, 2), :], yat[:], ACT.Copy).then_inc(yaT_hi_made, 1)

            def attention_a(g, r, first):
                dense_hi(r, 0)
                if not first:
                    evac_heads(g - 1)
                else:
                    act.wait_ge(acc_free, 2 + 2 * A1)
                act.activation(qkv[:, :, 0:4 * HEAD], proj[:, :, bass.ds(4 * HEAD * g, 4 * HEAD)],
                               ACT.Copy).then_inc(qkv_made, 1)
                act.activation(qkv[:, :, 4 * HEAD:5 * HEAD], proj[:, :, bass.ds(HEAD * g + K_OFF, HEAD)],
                               ACT.Copy).then_inc(qkv_made, 1)
                act.activation(qkv[:, :, 5 * HEAD:6 * HEAD], proj[:, :, bass.ds(HEAD * g + V_OFF, HEAD)],
                               ACT.Copy).then_inc(qkv_made, 1)
                dense_hi(r, 1)
                act.wait_ge(qkT_full, 3 * g + 3)
                for t in range(TT):
                    act.activation(qT[:, 2 * t:2 * t + 2, :, :].rearrange("p c h q -> p h c q"),
                                   bank[2 + t][0:HEAD, :].rearrange("p (h c q) -> p h c q", h=4, c=2),
                                   ACT.Copy).then_inc(qkT_made, 1)
                act.activation(kT[:], bank[4][0:HEAD, 0:T], ACT.Copy).then_inc(qkT_made, 1)
                dense_hi(r, 2)
                for b in range(2):
                    act.wait_ge(max_made, 2 * g + b + 1)
                    for tile in range(4):
                        w = CHUNK if b == 0 and tile < 2 else P
                        act.activation(prob[b][:, tile, 0:w], bank[5 + b][:, tile * P:tile * P + w], ACT.Exp,
                                       bias=nmx[:, b, tile:tile + 1], scale=SCALE,
                                       accum_out=rsum[:, b, tile:tile + 1]).then_inc(a_att, 1)
                    act.activation(esink[:, b, :], sdiff[:, b, :], ACT.Exp).then_inc(exp_made, 1)
                dense_hi(r, 3)
                for b in range(2):
                    act.wait_ge(pT_full, 2 * g + b + 1)
                    src = bank[7 if b == 0 else 2]
                    if b == 0:
                        act.activation(probT[0][0:CHUNK, 0:2, :], src[0:CHUNK, 0:2 * P].rearrange("p (a b) -> p a b", a=2),
                                       ACT.Copy).then_inc(pT_made, 1)
                        act.activation(probT[0][:, 2:4, :], src[:, 2 * P:4 * P].rearrange("p (a b) -> p a b", a=2),
                                       ACT.Copy).then_inc(pT_made, 1)
                    else:
                        act.activation(probT[1][:], src[:].rearrange("p (a b) -> p a b", a=4),
                                       ACT.Copy).then_inc(pT_made, 1)

            attention_a(0, A1, True)
            with act.Fori(1, NKV) as g:
                attention_a(g, A1 + g, False)

            def rounds_c(n, r, first):
                dense_hi(r, 0)
                if first:
                    evac_heads(NKV - 1)
                dense_hi(r, 1)
                if first:
                    act.wait_ge(acc_free, 2 + 2 * (A1 + A2))
                    for t in range(TT):
                        act.activation(proj[:, t, VS_OFF:VS_OFF + SGU_W], proj[:, t, VS_OFF:VS_OFF + SGU_W],
                                       ACT.Gelu_apprx_tanh).then_inc(gelu_v, 1)
                    for t in range(TT):
                        act.wait_ge(gelu_v, t + 1)
                        act.wait_ge(ssq_made, TT + t)
                        sum_squares(proj[:, t, VS_OFF:VS_OFF + SGU_W], sq_v[:], t)
                dense_hi(r, 2)
                if first:
                    for t in range(TT):
                        root(TT + t, t)
                    for t in range(TT):
                        act.activation(proj[:, t, U_OFF:U_OFF + SGU_W], proj[:, t, U_OFF:U_OFF + SGU_W],
                                       ACT.Gelu_apprx_tanh).then_inc(gelu_u, 1)
                dense_hi(r, 3)
                dense_hi(r + 1, 0)
                dense_hi(r + 1, 1)
                act.wait_ge(acc_free, 2 * (A1 + A2) + 2 * n + 4)
                act.activation(sga[:], sga[:], ACT.Sigmoid).then_inc(ga_sig, 1)
                dense_hi(r + 1, 2)
                if first:
                    for u in range(4):
                        act.wait_ge(ybT_full, u + 1)
                        t, k4 = divmod(u, 2)
                        act.activation(ybT_hi[:, 4 * k4:4 * k4 + 4, t * P:(t + 1) * P],
                                       bank[4 + u][:].rearrange("p (k t) -> p k t", k=4),
                                       ACT.Copy).then_inc(ybT_hi_made, 1)
                dense_hi(r + 1, 3)
                dense_hi(r + 2, 0)
                dense_hi(r + 2, 1)
                act.wait_ge(gb_free, 2 * n + 4)
                act.activation(sgb[:], sgb[:], ACT.Sigmoid).then_inc(gb_sig, 1)
                dense_hi(r + 2, 2)
                dense_hi(r + 2, 3)

            rounds_c(0, C_ROUND0, True)
            with act.Fori(1, NC) as n:
                rounds_c(n, 3 * n + C_ROUND0, False)

            dense_hi(D_ROUND0, 0)
            dense_hi(D_ROUND0, 1)
            for u in range(2 * NC):
                act.wait_ge(mT_full, u + 1)
                n, t = divmod(u, TT)
                act.activation(actT_hi[:, 4 * n:4 * n + 4, t * P:(t + 1) * P],
                               bank[u][:].rearrange("p (k t) -> p k t", k=4), ACT.Copy).then_inc(mT_hi_made, 1)
            dense_hi(D_ROUND0, 2)
            dense_hi(D_ROUND0, 3)
            with act.Fori(1, NC) as n:
                for k in range(ROUND):
                    dense_hi(n + D_ROUND0, k)

            act.wait_ge(acc_free, 2 * (A1 + A2 + 2 * NC) + 2)
            for t in range(TT):
                act.wait_ge(ssq_made, 2 * TT + t)
                sum_squares(resid[:, t, :], sq2[:], t)
            for t in range(TT):
                root(2 * TT + t, t)
            for u in range(4):
                act.wait_ge(x2T_full, u + 1)
                act.activation(x2T[:, 4 * u:4 * u + 4, 0:P],
                               bank[u][:].rearrange("p (k t) -> p k t", k=4), ACT.Copy).then_inc(x2T_a_made, 1)
            for t in range(TT):
                act.wait_ge(x2_made, t + 1)
                act.activation(x2_hi[:, t, :], x2[:, t, :], ACT.Copy).then_inc(x2_hi_made, 1)
            act.wait_ge(gmax_made, 1)
            for t in range(TT):
                act.activation(gexp[:, t, :], lg[:, t, 0:NG], ACT.Exp, bias=ngm[:, t:t + 1],
                               accum_out=gsum[:, t:t + 1]).then_inc(gexp_made, 1)
            act.wait_ge(ed_made, 1)
            act.activation(ee[:], ed[:], ACT.Exp).then_inc(ee_made, 1)

            def expert_hi(i, j, q):
                m = 6 * j - 2 + q
                act.wait_ge(piece_used, DENSE + PER_G * i + m)
                s = (4 + q) % EXP_RAW
                use = PER_G // EXP_RAW * i + j - (1 if q < 2 else 0)
                make_hi((4 + q) % EXP_PARTS, xraw_in[s], use, xraw[:, s, :]).then_inc(hi_made, 1)

            def hidden_hi(i, j):
                act.wait_ge(hT_full, EPG * i + j + 1)
                act.activation(hT_hi[:], bank[1][:, 0:T].rearrange("p (a b) -> p a b", a=2),
                               ACT.Copy).then_inc(hT_hi_made, 1)

            def silu(i, j):
                await_used(act, PER_G * i + (DENSE + 3) if isinstance(j, int) and j == 0 else
                           PER_G * i + 6 * j + (DENSE + 1))
                act.activation(s_act[:], bank[0][:, 0:FF], ACT.Silu).then_inc(silu_made, 1)

            def group_a(i):
                for q in range(3):
                    expert_hi(i, 0, 2 + q)
                act.wait_ge(selT_full, i + 1)
                act.activation(selT[:], bank[6][:, 0:T], ACT.Copy).then_inc(selT_made, 1)
                for k4, b in enumerate((0, 1, 7, 2)):
                    act.wait_ge(xg_full, 4 * i + k4 + 1)
                    act.activation(xg_hi[:, 4 * k4:4 * k4 + 4, :], bank[b][:].rearrange("p (k t) -> p k t", k=4),
                                   ACT.Copy).then_inc(xg_hi_made, 1)
                expert_hi(i, 0, 5)
                silu(i, 0)
                with act.Fori(1, EPG) as j:
                    expert_hi(i, j, 0)
                    expert_hi(i, j, 1)
                    hidden_hi(i, j - 1)
                    for q in range(2, 6):
                        expert_hi(i, j, q)
                    silu(i, j)
                expert_hi(i, EPG, 0)
                expert_hi(i, EPG, 1)
                hidden_hi(i, EPG - 1)
                for b in range(4):
                    if b < 3:
                        act.wait_ge(o_full, 3 * i + b + 1)
                    else:
                        await_used(act, PER_G * i + (DENSE + PER_G - 1))
                    act.activation(o_hi[:, b * COLS:(b + 1) * COLS], bank[2 + b][:], ACT.Copy).then_inc(o_hi_made, 1)

            with act.Fori(0, NG) as i:
                group_a(i)
            act.wait_ge(ctl_made, 1)
            more = act.value_load(ctl[0:1, 0:1], min_val=0, max_val=1)
            with act.If(more == 1):
                group_a(NG)
            act.wait_ge(small_made, 1)
            for t in range(TT):
                act.wait_ge(ssq_made, 3 * TT + t)
                sum_squares(resid[:, t, :], sq2[:], t)
            for t in range(TT):
                root(3 * TT + t, t)

        @block.vector
        def _(dve):
            order = Chain(dve, v_order)

            def dense_lo(r, k):
                dve.wait_ge(hi_made, ROUND * r + k + 1)
                s = k % DENSE_PARTS
                dve.tensor_tensor(wlo[:, s, :], raw[:, k, :], whi[:, s, :], ALU.subtract).then_inc(lo_made, 1)

            for n, (s, count) in enumerate(((lo_made, DENSE_RAW), (acc_free, 2), (gb_free, 2), (ya_free, 2), (yb_free, 2))):
                dve.memset(credit[:, n:n + 1], 0.0).then_inc(s, count)
            def inverse_mean(k, width):
                for t in range(TT):
                    n = TT * k + t
                    dve.wait_ge(ssq_made, n + 1)
                    dve.tensor_scalar(ms[:, t:t + 1], ssq[:, t:t + 1], 1.0 / width, EPS,
                                      ALU.mult, ALU.add).then_inc(mean_made, 1)
                    dve.wait_ge(mean_made, n + 1)
                    dve.reciprocal(ms[:, t:t + 1], ms[:, t:t + 1]).then_inc(ms_made, 1)

            inverse_mean(0, D)
            dve.wait_ge(g1_in, 16)
            for t in range(TT):
                dve.wait_ge(rstd_made, t + 1)
                dve.scalar_tensor_tensor(out=xs0[:, t, :], in0=x0[:, t, :], scalar=rstd[:, t:t + 1], in1=g1[:],
                                         op0=ALU.mult, op1=ALU.mult).then_inc(xs_made, 1)
            for u in range(8):
                dve.wait_ge(xT_hi_made, u + 1)
                t, k4 = divmod(u, 4)
                hi = actT_hi[:, 4 * k4:4 * k4 + 4, t * P:(t + 1) * P]
                dve.tensor_tensor(actT_lo[:, 4 * k4:4 * k4 + 4, t * P:(t + 1) * P],
                                  bank[u][:].rearrange("p (k t) -> p k t", k=4), hi, ALU.subtract).then_inc(xT_lo_made, 1)
            dve.wait_ge(wspT_full, 3)
            dve.wait_ge(consts, 1)
            for b in range(2):
                src = bank[b][:].rearrange("p (g i) -> p g i", g=4)
                dve.tensor_copy(wspT[0:CHUNK, 4 * b:4 * b + 4, :], src[0:CHUNK]).then_inc(wspT_made, 1)
                dve.tensor_copy(wspT[CHUNK:P, 4 * b:4 * b + 4, CHUNK:P], src[CHUNK:P, :, CHUNK:P]).then_inc(wspT_made, 1)
            dve.tensor_copy(bsT[:], bank[2][:, 0:SG]).then_inc(wspT_made, 1)
            dve.wait_ge(sink_in, 16)
            for h2 in range(2):
                rows = slice(h2 * CHUNK, (h2 + 1) * CHUNK)
                src = sink_row[rows, :].rearrange("p (g r h) -> p g r h", g=NKV, r=2)[:, :, :, h2]
                for c2 in range(2):
                    order.mark(dve.tensor_copy(sinkv[rows, :, c2, :], src))
            order.wait()

            def evac_proj(c):
                dve.wait_ge(bias_a_in, 16 * c + 16)
                for t in range(TT):
                    await_chunk(dve, t, acc_full, c, ROUND * c + 3)
                    dve.tensor_tensor(proj[:, t, bass.ds(c * COLS, COLS)], bank[t][:], bias_a[:],
                                      ALU.add).then_inc(acc_free, 1)

            for k in range(ROUND):
                dense_lo(0, k)
            with dve.Fori(1, A1) as c:
                dense_lo(c, 0)
                evac_proj(c - 1)
                for k in range(1, ROUND):
                    dense_lo(c, k)

            ATT_LINKS = 18

            def heads_lo(g):
                dve.wait_ge(yaT_hi_made, g + 1)
                dve.tensor_tensor(yaT_lo[:, bass.ds(2 * g, 2), :], yat[:], yaT_hi[:, bass.ds(2 * g, 2), :],
                                  ALU.subtract).then_inc(yaT_lo_made, 1)

            def attention_v(g, r, first):
                steps = Chain(dve, v_att, ATT_LINKS * g)
                dense_lo(r, 0)
                evac_proj(r - 1)
                if not first:
                    heads_lo(g - 1)
                dense_lo(r, 1)
                dve.wait_ge(qkv_made, 3 * g + 3)
                dve.tensor_copy(vmid[0:CHUNK, :], qkv[0:CHUNK, 1, 5 * HEAD:6 * HEAD]).then_inc(vmid_made, 1)
                dve.tensor_copy(vmid[CHUNK:P, :], qkv[CHUNK:P, 0, 5 * HEAD:6 * HEAD]).then_inc(vmid_made, 1)
                dense_lo(r, 2)
                for b in range(2):
                    dve.wait_ge(sc_full, 2 * g + b + 1)
                    sc = bank[5 + b][:].rearrange("p (a k) -> p a k", a=4)
                    if b == 0:
                        steps.mark(dve.tensor_reduce(mx[:, b, 0:2], sc[:, 0:2, 0:CHUNK], AX_X, ALU.max))
                        steps.mark(dve.tensor_reduce(mx[:, b, 2:4], sc[:, 2:4, :], AX_X, ALU.max))
                    else:
                        steps.mark(dve.tensor_reduce(mx[:, b, :], sc, AX_X, ALU.max))
                    steps.wait()
                    sinks = sinkv[:, bass.ds(g, 1), :, :].rearrange("p a c r -> p (a c r)")
                    steps.link(dve.scalar_tensor_tensor(out=mx[:, b, :], in0=mx[:, b, :], scalar=SCALE, in1=sinks,
                                                        op0=ALU.mult, op1=ALU.max))
                    steps.link(dve.tensor_tensor(sdiff[:, b, :], sinks, mx[:, b, :], ALU.subtract))
                    dve.tensor_scalar(nmx[:, b, :], mx[:, b, :], -1.0, None, ALU.mult).then_inc(max_made, 1)
                for b in range(2):
                    dve.wait_ge(exp_made, 2 * g + b + 1)
                    dve.wait_ge(a_att, 8 * g + 4 * b + 4)
                    steps.link(dve.tensor_tensor(rden[:, b, :], rsum[:, b, :], esink[:, b, :], ALU.add))
                    steps.link(dve.reciprocal(rden[:, b, :], rden[:, b, :]))
                    for tile in range(4):
                        w = CHUNK if b == 0 and tile < 2 else P
                        ins = dve.tensor_scalar(prob[b][:, tile, 0:w], prob[b][:, tile, 0:w],
                                                rden[:, b, tile:tile + 1], None, ALU.mult)
                        if tile < 3:
                            steps.mark(ins)
                        else:
                            ins.then_inc(prob_made, 1)
                assert steps.n <= ATT_LINKS, steps.n
                while steps.n < ATT_LINKS:
                    steps.mark(dve.memset(credit[:, 5:6], 0.0))
                    steps.wait()
                dense_lo(r, 3)

            attention_v(0, A1, True)
            with dve.Fori(1, NKV) as g:
                attention_v(g, A1 + g, False)

            def merge_b(n):
                dve.wait_ge(gb_sig, n + 1)
                for t in range(TT):
                    await_chunk(dve, t, yb_full, n, ROUND * (3 * n + C_ROUND0 + 2) + 3)
                    dve.tensor_tensor(gyb[:, t, :], bank[6 + t][:], sgb[:, t, :], ALU.mult).then_inc(yb_free, 1)
                dve.wait_ge(yb_free, 2 * n + 4)
                for t in range(TT):
                    mg = merged[:, t, bass.ds(n * COLS, COLS)]
                    dve.tensor_tensor(mg, mg, gyb[:, t, :], ALU.add).then_inc(gyb_made, 1)

            def rounds_v(n, r, first):
                dense_lo(r, 0)
                if first:
                    evac_proj(A1 + A2 - 1)
                    heads_lo(NKV - 1)
                else:
                    merge_b(n - 1)
                dense_lo(r, 1)
                dense_lo(r, 2)
                if first:
                    inverse_mean(1, SGU_W)
                    dve.wait_ge(gv_in, 16)
                    for t in range(TT):
                        dve.wait_ge(rstd_made, TT + t + 1)
                        v = proj[:, t, VS_OFF:VS_OFF + SGU_W]
                        dve.scalar_tensor_tensor(out=v, in0=v, scalar=rstd[:, t:t + 1], in1=gv[:],
                                                 op0=ALU.mult, op1=ALU.mult).then_inc(vn_made, 1)
                dense_lo(r, 3)
                dense_lo(r + 1, 0)
                dve.wait_ge(bias_a_in, 16 * (A1 + A2) + 16 * n + 16)
                for t in range(TT):
                    await_chunk(dve, t, acc_full, n + (A1 + A2), ROUND * r + 3)
                    if first:
                        dve.wait_ge(mix_full, 4)
                    dve.tensor_tensor(sga_of(t), bank[t][:], bias_a[:], ALU.add).then_inc(acc_free, 1)
                if first:
                    gate_u(0)
                dense_lo(r + 1, 1)
                if first:
                    gate_u(1)
                dense_lo(r + 1, 2)
                if first:
                    for u in range(4):
                        dve.wait_ge(ybT_hi_made, u + 1)
                        t, k4 = divmod(u, 2)
                        hi = ybT_hi[:, 4 * k4:4 * k4 + 4, t * P:(t + 1) * P]
                        dve.tensor_tensor(ybT_lo[:, 4 * k4:4 * k4 + 4, t * P:(t + 1) * P],
                                          bank[4 + u][:].rearrange("p (k t) -> p k t", k=4), hi,
                                          ALU.subtract).then_inc(ybT_lo_made, 1)
                dense_lo(r + 1, 3)
                dense_lo(r + 2, 0)
                dve.wait_ge(bias_b_in, 16 * n + 16)
                for t in range(TT):
                    await_chunk(dve, t, gb_full, n, ROUND * r + (ROUND + 3))
                    dve.tensor_tensor(sgb[:, t, :], bank[2 + t][:], bias_b[:], ALU.add).then_inc(gb_free, 1)
                dense_lo(r + 2, 1)
                dense_lo(r + 2, 2)
                dve.wait_ge(ga_sig, n + 1)
                for t in range(TT):
                    await_chunk(dve, t, ya_full, n, ROUND * r + (2 * ROUND + 1))
                    dve.tensor_tensor(merged[:, t, bass.ds(n * COLS, COLS)], bank[4 + t][:], sga[:, t, :],
                                      ALU.mult).then_inc(ya_free, 1)
                dense_lo(r + 2, 3)

            def sga_of(t):
                return sga[:, t, :]

            def gate_u(t):
                dve.wait_ge(gelu_u, t + 1)
                for g in range(SG):
                    u = proj[:, t, U_OFF + g * P:U_OFF + (g + 1) * P]
                    dve.wait_ge(mix_full, 2 * t + g // 4 + 1)
                    dve.scalar_tensor_tensor(out=u, in0=bank[4 + 2 * t + g // 4][:, (g % 4) * P:(g % 4 + 1) * P],
                                             scalar=bsT[:, g:g + 1], in1=u,
                                             op0=ALU.add, op1=ALU.mult).then_inc(yb_made, 1)

            rounds_v(0, C_ROUND0, True)
            with dve.Fori(1, NC) as n:
                rounds_v(n, 3 * n + C_ROUND0, False)

            dense_lo(D_ROUND0, 0)
            merge_b(NC - 1)
            dense_lo(D_ROUND0, 1)
            for u in range(2 * NC):
                dve.wait_ge(mT_hi_made, u + 1)
                n, t = divmod(u, TT)
                hi = actT_hi[:, 4 * n:4 * n + 4, t * P:(t + 1) * P]
                dve.tensor_tensor(actT_lo[:, 4 * n:4 * n + 4, t * P:(t + 1) * P],
                                  bank[u][:].rearrange("p (k t) -> p k t", k=4), hi, ALU.subtract).then_inc(mT_lo_made, 1)
            dense_lo(D_ROUND0, 2)
            dense_lo(D_ROUND0, 3)

            def evac_out(n):
                dve.wait_ge(resid_in, 16 * TT)
                for t in range(TT):
                    await_chunk(dve, t, acc_full, n + (A1 + A2 + NC), ROUND * n + (ROUND * D_ROUND0 + 3))
                    h = resid[:, t, bass.ds(n * COLS, COLS)]
                    dve.tensor_tensor(h, bank[t][:], h, ALU.add).then_inc(acc_free, 1)

            with dve.Fori(1, NC) as n:
                dense_lo(n + D_ROUND0, 0)
                evac_out(n - 1)
                for k in range(1, ROUND):
                    dense_lo(n + D_ROUND0, k)
            evac_out(NC - 1)

            inverse_mean(2, D)
            dve.wait_ge(g2_in, 16)
            for t in range(TT):
                dve.wait_ge(rstd_made, 2 * TT + t + 1)
                dve.scalar_tensor_tensor(out=x2[:, t, :].rearrange("t (k p) -> t k p", p=P),
                                         in0=resid[:, t, :].rearrange("t (p k) -> t k p", k=KT),
                                         scalar=rstd[:, t:t + 1],
                                         in1=gbig[:].rearrange("t (p k) -> t k p", k=KT),
                                         op0=ALU.mult, op1=ALU.mult).then_inc(x2_made, 1)
            order.link(dve.memset(gl8[:], LOWEST))
            for u in range(4):
                dve.wait_ge(x2T_full, 4 + u + 1)
                dve.tensor_copy(x2T[:, 4 * u:4 * u + 4, P:T],
                                bank[4 + u][:].rearrange("p (k t) -> p k t", k=4)).then_inc(x2T_v_made, 1)
            for t in range(TT):
                dve.wait_ge(x2_hi_made, t + 1)
                dve.tensor_tensor(x2_lo[:, t, :], x2[:, t, :], x2_hi[:, t, :], ALU.subtract).then_inc(x2_lo_made, 1)
            dve.wait_ge(br_in, 32)
            for t in range(TT):
                dve.wait_ge(lg_full, t + 1)
                order.mark(dve.tensor_tensor(lg[:, t, :], bank[t][:, 0:NR], br[:], ALU.add))
            order.wait()
            order.link(dve.tensor_copy(gl8[:, :, 0:NG], lg[:, :, 0:NG]))
            for t in range(TT):
                order.mark(dve.max(gm8[:, t, :], gl8[:, t, :]))
            order.wait()
            dve.tensor_scalar(ngm[:], gm8[:, :, 0], -1.0, None, ALU.mult).then_inc(gmax_made, 1)
            for t in range(TT):
                order.mark(dve.max_index(gi8[:, t, :], gm8[:, t, :], gl8[:, t, :]))
            order.wait()
            order.link(dve.tensor_copy(gif[:], gi8[:]))
            for t in range(TT):
                dve.tensor_scalar(goh[:, t, :], slot_no[:, 0:NG], gif[:, t, 0:1], None,
                                  ALU.is_equal).then_inc(goh_made, 1)
            dve.wait_ge(goh_made, TT)
            for t in range(TT):
                order.mark(dve.tensor_tensor(own[:, t, :, :], lg[:, t, NG:NR].rearrange("p (g e) -> p g e", g=NG),
                                             goh[:, t, :].to_broadcast([P, NG, EPG]), ALU.mult))
            order.wait()
            for t in range(TT):
                order.mark(dve.tensor_reduce(inl[:, t, :], own[:, t, :, :].rearrange("p g e -> p e g"), AX_X, ALU.add))
            order.wait()
            for t in range(TT):
                order.mark(dve.max(em8[:, t, :], inl[:, t, :]))
            order.wait()
            dve.tensor_tensor(ed[:], em8[:, :, 1], em8[:, :, 0], ALU.subtract).then_inc(ed_made, 1)
            for t in range(TT):
                order.mark(dve.max_index(ei8[:, t, :], em8[:, t, :], inl[:, t, :]))
            order.wait()
            order.link(dve.tensor_copy(eif[:], ei8[:]))
            dve.wait_ge(gexp_made, TT)
            order.link(dve.reciprocal(gval[:], gsum[:]))
            dve.wait_ge(ee_made, 1)
            order.link(dve.tensor_scalar(es1[:], ee[:], 1.0, None, ALU.add))
            order.link(dve.reciprocal(es1[:], es1[:]))
            order.link(dve.tensor_tensor(ew0[:], es1[:], gval[:], ALU.mult))
            order.link(dve.tensor_tensor(ew1[:], ew0[:], ee[:], ALU.mult))
            for t in range(TT):
                order.mark(dve.tensor_scalar(ca[:, t, :], slot_no[:, 0:EPG], eif[:, t, 0:1], ew0[:, t:t + 1],
                                             ALU.is_equal, ALU.mult))
                order.mark(dve.tensor_scalar(cb[:, t, :], slot_no[:, 0:EPG], eif[:, t, 1:2], ew1[:, t:t + 1],
                                             ALU.is_equal, ALU.mult))
            order.wait()
            order.link(dve.tensor_tensor(ca[:], ca[:], cb[:], ALU.add))
            order.link(dve.tensor_copy(cw_hi[:], ca[:]))
            dve.tensor_tensor(cw_lo[:], ca[:], cw_hi[:], ALU.subtract).then_inc(cwparts_made, 1)
            dve.wait_ge(rank_full, 3)
            for t in range(TT):
                order.mark(dve.tensor_tensor(rkp[:, t, :], bank[2 + t][:, 0:NG], goh[:, t, :], ALU.mult))
            order.wait()
            order.link(dve.tensor_reduce(rank[:], rkp[:], AX_X, ALU.add))
            order.mark(dve.tensor_scalar(fits[:], rank[:], float(P), None, ALU.is_lt))
            order.mark(dve.tensor_scalar(over[:], rank[:], float(P), None, ALU.is_ge))
            order.wait()
            order.mark(dve.scalar_tensor_tensor(out=rk1[:], in0=rank[:], scalar=1.0, in1=fits[:], op0=ALU.add, op1=ALU.mult))
            order.mark(dve.scalar_tensor_tensor(out=rk2[:], in0=rank[:], scalar=1.0 - P, in1=over[:], op0=ALU.add, op1=ALU.mult))
            order.wait()
            for t in range(TT):
                order.mark(dve.tensor_scalar(pos[:, t, 0:NG], goh[:, t, :], rk1[:, t:t + 1], -1.0, ALU.mult, ALU.add))
            order.mark(dve.tensor_scalar(pos[:, :, NG], rk2[:], -1.0, None, ALU.add))
            order.link(dve.tensor_scalar(ovg[:], bank[4][:, 0:NG], float(P), None, ALU.is_gt))
            order.link(dve.tensor_tensor(ovn[:], ovg[:], slot_no[:, 0:NG], ALU.mult))
            order.mark(dve.tensor_reduce(ctlf[:, 0:1], ovg[:], AX_X, ALU.add))
            order.mark(dve.tensor_reduce(ctlf[:, 1:2], ovn[:], AX_X, ALU.add))
            order.wait()
            dve.tensor_copy(ctl[:], ctlf[:]).then_inc(ctl_made, 1)

            def expert_lo(i, j, q):
                m = 6 * j - 2 + q
                s, sp_ = (4 + q) % EXP_RAW, (4 + q) % EXP_PARTS
                dve.wait_ge(hi_made, DENSE + PER_G * i + m + 1)
                dve.tensor_tensor(wlo[:, sp_, :], xraw[:, s, :], whi[:, sp_, :], ALU.subtract).then_inc(lo_made, 1)

            def hidden_lo(i, j):
                dve.wait_ge(hT_hi_made, EPG * i + j + 1)
                dve.tensor_tensor(hT_lo[:], bank[1][:, 0:T].rearrange("p (a b) -> p a b", a=2), hT_hi[:],
                                  ALU.subtract).then_inc(hT_lo_made, 1)

            def hidden(i, j):
                dve.wait_ge(silu_made, EPG * i + j + 1)
                dve.scalar_tensor_tensor(out=hid[:], in0=bank[0][:, FF:2 * FF], scalar=cw[:, bass.ds(j, 1)],
                                         in1=s_act[:], op0=ALU.mult, op1=ALU.mult).then_inc(hid_made, 1)

            def group_v(i):
                for t in range(TT):
                    dve.tensor_scalar(sel[:, t, :], slot_no[:], pos[:, t, bass.ds(i, 1)], None,
                                      ALU.is_equal).then_inc(sel_made, 1)
                for q in range(3):
                    expert_lo(i, 0, 2 + q)
                dve.wait_ge(selT_full, i + 1)
                dve.tensor_copy(cw[:], bank[3][:, 0:EPG]).then_inc(cw_made, 1)
                for k4, b in enumerate((0, 1, 7, 2)):
                    dve.wait_ge(xg_hi_made, 4 * i + k4 + 1)
                    dve.tensor_tensor(xg_lo[:, 4 * k4:4 * k4 + 4, :], bank[b][:].rearrange("p (k t) -> p k t", k=4),
                                      xg_hi[:, 4 * k4:4 * k4 + 4, :], ALU.subtract).then_inc(xg_lo_made, 1)
                expert_lo(i, 0, 5)
                dve.wait_ge(cw_made, i + 1)
                hidden(i, 0)
                with dve.Fori(1, EPG) as j:
                    expert_lo(i, j, 0)
                    expert_lo(i, j, 1)
                    hidden_lo(i, j - 1)
                    for q in range(2, 6):
                        expert_lo(i, j, q)
                    hidden(i, j)
                expert_lo(i, EPG, 0)
                expert_lo(i, EPG, 1)
                hidden_lo(i, EPG - 1)
                for b in range(4):
                    dve.wait_ge(o_hi_made, 4 * i + b + 1)
                    cols = slice(b * COLS, (b + 1) * COLS)
                    dve.tensor_tensor(o_lo[:, cols], bank[2 + b][:], o_hi[:, cols], ALU.subtract).then_inc(o_lo_made, 1)
                for u in range(8):
                    b, t = divmod(u, TT)
                    dve.wait_ge(scat_full, 8 * i + u + 1)
                    h = resid[:, t, b * COLS:(b + 1) * COLS]
                    dve.tensor_tensor(h, bank[6 + t][:], h, ALU.add).then_inc(added, 1)

            dve.wait_ge(v_order, order.n)
            with dve.Fori(0, NG) as i:
                group_v(i)
            dve.wait_ge(ctl_made, 1)
            more = dve.value_load(ctl[0:1, 0:1], min_val=0, max_val=1)
            with dve.If(more == 1):
                group_v(NG)
            dve.wait_ge(added, 8 * NG)
            dve.memset(credit[:, 6:7], 0.0).then_inc(small_made, 1)
            inverse_mean(3, D)
            dve.wait_ge(gf_in, 16)
            for t in range(TT):
                dve.wait_ge(rstd_made, 3 * TT + t + 1)
                dve.scalar_tensor_tensor(out=y_out[:, t, :], in0=resid[:, t, :], scalar=rstd[:, t:t + 1], in1=gbig[:],
                                         op0=ALU.mult, op1=ALU.mult).then_inc(y_made, 1)

        @block.tensor
        def _(pe):
            def three(o, x_hi, x_lo, w_hi, w_lo, start, stop):
                pe.matmul(o, x_hi, w_hi, start=start, stop=False)
                pe.matmul(o, x_lo, w_hi, start=False, stop=False)
                return pe.matmul(o, x_hi, w_lo, start=False, stop=stop)

            pe.wait_ge(consts, 1)
            for t in range(TT):
                pe.wait_ge(xs_made, t + 1)
                for k4 in range(4):
                    for k in range(4):
                        d0 = (4 * k4 + k) * P
                        mm = pe.transpose(bank[4 * t + k4][:, k * P:(k + 1) * P], xs0[:, t, d0:d0 + P], ident[:])
                    mm.then_inc(xT_full, 1)
            pe.wait_ge(wsp_in, 16)
            for b in range(2):
                pe.wait_ge(xT_lo_made, b + 1)
                for g in range(4):
                    mm = pe.transpose(bank[b][:, g * P:(g + 1) * P], wsp[:, 4 * b + g, :], ident[:])
                    if g == 2:
                        mm.then_inc(piece_used, 1)
                mm.then_inc(wspT_full, 1)
            pe.wait_ge(bs_in, 16)
            pe.wait_ge(xT_lo_made, 3)
            pe.transpose(bank[2][:, 0:SG], bs8[:], ident[0:SG, 0:SG]).then_inc(wspT_full, 1)
            pe.wait_ge(xT_lo_made, 8)
            pe.wait_ge(wspT_made, 5)

            def proj_piece(c, k):
                dense_piece(c, k, 0, actT_hi, actT_lo, 4 * k, k == 0, k == ROUND - 1, (acc_free, 2 * c), acc_full)

            def dense_piece(r, k, banks, x_hi, x_lo, kt, first, last, free, full):
                pe.wait_ge(lo_made, DENSE_RAW + ROUND * r + k + 1)
                s = k % DENSE_PARTS
                for t in range(TT):
                    if first:
                        pe.wait_ge(free[0], free[1] + t + 1)
                    for q in range(4):
                        cols = slice(q * COLS, (q + 1) * COLS)
                        tok = slice(t * P, (t + 1) * P)
                        mm = three(bank[banks + t][:], x_hi[:, kt + q, tok], x_lo[:, kt + q, tok],
                                   whi[:, s, cols], wlo[:, s, cols], first and q == 0, last and q == 3)
                    if last and t == 0:
                        mm.then_inc(full, 1)
                mm.then_inc(piece_used, 1)

            with pe.Fori(0, A1) as c:
                for k in range(ROUND):
                    proj_piece(c, k)

            def attention_t(g, r):
                proj_piece(r, 0)
                pe.wait_ge(qkv_made, 3 * g + 3)
                for t in range(TT):
                    for h, w in enumerate((P, HEAD, HEAD, HEAD)):
                        mm = pe.transpose(bank[2 + t][0:w, h * P:(h + 1) * P],
                                          qkv[:, t, h * HEAD:h * HEAD + w], ident[:])
                    mm.then_inc(qkT_full, 1)
                for t in range(TT):
                    mm = pe.transpose(bank[4][0:HEAD, t * P:(t + 1) * P], qkv[:, t, 4 * HEAD:5 * HEAD], ident[:])
                mm.then_inc(qkT_full, 1)
                proj_piece(r, 1)
                pe.wait_ge(qkT_made, 3 * g + 3)
                for b in range(2):
                    for c2 in range(2):
                        c = 2 * b + c2
                        for rr in range(2):
                            o = (c2 * 2 + rr) * P
                            q = qT[:, c, 2 * rr:2 * rr + 2, :].rearrange("p h q -> p (h q)")
                            spans = {0: [(0, 0, CHUNK)], 1: [(0, 0, P)], 3: [(0, P, 2 * P)],
                                     2: [(0, P, P + CHUNK), (CHUNK, CHUNK, P)]}[c]
                            for off, k0, k1 in spans:
                                mm = pe.matmul(bank[5 + b][:, o + off:o + off + k1 - k0], q, kT[:, k0:k1],
                                               start=True, stop=True)
                    mm.then_inc(sc_full, 1)
                proj_piece(r, 2)
                for b in range(2):
                    pe.wait_ge(prob_made, 2 * g + b + 1)
                    dst = bank[7 if b == 0 else 2]
                    for tile in (2, 3, 0, 1):
                        w = CHUNK if b == 0 and tile < 2 else P
                        mm = pe.transpose(dst[0:w, tile * P:(tile + 1) * P], prob[b][:, tile, 0:w], ident[:])
                    mm.then_inc(pT_full, 1)
                proj_piece(r, 3)
                pe.wait_ge(vmid_made, 2 * g + 2)
                for b in range(2):
                    pe.wait_ge(pT_made, 3 * g + 2 + b)
                    for tile in (2, 3, 0, 1):
                        c = 2 * b + tile // 2
                        w = CHUNK if c == 0 else P
                        v = {0: qkv[0:CHUNK, 0, 5 * HEAD:6 * HEAD], 1: qkv[:, 0, 5 * HEAD:6 * HEAD],
                             2: vmid[:], 3: qkv[:, 1, 5 * HEAD:6 * HEAD]}[c]
                        mm = pe.matmul(bank[3 + b][0:HEAD, tile * P:(tile + 1) * P], v, probT[b][0:w, tile, :],
                                       start=True, stop=True)
                    mm.then_inc(ya_t_full, 1)

            with pe.Fori(0, NKV) as g:
                attention_t(g, A1 + g)

            def rounds_t(n, r, first):
                for k in range(ROUND):
                    dense_piece(r, k, 0, actT_hi, actT_lo, 4 * k, k == 0, k == 3,
                                     (acc_free, 2 * (A1 + A2) + 2 * n), acc_full)
                    if first and k == 2:
                        pe.wait_ge(yaT_hi_made, NKV)
                        for t in range(TT):
                            pe.wait_ge(vn_made, t + 1)
                            for gg in range(2):
                                for g in range(4):
                                    ch = 4 * gg + g
                                    mm = pe.matmul(bank[4 + 2 * t + gg][:, g * P:(g + 1) * P], wspT[:, ch, :],
                                                   proj[:, t, VS_OFF + ch * P:VS_OFF + (ch + 1) * P],
                                                   start=True, stop=True)
                                mm.then_inc(mix_full, 1)
                for k in range(ROUND):
                    dense_piece(r + 1, k, 2, actT_hi, actT_lo, 4 * k, k == 0, k == 3,
                                     (gb_free, 2 * n), gb_full)
                    if first and k == 1:
                        for t in range(TT):
                            pe.wait_ge(yb_made, SG * (t + 1) if t == 0 else TT * SG)
                            for k4 in range(2):
                                for q in range(4):
                                    c0 = U_OFF + (4 * k4 + q) * P
                                    mm = pe.transpose(bank[4 + 2 * t + k4][:, q * P:(q + 1) * P],
                                                      proj[:, t, c0:c0 + P], ident[:])
                                mm.then_inc(ybT_full, 1)
                if first:
                    pe.wait_ge(yaT_lo_made, NKV)
                    pe.wait_ge(ybT_lo_made, 4)
                for k in range(2):
                    dense_piece(r + 2, k, 4, yaT_hi, yaT_lo, 4 * k, k == 0, k == 1, (ya_free, 2 * n), ya_full)
                for k in range(2):
                    dense_piece(r + 2, 2 + k, 6, ybT_hi, ybT_lo, 4 * k, k == 0, k == 1, (yb_free, 2 * n), yb_full)

            rounds_t(0, C_ROUND0, True)
            with pe.Fori(1, NC) as n:
                rounds_t(n, 3 * n + C_ROUND0, False)

            pe.wait_ge(acc_free, 2 * (A1 + A2 + NC) + 2)
            pe.wait_ge(gb_free, 2 * NC + 2)
            pe.wait_ge(ya_free, 2 * NC + 2)
            for n in range(NC):
                pe.wait_ge(gyb_made, 2 * n + 2)
                for t in range(TT):
                    for q in range(4):
                        c0 = (4 * n + q) * P
                        mm = pe.transpose(bank[2 * n + t][:, q * P:(q + 1) * P], merged[:, t, c0:c0 + P], ident[:])
                    mm.then_inc(mT_full, 1)
            pe.wait_ge(mT_lo_made, 2 * NC)
            with pe.Fori(0, NC) as n:
                for k in range(ROUND):
                    dense_piece(n + D_ROUND0, k, 0, actT_hi, actT_lo, 4 * k, k == 0, k == 3,
                                     (acc_free, 2 * (A1 + A2 + NC) + 2 * n), acc_full)

            pe.wait_ge(acc_free, 2 * (A1 + A2 + 2 * NC) + 2)
            for t in range(TT):
                pe.wait_ge(x2_made, t + 1)
                for k4 in range(4):
                    for q in range(4):
                        c0 = (4 * k4 + q) * P
                        mm = pe.transpose(bank[4 * t + k4][:, q * P:(q + 1) * P], x2[:, t, c0:c0 + P], ident[:])
                    mm.then_inc(x2T_full, 1)
            pe.wait_ge(wr_in, 32)
            pe.wait_ge(x2T_a_made, 4)
            for t in range(TT):
                if t:
                    pe.wait_ge(x2T_v_made, 4)
                for k in range(KT):
                    mm = pe.matmul(bank[t][:, 0:NR], x2T[:, k, t * P:(t + 1) * P], wr[:, k, :],
                                   start=(k == 0), stop=(k == KT - 1))
                mm.then_inc(lg_full, 1)
            pe.wait_ge(goh_made, TT)
            pe.matmul(bank[2][:, 0:NG], before[:], goh[:, 0, :], start=True, stop=True).then_inc(rank_full, 1)
            pe.matmul(bank[3][:, 0:NG], before[:], goh[:, 1, :], start=True, stop=False)
            pe.matmul(bank[3][:, 0:NG], ones[:], goh[:, 0, :], start=False, stop=True).then_inc(rank_full, 1)
            pe.matmul(bank[4][:, 0:NG], ones[:], goh[:, 0, :], start=True, stop=False)
            pe.matmul(bank[4][:, 0:NG], ones[:], goh[:, 1, :], start=False, stop=True).then_inc(rank_full, 1)
            pe.wait_ge(cwparts_made, 1)
            pe.wait_ge(x2_lo_made, TT)
            pe.wait_ge(ident_r_made, 1)

            def gu_piece(i, j, q):
                m = 6 * j - 2 + q
                s = (4 + q) % EXP_PARTS
                pe.wait_ge(lo_made, DENSE_RAW + DENSE + PER_G * i + m + 1)
                w_hi = whi[:, s, :].rearrange("p (u k f) -> p u k f", u=2, k=4)
                w_lo = wlo[:, s, :].rearrange("p (u k f) -> p u k f", u=2, k=4)
                return w_hi, w_lo

            def gate_up(i, j, q0):
                for k4 in range(4):
                    w_hi, w_lo = gu_piece(i, j, q0 + k4)
                    for k in range(4):
                        kt = 4 * k4 + k
                        mm = three(bank[0][:], xg_hi[:, kt, :], xg_lo[:, kt, :], w_hi[:, :, k, :], w_lo[:, :, k, :],
                                   kt == 0, kt == KT - 1)
                    mm.then_inc(piece_used, 1)

            def down(i, j, start, stop):
                pe.wait_ge(hT_lo_made, EPG * i + j)
                for f in range(2):
                    m = 6 * j + 2 + f
                    q = 4 + f if not stop else f
                    if stop:
                        m = 6 * j - 2 + f
                    s = (4 + q) % EXP_PARTS
                    pe.wait_ge(lo_made, DENSE_RAW + DENSE + PER_G * i + m + 1)
                    for b in range(4):
                        cols = slice(b * COLS, (b + 1) * COLS)
                        mm = three(bank[2 + b][:], hT_hi[:, f, :], hT_lo[:, f, :], whi[:, s, cols], wlo[:, s, cols],
                                   start and f == 0, stop and f == 1)
                        if stop and f == 1 and b < 3:
                            mm.then_inc(o_full, 1)
                    mm.then_inc(piece_used, 1)

            def turn_hidden(i, j):
                pe.wait_ge(hid_made, EPG * i + j + 1)
                for f in range(2):
                    mm = pe.transpose(bank[1][:, f * P:(f + 1) * P], hid[:, f * P:(f + 1) * P], ident[:])
                mm.then_inc(hT_full, 1)

            def group_t(i):
                pe.wait_ge(sel_made, TT * i + 2)
                for t in range(TT):
                    mm = pe.matmul(bank[6][:, t * P:(t + 1) * P], sel[:, t, :], ident_r[:], start=True, stop=True)
                n = 0
                for t in range(TT):
                    for part in (cw_hi, cw_lo):
                        mm = pe.matmul(bank[3][:, 0:EPG], sel[:, t, :], part[:, t, :], start=(n == 0), stop=(n == 3))
                        n += 1
                mm.then_inc(selT_full, 1)
                for k4, b in enumerate((0, 1, 7, 2)):
                    for q in range(4):
                        kt = 4 * k4 + q
                        n = 0
                        for part in (x2_hi, x2_lo):
                            for t in range(TT):
                                mm = pe.matmul(bank[b][:, q * P:(q + 1) * P], part[:, t, kt * P:(kt + 1) * P],
                                               sel[:, t, :], start=(n == 0), stop=(n == 3))
                                n += 1
                    mm.then_inc(xg_full, 1)
                pe.wait_ge(xg_lo_made, 4 * i + 4)
                gate_up(i, 0, 2)
                turn_hidden(i, 0)
                pe.wait_ge(cw_made, i + 1)

                def step(j, start):
                    pe.wait_ge(hid_made, EPG * i + j)
                    gate_up(i, j, 0)
                    down(i, j, start, False)
                    turn_hidden(i, j)

                step(1, True)
                with pe.Fori(2, EPG) as j:
                    step(j, False)
                down(i, EPG, False, True)
                pe.wait_ge(selT_made, i + 1)
                for u in range(8):
                    b, t = divmod(u, TT)
                    cols = slice(b * COLS, (b + 1) * COLS)
                    pe.wait_ge(o_lo_made, 4 * i + b + 1)
                    if u >= 2:
                        pe.wait_ge(added, 8 * i + u - 1)
                    tok = slice(t * P, (t + 1) * P)
                    pe.matmul(bank[6 + t][:], selT[:, tok], o_hi[:, cols], start=True, stop=False)
                    pe.matmul(bank[6 + t][:], selT[:, tok], o_lo[:, cols], start=False, stop=True).then_inc(scat_full, 1)

            with pe.Fori(0, NG) as i:
                group_t(i)
            pe.wait_ge(ctl_made, 1)
            more = pe.value_load(ctl[0:1, 0:1], min_val=0, max_val=1)
            with pe.If(more == 1):
                group_t(NG)


_INS = ["x", "norm_mix_g", "w_in", "b_in", "attn_sinks", "norm_v_g", "w_spatial", "b_spatial", "w_gate", "b_gate",
        "w_branch_a", "w_branch_b", "w_out", "norm_ffn_g", "w_router_group", "b_router_group", "w_router_expert",
        "b_router_expert", "w_e_gate", "w_e_up", "w_e_down", "norm_final_g"]


def kernel(**inputs):
    import numpy as _np
    import concourse.bacc as _bacc
    from concourse import mybir as _mybir
    from concourse.bass_utils import run_bass_kernel_spmd as _run

    nc = _bacc.Bacc("TRN2", target_bir_lowering=False, num_devices=1)
    arrays, views = {}, {}
    for name in _INS:
        v = _np.ascontiguousarray(inputs[name])
        arrays[f"in_{name}"] = v
        views[name] = nc.dram_tensor(f"in_{name}", v.shape, _mybir.dt.from_np(v.dtype), kind="ExternalInput").ap()
    x = arrays["in_x"]
    out = nc.dram_tensor("out_y", x.shape, _mybir.dt.from_np(x.dtype), kind="ExternalOutput").ap()
    build_trunk(nc, views, out)
    r = _run(nc, [arrays], core_ids=[0])
    return r.results[0]["out_y"]
```

```python
from contextlib import ExitStack

import concourse.bass as bass
from concourse import mybir

F32 = mybir.dt.float32
F32R = mybir.dt.float32r
I32 = mybir.dt.int32
U32 = mybir.dt.uint32
ALU = mybir.AluOpType
ACT = mybir.ActivationFunctionType
AX_X = mybir.AxisListType.X

P = 128
KB = 1024
CHUNK, HEAD, Q_PER_KV = 64, 64, 4
COLS = 512
PIECE = 2048
ROUND = 4
EPS = 1e-6
DENSE_RAW, DENSE_PARTS = 4, 2
EXP_RAW, EXP_PARTS = 6, 3
LOWEST = -3.0e38


class Chain:

    def __init__(self, eng, sem, base=0):
        self.eng, self.sem, self.base, self.n = eng, sem, base, 0

    def mark(self, ins):
        self.n += 1
        return ins.then_inc(self.sem, 1)

    def wait(self):
        self.eng.wait_ge(self.sem, self.base + self.n)

    def link(self, ins):
        self.mark(ins)
        self.wait()


def build_trunk(nc, a, out):
    T, D = a["x"].shape[1], a["x"].shape[2]
    TT, KT = T // P, D // P
    IN_W = a["w_in"].shape[2]
    SGU_W = a["norm_v_g"].shape[1]
    NH = a["attn_sinks"].shape[1]
    NKV = NH // Q_PER_KV
    ATT_W, KV_W = NH * HEAD, NKV * HEAD
    K_OFF, V_OFF = ATT_W, ATT_W + KV_W
    U_OFF, VS_OFF = ATT_W + 2 * KV_W, ATT_W + 2 * KV_W + SGU_W
    SG = a["w_spatial"].shape[1]
    KB2 = SGU_W // P
    NG = a["w_router_group"].shape[2]
    NE = a["w_router_expert"].shape[2]
    EPG = NE // NG
    FF = a["w_e_gate"].shape[3]
    NR = NG + NE
    A1, A2 = 3, IN_W // COLS - 3
    NC = D // COLS
    C_ROUND0 = A1 + A2
    D_ROUND0 = C_ROUND0 + 3 * NC
    DENSE = ROUND * (D_ROUND0 + NC)
    PER_G = 6 * EPG
    assert TT == 2 and KT == 16 and A2 == NKV == 4 and NC == 4 and KB2 == 8 and SG == 8 and FF == 256
    SCALE = float(HEAD) ** -0.5

    with ExitStack() as ctx:
        base = (nc.sbuf_base + 31) // 32 * 32
        room = (nc.sbuf_usable_end - base) // 32 * 32
        ctx.enter_context(nc.sbuf_tensor("arena", [P, room // 4], F32))

        def at(name, kb, shape, dt=F32):
            nbytes = 4
            for n in shape[1:]:
                nbytes *= n
            assert kb * KB + nbytes <= room, name
            return nc.alloc_sbuf_tensor_at(name, shape, dt, offset=base + int(kb * KB))

        def sem(name):
            return ctx.enter_context(nc.semaphore(name))

        bank = [ctx.enter_context(nc.psum_tensor(f"bank{i}", [P, COLS], F32)) for i in range(8)]

        resid = at("resid", 0, [P, TT, D])
        wsp = at("wsp", 0, [P, SG, P])
        yat = at("yat", 0, [P, 2, T])
        wspT = at("wspT", 4, [P, SG, P])
        gv = at("gv", 8, [P, SGU_W])
        probT = [at(f"probT{b}", 12 + 2 * b, [P, 4, P]) for b in range(2)]
        whi = at("whi", 16, [P, EXP_PARTS, PIECE], F32R)
        wlo = at("wlo", 40, [P, EXP_PARTS, PIECE], F32R)
        actT_hi = at("actT_hi", 64, [P, KT, T], F32R)
        actT_lo = at("actT_lo", 80, [P, KT, T], F32R)
        x2_hi = actT_hi[:].rearrange("p k t -> p (k t)").rearrange("p (t d) -> p t d", t=TT)
        x2_lo = actT_lo[:].rearrange("p k t -> p (k t)").rearrange("p (t d) -> p t d", t=TT)
        raw = at("raw", 96, [P, DENSE_RAW, PIECE])
        xg_hi = at("xg_hi", 96, [P, KT, P], F32R)
        xg_lo = at("xg_lo", 104, [P, KT, P], F32R)
        o_hi = at("o_hi", 112, [P, D], F32R)
        o_lo = at("o_lo", 120, [P, D], F32R)
        y_out = at("y_out", 96, [P, TT, D])
        xraw = at("xraw", 128, [P, EXP_RAW, PIECE])
        x0 = at("x0", 128, [P, TT, D])
        xs0 = at("xs0", 144, [P, 4 * TT, KT // 4, P])
        g_rows = at("g_rows", 160, [2 * KT, P])
        sq0 = at("sq0", 168, [P, D])
        proj = at("proj", 128, [P, TT, IN_W])
        merged = at("merged", 128, [P, TT, D])
        sga = at("sga", 144, [P, TT, COLS])
        sgb = at("sgb", 148, [P, TT, COLS])
        gyb = at("gyb", 152, [P, TT, COLS])
        yaT_hi = at("yaT_hi", 156, [P, KB2, T], F32R)
        yaT_lo = at("yaT_lo", 164, [P, KB2, T], F32R)
        ybT_hi = at("ybT_hi", 172, [P, KB2, T], F32R)
        ybT_lo = at("ybT_lo", 180, [P, KB2, T], F32R)
        sq_v = at("sq_v", 172, [P, SGU_W])
        s_act = at("s_act", 176, [P, FF])
        hid = at("hid", 177, [P, FF])
        hT_hi = at("hT_hi", 178, [P, 2, P], F32R)
        hT_lo = at("hT_lo", 179, [P, 2, P], F32R)
        sel = at("sel", 180, [P, TT, P], F32R)
        selT = at("selT", 181, [P, T], F32R)
        sq2 = at("sq2", 180, [P, D])
        hg = [at("hg0", 32, [P, D]), at("hg1", 56, [P, D])]
        h_chunk = at("h_chunk", 176, [P, TT, COLS])
        hT = at("hT", 182, [P, COLS // P, T])
        sq_h = at("sq_h", 186, [P, COLS])
        bias_a = at("bias_a", 188, [P, COLS])
        bias_b = at("bias_b", 190, [P, COLS])
        ident = at("ident", 192, [P, P])
        ident_r = at("ident_r", 192.5, [P, P], F32R)
        before = at("before", 193, [P, P])
        ones = at("ones", 193.5, [P, P])
        slot_no = at("slot_no", 194, [P, P])
        qkv = at("qkv", 194.5, [P, TT, (Q_PER_KV + 2) * HEAD])
        qT = at("qT", 197.5, [HEAD, T // CHUNK, Q_PER_KV, CHUNK])
        kT = at("kT", 201.5, [HEAD, T])
        prob = [at(f"prob{b}", 202.5 + 2 * b, [P, 4, P]) for b in range(2)]
        gbig = at("gbig", 196.875, [P, D])
        wr = at("wr", 194.5, [P, KT, NR])
        small_at = [206.5]

        def small(name, shape, dt=F32):
            n = 4
            for s in shape[1:]:
                n *= s
            t = at(name, small_at[0], shape, dt)
            small_at[0] += (n + 31) // 32 * 32 / KB
            return t

        ssq = small("ssq", [P, 4 * TT])
        ms = small("ms", [P, 4 * TT])
        rstd = small("rstd", [P, 4 * TT])
        gT = small("gT", [P, 2 * KT])
        credit = small("credit", [P, 16])
        bsT = small("bsT", [P, SG])
        sink_row = small("sink_row", [P, NH])
        sinkv = small("sinkv", [P, NKV, 2, 2])
        mx = small("mx", [P, 2, 4])
        nmx = small("nmx", [P, 2, 4])
        sdiff = small("sdiff", [P, 2, 4])
        rsum = small("rsum", [P, 2, 4])
        esink = small("esink", [P, 2, 4])
        rden = small("rden", [P, 2, 4])
        vmid = small("vmid", [P, HEAD])
        bs8 = at("bs8", 202.5, [SG, P])
        br = at("br", 188, [P, NR])

        def rsmall(name, shape, dt=F32):
            t = small(name, shape, dt)
            assert small_at[0] <= 192, name
            return t

        small_at[0] = 188.25
        lg = rsmall("lg", [P, TT, NR])
        lgs = rsmall("lgs", [P, TT, NR])
        ssq_h = rsmall("ssq_h", [P, TT, NC])
        gl8 = rsmall("gl8", [P, TT, 8])
        gm8 = rsmall("gm8", [P, TT, 8])
        gi8 = rsmall("gi8", [P, TT, 8], U32)
        gif = rsmall("gif", [P, TT, 8])
        ngm = rsmall("ngm", [P, TT])
        gexp = rsmall("gexp", [P, TT, NG])
        gsum = rsmall("gsum", [P, TT])
        gval = rsmall("gval", [P, TT])
        goh = rsmall("goh", [P, TT, NG])
        own = rsmall("own", [P, TT, NG, EPG])
        inl = rsmall("inl", [P, TT, EPG])
        em8 = rsmall("em8", [P, TT, 8])
        ei8 = rsmall("ei8", [P, TT, 8], U32)
        eif = rsmall("eif", [P, TT, 8])
        ed = rsmall("ed", [P, TT])
        ee = rsmall("ee", [P, TT])
        es1 = rsmall("es1", [P, TT])
        ew0 = rsmall("ew0", [P, TT])
        ew1 = rsmall("ew1", [P, TT])
        ca = rsmall("ca", [P, TT, EPG + 2])
        cb = rsmall("cb", [P, TT, EPG])
        cw_hi = rsmall("cw_hi", [P, TT, EPG + 2], F32R)
        cw_lo = rsmall("cw_lo", [P, TT, EPG + 2], F32R)
        rkp = rsmall("rkp", [P, TT, NG])
        rank = rsmall("rank", [P, TT])
        fits = rsmall("fits", [P, TT])
        over = rsmall("over", [P, TT])
        rk1 = rsmall("rk1", [P, TT])
        rk2 = rsmall("rk2", [P, TT])
        pos = rsmall("pos", [P, TT, NG + 1])
        ovg = rsmall("ovg", [P, NG])
        ovn = rsmall("ovn", [P, NG])
        ctlf = rsmall("ctlf", [P, 2])
        ctl = rsmall("ctl", [P, 2], I32)
        cw = rsmall("cw", [P, EPG + 2])

        x_in = [sem(f"x_in{n}") for n in range(2 * TT)]
        g_in, gv_in, wsp_in, bs_in, sink_in = (sem(n) for n in ("g_in", "gv_in", "wsp_in", "bs_in", "sink_in"))
        raw_in = [sem(f"raw_in{s}") for s in range(DENSE_RAW)]
        xraw_in = [sem(f"xraw_in{s}") for s in range(EXP_RAW)]
        bias_a_in, bias_b_in = sem("bias_a_in"), sem("bias_b_in")
        resid_in, g2_in, wr_in, br_in, gf_in = (sem(n) for n in ("resid_in", "g2_in", "wr_in", "br_in", "gf_in"))
        out_done = sem("out_done")
        hi_made, lo_made, piece_used = sem("hi_made"), sem("lo_made"), sem("piece_used")
        consts, ident_r_made, small_made = sem("consts"), sem("ident_r_made"), sem("small_made")
        ssq_made, mean_made, ms_made, rstd_made = (sem(n) for n in ("ssq_made", "mean_made", "ms_made", "rstd_made"))
        gT_full, gT_made = sem("gT_full"), sem("gT_made")
        xs_made, xT_full, xT_hi_made, xT_lo_made = sem("xs_made"), sem("xT_full"), sem("xT_hi_made"), sem("xT_lo_made")
        wspT_full, wspT_made = sem("wspT_full"), sem("wspT_made")
        acc_full, acc_free = sem("acc_full"), sem("acc_free")
        gb_full, gb_free = sem("gb_full"), sem("gb_free")
        ya_full, ya_free = sem("ya_full"), sem("ya_free")
        yb_full, yb_free = sem("yb_full"), sem("yb_free")
        ga_sig, gb_sig, gyb_made = sem("ga_sig"), sem("gb_sig"), sem("gyb_made")
        qkv_made, qkT_full, qkT_made, vmid_made = sem("qkv_made"), sem("qkT_full"), sem("qkT_made"), sem("vmid_made")
        sc_full, max_made, exp_made, prob_made = sem("sc_full"), sem("max_made"), sem("exp_made"), sem("prob_made")
        pT_full, pT_made, ya_t_full, yat_made = sem("pT_full"), sem("pT_made"), sem("ya_t_full"), sem("yat_made")
        yaT_hi_made, yaT_lo_made = sem("yaT_hi_made"), sem("yaT_lo_made")
        gelu_v, gelu_u, vn_made, mix_full, yb_made = (sem(n) for n in ("gelu_v", "gelu_u", "vn_made", "mix_full", "yb_made"))
        ybT_full, ybT_hi_made, ybT_lo_made = sem("ybT_full"), sem("ybT_hi_made"), sem("ybT_lo_made")
        mT_full, mT_hi_made, mT_lo_made = sem("mT_full"), sem("mT_hi_made"), sem("mT_lo_made")
        wr_made, hg_made, hT_h_full, hT_h_made = sem("wr_made"), sem("hg_made"), sem("hT_h_full"), sem("hT_h_made")
        sq_h_made, lgs_made = sem("sq_h_made"), sem("lgs_made")
        h_chunk_made = sem("h_chunk_made")
        x2_hi_made, x2_lo_made, lg_full = sem("x2_hi_made"), sem("x2_lo_made"), sem("lg_full")
        gmax_made, gexp_made, goh_made, rank_full = sem("gmax_made"), sem("gexp_made"), sem("goh_made"), sem("rank_full")
        ed_made, ee_made, cwparts_made, ctl_made = sem("ed_made"), sem("ee_made"), sem("cwparts_made"), sem("ctl_made")
        sel_made, selT_full, selT_made, cw_made = sem("sel_made"), sem("selT_full"), sem("selT_made"), sem("cw_made")
        cw_full = sem("cw_full")
        xg_full, xg_hi_made, xg_lo_made = sem("xg_full"), sem("xg_hi_made"), sem("xg_lo_made")
        silu_made, hid_made = sem("silu_made"), sem("hid_made")
        hT_full, hT_hi_made, hT_lo_made = sem("hT_full"), sem("hT_hi_made"), sem("hT_lo_made")
        o_full, o_hi_made, o_lo_made = sem("o_full"), sem("o_hi_made"), sem("o_lo_made")
        scat_full, added = sem("scat_full"), sem("added")
        y_made = sem("y_made")
        v_order, v_att, v_c, pool_order = sem("v_order"), sem("v_att"), sem("v_c"), sem("pool_order")
        a_att = sem("a_att")

        block = ctx.enter_context(nc.Block())

        def await_used(eng, n):
            eng.wait_ge(piece_used, n + (DENSE_PARTS + 1))

        def await_chunk(eng, t, full, n, last_piece):
            if t == 0:
                eng.wait_ge(full, n + 1)
            else:
                await_used(eng, last_piece)

        OUT_BANKS = (2, 3, 4, 5)
        GATHER_BANKS = (6, 7, 0, 6)
        SCATTER = [(2, 0, 0), (3, 0, 1), (4, 1, 0), (5, 1, 1), (6, 2, 0), (7, 2, 1), (6, 3, 0), (7, 3, 1)]
        SCATTER_LAST = [(6, 0, 0), (7, 1, 0), (0, 2, 0), (1, 3, 0), (2, 0, 1), (3, 1, 1), (4, 2, 1), (5, 3, 1)]

        x_v = a["x"].rearrange("b (t p) d -> p (b t) d", p=P)
        out_v = out.rearrange("b (t p) d -> p (b t) d", p=P)

        def chunked(w):
            return w[0].rearrange("(k p) (c n) -> p k c n", p=P, n=COLS)

        w_in_v, w_gate_v, w_out_v = chunked(a["w_in"]), chunked(a["w_gate"]), chunked(a["w_out"])
        w_a_v, w_b_v = chunked(a["w_branch_a"]), chunked(a["w_branch_b"])
        b_in_v = a["b_in"].rearrange("a (c n) -> a c n", n=COLS)
        b_gate_v = a["b_gate"].rearrange("a (c n) -> a c n", n=COLS)
        wg_v = a["w_e_gate"][0].rearrange("e (p k) f -> e p k f", p=P)
        wu_v = a["w_e_up"][0].rearrange("e (p k) f -> e p k f", p=P)
        wd_v = a["w_e_down"][0].rearrange("e (k p) d -> e p k d", p=P)

        def wide(row):
            return row.partition_broadcast(P).rearrange("p a n -> p (a n)")

        @block.sync
        def _(sp):
            def load_piece(r, k, view, kt, c):
                sp.wait_ge(lo_made, ROUND * r + k + 1)
                for h in range(2):
                    sp.dma_start(raw[:, k, h * KB:(h + 1) * KB].rearrange("p (k n) -> p k n", n=COLS),
                                 view[:, kt + 2 * h:kt + 2 * h + 2, c, :]).then_inc(raw_in[k], 16)

            def load_round(r, views):
                for k, (view, kt, c) in enumerate(views):
                    load_piece(r, k, view, kt, c)

            def full(view, c):
                return [(view, 4 * k, c) for k in range(4)]

            def load_bias(tile, row, arrived, freed, n):
                sp.wait_ge(freed, 2 * n + 2)
                sp.dma_start(tile[:], wide(row)).then_inc(arrived, 16)

            for n, gain in enumerate(("norm_mix_g", "norm_ffn_g")):
                sp.dma_start(g_rows[n * KT:(n + 1) * KT, :],
                             a[gain].rearrange("a (k p) -> (a k) p", p=P)).then_inc(g_in, 16)
            for t in range(TT):
                for h in range(2):
                    cols = slice(h * D // 2, (h + 1) * D // 2)
                    sp.dma_start(x0[:, t, cols], x_v[:, t, cols]).then_inc(x_in[2 * t + h], 16)
                if t == 0:
                    load_piece(0, 0, w_in_v, 0, 0)
            for k in range(1, ROUND):
                load_piece(0, k, w_in_v, 4 * k, 0)
            load_bias(bias_a, b_in_v[:, 0, :], bias_a_in, acc_free, 0)
            sp.dma_start(wsp[:], a["w_spatial"][0].rearrange("g i j -> i g j")).then_inc(wsp_in, 16)
            sp.dma_start(bs8[:], a["b_spatial"][0]).then_inc(bs_in, 16)
            sp.dma_start(sink_row[:], wide(a["attn_sinks"])).then_inc(sink_in, 16)
            with sp.Fori(1, A1 + A2) as c:
                load_round(c, full(w_in_v, c))
                load_bias(bias_a, b_in_v[:, c, :], bias_a_in, acc_free, c)
            sp.dma_start(gv[:], wide(a["norm_v_g"])).then_inc(gv_in, 16)

            def load_c(n, extra=None):
                r = C_ROUND0 + 3 * n
                load_round(r, full(w_gate_v, n))
                load_bias(bias_a, b_gate_v[:, n, :], bias_a_in, acc_free, A1 + A2 + n)
                load_round(r + 1, full(w_gate_v, NC + n))
                load_bias(bias_b, b_gate_v[:, NC + n, :], bias_b_in, gb_free, n)
                load_round(r + 2, [(w_a_v, 0, n), (w_a_v, 4, n), (w_b_v, 0, n), (w_b_v, 4, n)])

            load_c(0)
            sp.wait_ge(ybT_lo_made, 4)
            for t in range(TT):
                sp.dma_start(resid[:, t, :], x_v[:, t, :]).then_inc(resid_in, 16)
            sp.wait_ge(yaT_lo_made, NKV)
            sp.dma_start(gbig[:], wide(a["norm_ffn_g"])).then_inc(g2_in, 16)
            sp.dma_start(wr[:, :, 0:NG], a["w_router_group"][0].rearrange("(k p) n -> p k n", p=P)).then_inc(wr_in, 16)
            sp.dma_start(wr[:, :, NG:NR], a["w_router_expert"][0].rearrange("(k p) n -> p k n", p=P)).then_inc(wr_in, 16)
            with sp.Fori(1, NC) as n:
                load_c(n)
            def load_expert(i, e, m, kind, k):
                s, use = m % EXP_RAW, PER_G // EXP_RAW * i + m // EXP_RAW
                if kind == "gu":
                    for h, view in enumerate((wg_v, wu_v)):
                        sp.dma_start(xraw[:, s, h * KB:(h + 1) * KB].rearrange("p (k f) -> p k f", f=FF),
                                     view[e, :, 4 * k:4 * k + 4, :]).then_inc(xraw_in[s], 16)
                else:
                    for h in range(2):
                        sp.dma_start(xraw[:, s, h * KB:(h + 1) * KB],
                                     wd_v[e, :, k, h * KB:(h + 1) * KB]).then_inc(xraw_in[s], 16)

            def await_slot(i, m):
                sp.wait_ge(lo_made, DENSE_RAW + DENSE + PER_G * i + m - EXP_RAW + 1)

            for n in range(NC):
                load_round(D_ROUND0 + n, full(w_out_v, n))
                if n == 0:
                    sp.wait_ge(mT_lo_made, 2 * NC)
                    sp.wait_ge(acc_free, 2 * (A1 + A2 + NC) + 2)
                    sp.wait_ge(gb_free, 2 * NC + 2)
                    sp.dma_start(br[:, 0:NG], wide(a["b_router_group"])).then_inc(br_in, 16)
                    sp.dma_start(br[:, NG:NR], wide(a["b_router_expert"])).then_inc(br_in, 16)
                for m in range(2 * n, min(2 * n + 2, EXP_RAW)):
                    if m < 4:
                        load_expert(0, 0, m, "gu", m)
                    else:
                        load_expert(0, 1, m, "gu", m - 4)
            sp.wait_ge(hg_made, TT * NC)
            sp.dma_start(gbig[:], wide(a["norm_final_g"].rearrange("(a n) -> a n", a=1))).then_inc(gf_in, 16)

            def load_step(i, e, j, gu_from=0):
                for k in range(gu_from, 4):
                    await_slot(i, 6 * j - 2 + k)
                    load_at(i, e + j, j, k, "gu", k)
                for k in range(2):
                    await_slot(i, 6 * j + 2 + k)
                    load_at(i, e + j - 1, j, 4 + k, "down", k)

            def load_at(i, e, j, q, kind, k):
                s = (4 + q) % EXP_RAW
                if kind == "gu":
                    for h, view in enumerate((wg_v, wu_v)):
                        sp.dma_start(xraw[:, s, h * KB:(h + 1) * KB].rearrange("p (k f) -> p k f", f=FF),
                                     view[e, :, 4 * k:4 * k + 4, :]).then_inc(xraw_in[s], 16)
                else:
                    for h in range(2):
                        sp.dma_start(xraw[:, s, h * KB:(h + 1) * KB],
                                     wd_v[e, :, k, h * KB:(h + 1) * KB]).then_inc(xraw_in[s], 16)

            def load_tail(i, e):
                for k in range(2):
                    await_slot(i, PER_G - 2 + k)
                    load_expert(0, e + EPG - 1, PER_G - 2 + k, "down", k)

            def load_group(i, e):
                for k in range(4):
                    await_slot(i, k)
                    load_expert(0, e, k, "gu", k)
                with sp.Fori(1, EPG) as j:
                    load_step(i, e, j)
                load_tail(i, e)

            load_step(0, 0, 1, gu_from=2)
            with sp.Fori(2, EPG) as j:
                load_step(0, 0, j)
            load_tail(0, 0)
            with sp.Fori(1, NG) as i:
                load_group(i, i * EPG)
            sp.wait_ge(ctl_made, 1)
            more = sp.value_load(ctl[0:1, 0:1], min_val=0, max_val=1)
            group = sp.value_load(ctl[0:1, 1:2], min_val=0, max_val=NG - 1)
            with sp.If(more == 1):
                load_group(NG, group * EPG)
            for t in range(TT):
                sp.wait_ge(y_made, t + 1)
                sp.dma_start(out_v[:, t, :], y_out[:, t, :]).then_inc(out_done, 16)
            sp.wait_ge(out_done, 16 * TT)

        @block.gpsimd
        def _(pool):
            order = Chain(pool, pool_order)
            pool.memset(ident[:], 0.0).then_inc(pool_order, 1)
            pool.memset(before[:], 1.0).then_inc(pool_order, 1)
            pool.memset(ones[:], 1.0).then_inc(pool_order, 1)
            pool.iota(slot_no[:], [[1, P]], base=0, channel_multiplier=0,
                      allow_small_or_imprecise_dtypes=True).then_inc(pool_order, 1)
            pool.memset(wspT[:], 0.0).then_inc(pool_order, 1)
            order.n = 5
            order.wait()
            order.link(pool.affine_select(out=ident[:], in_=ident[:], compare_op=ALU.not_equal, fill=1.0,
                                          base=0, pattern=[[-1, P]], channel_multiplier=1))
            order.link(pool.affine_select(out=before[:], in_=before[:], compare_op=ALU.is_gt, fill=0.0,
                                          base=0, pattern=[[1, P]], channel_multiplier=-1))
            pool.memset(credit[:, 15:16], 0.0).then_inc(consts, 1)

            def permuted(tile, chunk):
                return tile.rearrange("t (k p) -> t k p", p=P)[:, :, bass.ds(chunk * (COLS // KT), COLS // KT)]

            pool.wait_ge(g2_in, 16)
            with pool.Fori(0, NC) as n:
                for t in range(TT):
                    pool.wait_ge(acc_free, 2 * (A1 + A2 + NC) + 2 + 2 * n + t + 1)
                    cols = bass.ds(n * COLS, COLS)
                    pool.tensor_tensor(permuted(hg[t][:], n),
                                       resid[:, t, cols].rearrange("t (p k) -> t k p", k=KT),
                                       gbig[:, cols].rearrange("t (p k) -> t k p", k=KT), ALU.mult).then_inc(hg_made, 1)
            for t in range(TT):
                pool.wait_ge(x2_hi_made, t + 1)
                pool.tensor_tensor(x2_lo[:, t, :], hg[t][:], x2_hi[:, t, :], ALU.subtract).then_inc(x2_lo_made, 1)

        @block.scalar
        def _(act):
            def make_hi(slot, arrived, use, src):
                act.wait_ge(arrived, 32 * use + 32)
                return act.activation(whi[:, slot, :], src, ACT.Copy)

            def dense_hi(r, k):
                act.wait_ge(piece_used, ROUND * r + k + 1)
                make_hi(k % DENSE_PARTS, raw_in[k], r, raw[:, k, :]).then_inc(hi_made, 1)

            def sum_squares(n, src, junk):
                act.activation(junk, src, ACT.Square, accum_out=ssq[:, n:n + 1]).then_inc(ssq_made, 1)

            def root(n):
                act.wait_ge(ms_made, n + 1)
                act.activation(rstd[:, n:n + 1], ms[:, n:n + 1], ACT.Sqrt).then_inc(rstd_made, 1)

            for u in range(8):
                if u == 4:
                    dense_hi(0, 0)
                act.wait_ge(xs_made, u + 1)
                t, k4 = divmod(u, 4)
                act.activation(actT_hi[:, 4 * k4:4 * k4 + 4, t * P:(t + 1) * P], xs0[:, u, :, :],
                               ACT.Copy).then_inc(xT_hi_made, 1)
            act.activation(ident_r[:], ident[:], ACT.Copy).then_inc(ident_r_made, 1)
            dense_hi(0, 1)
            for t in range(TT):
                if t:
                    act.wait_ge(ssq_made, t)
                sum_squares(t, x0[:, t, :], sq0[:])
            dense_hi(0, 2)
            for t in range(TT):
                root(t)
            dense_hi(0, 3)

            with act.Fori(1, A1) as c:
                for k in range(ROUND):
                    dense_hi(c, k)

            def evac_heads(g):
                act.wait_ge(ya_t_full, 2 * g + 2)
                for b in range(2):
                    for h2 in range(2):
                        ins = act.activation(
                            yat[h2 * HEAD:(h2 + 1) * HEAD, :, b * P:(b + 1) * P].rearrange("p r (c q) -> p c r q", c=2),
                            bank[3 + b][0:HEAD, :].rearrange("p (c r h q) -> p c r h q", c=2, r=2, h=2)[:, :, :, h2, :],
                            ACT.Copy)
                        ins.then_inc(yat_made, 1)
                act.wait_ge(yat_made, 4 * g + 4)
                act.activation(yaT_hi[:, bass.ds(2 * g, 2), :], yat[:], ACT.Copy).then_inc(yaT_hi_made, 1)

            def attention_a(g, r, first):
                dense_hi(r, 0)
                if not first:
                    evac_heads(g - 1)
                else:
                    act.wait_ge(acc_free, 2 + 2 * A1)
                act.activation(qkv[:, :, 0:4 * HEAD], proj[:, :, bass.ds(4 * HEAD * g, 4 * HEAD)],
                               ACT.Copy).then_inc(qkv_made, 1)
                act.activation(qkv[:, :, 4 * HEAD:5 * HEAD], proj[:, :, bass.ds(HEAD * g + K_OFF, HEAD)],
                               ACT.Copy).then_inc(qkv_made, 1)
                act.activation(qkv[:, :, 5 * HEAD:6 * HEAD], proj[:, :, bass.ds(HEAD * g + V_OFF, HEAD)],
                               ACT.Copy).then_inc(qkv_made, 1)
                dense_hi(r, 1)
                act.wait_ge(qkT_full, 3 * g + 3)
                for t in range(TT):
                    act.activation(qT[:, 2 * t:2 * t + 2, :, :].rearrange("p c h q -> p h c q"),
                                   bank[2 + t][0:HEAD, :].rearrange("p (h c q) -> p h c q", h=4, c=2),
                                   ACT.Copy).then_inc(qkT_made, 1)
                act.activation(kT[:], bank[4][0:HEAD, 0:T], ACT.Copy).then_inc(qkT_made, 1)
                dense_hi(r, 2)
                for b in range(2):
                    act.wait_ge(max_made, 2 * g + b + 1)
                    for tile in range(4):
                        w = CHUNK if b == 0 and tile < 2 else P
                        act.activation(prob[b][:, tile, 0:w], bank[5 + b][:, tile * P:tile * P + w], ACT.Exp,
                                       bias=nmx[:, b, tile:tile + 1], scale=SCALE,
                                       accum_out=rsum[:, b, tile:tile + 1]).then_inc(a_att, 1)
                    act.activation(esink[:, b, :], sdiff[:, b, :], ACT.Exp).then_inc(exp_made, 1)
                dense_hi(r, 3)
                for b in range(2):
                    act.wait_ge(pT_full, 2 * g + b + 1)
                    src = bank[7 if b == 0 else 2]
                    if b == 0:
                        act.activation(probT[0][0:CHUNK, 0:2, :], src[0:CHUNK, 0:2 * P].rearrange("p (a b) -> p a b", a=2),
                                       ACT.Copy).then_inc(pT_made, 1)
                        act.activation(probT[0][:, 2:4, :], src[:, 2 * P:4 * P].rearrange("p (a b) -> p a b", a=2),
                                       ACT.Copy).then_inc(pT_made, 1)
                    else:
                        act.activation(probT[1][:], src[:].rearrange("p (a b) -> p a b", a=4),
                                       ACT.Copy).then_inc(pT_made, 1)

            attention_a(0, A1, True)
            with act.Fori(1, NKV) as g:
                attention_a(g, A1 + g, False)

            def rounds_c(n, r, first):
                dense_hi(r, 0)
                if first:
                    evac_heads(NKV - 1)
                dense_hi(r, 1)
                if first:
                    act.wait_ge(acc_free, 2 + 2 * (A1 + A2))
                    for t in range(TT):
                        act.activation(proj[:, t, VS_OFF:VS_OFF + SGU_W], proj[:, t, VS_OFF:VS_OFF + SGU_W],
                                       ACT.Gelu_apprx_tanh).then_inc(gelu_v, 1)
                    for t in range(TT):
                        act.wait_ge(gelu_v, t + 1)
                        act.wait_ge(ssq_made, TT + t)
                        sum_squares(TT + t, proj[:, t, VS_OFF:VS_OFF + SGU_W], sq_v[:])
                dense_hi(r, 2)
                if first:
                    for t in range(TT):
                        root(TT + t)
                    for t in range(TT):
                        act.activation(proj[:, t, U_OFF:U_OFF + SGU_W], proj[:, t, U_OFF:U_OFF + SGU_W],
                                       ACT.Gelu_apprx_tanh).then_inc(gelu_u, 1)
                dense_hi(r, 3)
                dense_hi(r + 1, 0)
                dense_hi(r + 1, 1)
                act.wait_ge(acc_free, 2 * (A1 + A2) + 2 * n + 4)
                act.activation(sga[:], sga[:], ACT.Sigmoid).then_inc(ga_sig, 1)
                dense_hi(r + 1, 2)
                if first:
                    for u in range(4):
                        act.wait_ge(ybT_full, u + 1)
                        t, k4 = divmod(u, 2)
                        act.activation(ybT_hi[:, 4 * k4:4 * k4 + 4, t * P:(t + 1) * P],
                                       bank[4 + u][:].rearrange("p (k t) -> p k t", k=4),
                                       ACT.Copy).then_inc(ybT_hi_made, 1)
                dense_hi(r + 1, 3)
                dense_hi(r + 2, 0)
                dense_hi(r + 2, 1)
                act.wait_ge(gb_free, 2 * n + 4)
                act.activation(sgb[:], sgb[:], ACT.Sigmoid).then_inc(gb_sig, 1)
                dense_hi(r + 2, 2)
                dense_hi(r + 2, 3)

            rounds_c(0, C_ROUND0, True)
            with act.Fori(1, NC) as n:
                rounds_c(n, 3 * n + C_ROUND0, False)

            dense_hi(D_ROUND0, 0)
            dense_hi(D_ROUND0, 1)
            for u in range(2 * NC):
                act.wait_ge(mT_full, u + 1)
                n, t = divmod(u, TT)
                act.activation(actT_hi[:, 4 * n:4 * n + 4, t * P:(t + 1) * P],
                               bank[u][:].rearrange("p (k t) -> p k t", k=4), ACT.Copy).then_inc(mT_hi_made, 1)
            dense_hi(D_ROUND0, 2)
            dense_hi(D_ROUND0, 3)

            def residual_squares(n):
                for t in range(TT):
                    act.wait_ge(acc_free, 2 * (A1 + A2 + NC) + 2 + 2 * n + t + 1)
                    act.wait_ge(sq_h_made, 2 * n + t + 1)
                    act.activation(sq_h[:], resid[:, t, bass.ds(n * COLS, COLS)], ACT.Square,
                                   accum_out=ssq_h[:, t, bass.ds(n, 1)]).then_inc(sq_h_made, 1)

            def residual_turned(n):
                for t in range(TT):
                    act.wait_ge(hT_h_full, 2 * n + t + 1)
                    act.activation(hT[:, :, t * P:(t + 1) * P], bank[2 + t][:].rearrange("p (k t) -> p k t", k=4),
                                   ACT.Copy).then_inc(hT_h_made, 1)

            with act.Fori(1, NC) as n:
                dense_hi(n + D_ROUND0, 0)
                dense_hi(n + D_ROUND0, 1)
                for t in range(TT):
                    act.wait_ge(acc_free, 2 * (A1 + A2 + NC) + 2 * n + t + 1)
                    act.wait_ge(hT_h_made, 2 * n)
                    act.activation(h_chunk[:, t, :], resid[:, t, bass.ds(n * COLS - COLS, COLS)],
                                   ACT.Copy).then_inc(h_chunk_made, 1)
                residual_squares(n - 1)
                dense_hi(n + D_ROUND0, 2)
                residual_turned(n - 1)
                dense_hi(n + D_ROUND0, 3)

            residual_turned(NC - 1)
            residual_squares(NC - 1)
            await_used(act, DENSE - 1)
            for t in range(TT):
                act.wait_ge(hg_made, TT * (NC - 1) + t + 1)
                act.activation(x2_hi[:, t, :], hg[t][:], ACT.Copy).then_inc(x2_hi_made, 1)
                if t == 0:
                    for t2 in range(TT):
                        root(2 * TT + t2)
            act.wait_ge(gmax_made, 1)
            for t in range(TT):
                act.activation(gexp[:, t, :], lg[:, t, 0:NG], ACT.Exp, bias=ngm[:, t:t + 1],
                               accum_out=gsum[:, t:t + 1]).then_inc(gexp_made, 1)
            act.wait_ge(ed_made, 1)
            act.activation(ee[:], ed[:], ACT.Exp).then_inc(ee_made, 1)

            def expert_hi(i, j, q):
                m = 6 * j - 2 + q
                act.wait_ge(piece_used, DENSE + PER_G * i + m)
                s = (4 + q) % EXP_RAW
                use = PER_G // EXP_RAW * i + j - (1 if q < 2 else 0)
                make_hi((4 + q) % EXP_PARTS, xraw_in[s], use, xraw[:, s, :]).then_inc(hi_made, 1)

            def hidden_hi(i, j):
                act.wait_ge(hT_full, EPG * i + j + 1)
                act.activation(hT_hi[:], bank[1][:, 0:T].rearrange("p (a b) -> p a b", a=2),
                               ACT.Copy).then_inc(hT_hi_made, 1)

            def silu(i, j):
                await_used(act, PER_G * i + (DENSE + 3) if isinstance(j, int) and j == 0 else
                           PER_G * i + 6 * j + (DENSE + 1))
                act.activation(s_act[:], bank[0][:, 0:FF], ACT.Silu, scale=cw[:, EPG:EPG + 1]).then_inc(silu_made, 1)

            def gathered_hi(i, chunks):
                for k4 in chunks:
                    b = GATHER_BANKS[k4]
                    act.wait_ge(xg_full, 4 * i + k4 + 1)
                    act.activation(xg_hi[:, 4 * k4:4 * k4 + 4, :], bank[b][:].rearrange("p (k t) -> p k t", k=4),
                                   ACT.Copy).then_inc(xg_hi_made, 1)

            def output_hi(i, chunks):
                for b in chunks:
                    if b < 3:
                        act.wait_ge(o_full, 3 * i + b + 1)
                    else:
                        await_used(act, PER_G * i + (DENSE + PER_G - 1))
                    act.activation(o_hi[:, b * COLS:(b + 1) * COLS], bank[2 + b][:], ACT.Copy).then_inc(o_hi_made, 1)

            def group_a(i, after_another, another_follows):
                if not after_another:
                    expert_hi(i, 0, 2)
                    gathered_hi(i, range(4))
                expert_hi(i, 0, 3)
                if isinstance(i, int) and i == 0:
                    act.wait_ge(x2_lo_made, TT)
                expert_hi(i, 0, 4)
                if after_another:
                    output_hi(i - 1, range(0, 2))
                expert_hi(i, 0, 5)
                if after_another:
                    output_hi(i - 1, range(2, 4))
                expert_hi(i, 1, 0)
                expert_hi(i, 1, 1)
                act.wait_ge(cw_made, i + 1)
                silu(i, 0)
                expert_hi(i, 1, 2)
                hidden_hi(i, 0)
                for q in range(3, 6):
                    expert_hi(i, 1, q)
                silu(i, 1)
                expert_hi(i, 2, 0)
                expert_hi(i, 2, 1)
                hidden_hi(i, 1)
                act.wait_ge(selT_full, i + 1)
                act.activation(selT[:], bank[6][:, 0:T], ACT.Copy).then_inc(selT_made, 1)
                for q in range(2, 6):
                    expert_hi(i, 2, q)
                silu(i, 2)
                with act.Fori(3, EPG) as j:
                    expert_hi(i, j, 0)
                    expert_hi(i, j, 1)
                    hidden_hi(i, j - 1)
                    for q in range(2, 6):
                        expert_hi(i, j, q)
                    silu(i, j)
                expert_hi(i, EPG, 0)
                expert_hi(i, EPG, 1)
                if another_follows:
                    expert_hi(i + 1, 0, 2)
                    gathered_hi(i + 1, range(0, 2))
                hidden_hi(i, EPG - 1)
                if another_follows:
                    gathered_hi(i + 1, range(2, 4))
                else:
                    output_hi(i, range(4))

            group_a(0, False, True)
            with act.Fori(1, NG - 1) as i:
                group_a(i, True, True)
            group_a(NG - 1, True, False)
            act.wait_ge(ctl_made, 1)
            more = act.value_load(ctl[0:1, 0:1], min_val=0, max_val=1)
            with act.If(more == 1):
                group_a(NG, False, False)
            act.wait_ge(small_made, 1)
            for t in range(TT):
                act.wait_ge(ssq_made, 3 * TT + t)
                sum_squares(3 * TT + t, resid[:, t, :], sq2[:])
            for t in range(TT):
                root(3 * TT + t)

        @block.vector
        def _(dve):
            order = Chain(dve, v_order)

            def dense_lo(r, k):
                dve.wait_ge(hi_made, ROUND * r + k + 1)
                s = k % DENSE_PARTS
                dve.tensor_tensor(wlo[:, s, :], raw[:, k, :], whi[:, s, :], ALU.subtract).then_inc(lo_made, 1)

            for n, (s, count) in enumerate(((lo_made, DENSE_RAW), (acc_free, 2), (gb_free, 2), (ya_free, 2), (yb_free, 2),
                                                (hT_h_made, 2), (sq_h_made, 1))):
                dve.memset(credit[:, n:n + 1], 0.0).then_inc(s, count)
            def inverse_mean(k, width):
                for t in range(TT):
                    n = TT * k + t
                    dve.wait_ge(ssq_made, n + 1)
                    dve.tensor_scalar(ms[:, n:n + 1], ssq[:, n:n + 1], 1.0 / width, EPS,
                                      ALU.mult, ALU.add).then_inc(mean_made, 1)
                    dve.wait_ge(mean_made, n + 1)
                    dve.reciprocal(ms[:, n:n + 1], ms[:, n:n + 1]).then_inc(ms_made, 1)

            dve.wait_ge(gT_full, 1)
            dve.tensor_copy(gT[:], bank[7][:, 0:2 * KT]).then_inc(gT_made, 1)
            dve.wait_ge(gT_made, 1)

            def gain(u):
                dve.wait_ge(xT_full, u + 1)
                k4 = u % 4
                dve.tensor_tensor(xs0[:, u, :, :], bank[u][:].rearrange("p (k t) -> p k t", k=4),
                                  gT[:, 4 * k4:4 * k4 + 4].to_broadcast([P, 4, P]), ALU.mult).then_inc(xs_made, 1)

            def xT_low(u):
                dve.wait_ge(xT_hi_made, u + 1)
                t, k4 = divmod(u, 4)
                part = (slice(None), slice(4 * k4, 4 * k4 + 4), slice(t * P, (t + 1) * P))
                dve.tensor_tensor(actT_lo[part], xs0[:, u, :, :], actT_hi[part], ALU.subtract).then_inc(xT_lo_made, 1)

            gain(0)
            for u in range(1, 4):
                gain(u)
                xT_low(u - 1)
            xT_low(3)
            dense_lo(0, 0)
            gain(4)
            for u in range(5, 8):
                gain(u)
                xT_low(u - 1)
            xT_low(7)
            dense_lo(0, 1)
            inverse_mean(0, D)
            dense_lo(0, 2)
            dense_lo(0, 3)
            dve.wait_ge(wspT_full, 3)
            dve.wait_ge(consts, 1)
            for b in range(2):
                src = bank[4 + b][:].rearrange("p (g i) -> p g i", g=4)
                dve.tensor_copy(wspT[0:CHUNK, 4 * b:4 * b + 4, :], src[0:CHUNK]).then_inc(wspT_made, 1)
                dve.tensor_copy(wspT[CHUNK:P, 4 * b:4 * b + 4, CHUNK:P], src[CHUNK:P, :, CHUNK:P]).then_inc(wspT_made, 1)
            dve.tensor_copy(bsT[:], bank[6][:, 0:SG]).then_inc(wspT_made, 1)
            dve.wait_ge(sink_in, 16)
            for h2 in range(2):
                rows = slice(h2 * CHUNK, (h2 + 1) * CHUNK)
                src = sink_row[rows, :].rearrange("p (g r h) -> p g r h", g=NKV, r=2)[:, :, :, h2]
                for c2 in range(2):
                    order.mark(dve.tensor_copy(sinkv[rows, :, c2, :], src))
            order.wait()

            def evac_proj(c):
                dve.wait_ge(bias_a_in, 16 * c + 16)
                dve.wait_ge(rstd_made, TT)
                for t in range(TT):
                    await_chunk(dve, t, acc_full, c, ROUND * c + 3)
                    dve.scalar_tensor_tensor(out=proj[:, t, bass.ds(c * COLS, COLS)], in0=bank[t][:],
                                             scalar=rstd[:, t:t + 1], in1=bias_a[:],
                                             op0=ALU.mult, op1=ALU.add).then_inc(acc_free, 1)

            with dve.Fori(1, A1) as c:
                dense_lo(c, 0)
                evac_proj(c - 1)
                for k in range(1, ROUND):
                    dense_lo(c, k)

            ATT_LINKS = 18

            def heads_lo(g):
                dve.wait_ge(yaT_hi_made, g + 1)
                dve.tensor_tensor(yaT_lo[:, bass.ds(2 * g, 2), :], yat[:], yaT_hi[:, bass.ds(2 * g, 2), :],
                                  ALU.subtract).then_inc(yaT_lo_made, 1)

            def attention_v(g, r, first):
                steps = Chain(dve, v_att, ATT_LINKS * g)
                dense_lo(r, 0)
                evac_proj(r - 1)
                if not first:
                    heads_lo(g - 1)
                dense_lo(r, 1)
                dve.wait_ge(qkv_made, 3 * g + 3)
                dve.tensor_copy(vmid[0:CHUNK, :], qkv[0:CHUNK, 1, 5 * HEAD:6 * HEAD]).then_inc(vmid_made, 1)
                dve.tensor_copy(vmid[CHUNK:P, :], qkv[CHUNK:P, 0, 5 * HEAD:6 * HEAD]).then_inc(vmid_made, 1)
                dense_lo(r, 2)
                for b in range(2):
                    dve.wait_ge(sc_full, 2 * g + b + 1)
                    sc = bank[5 + b][:].rearrange("p (a k) -> p a k", a=4)
                    if b == 0:
                        steps.mark(dve.tensor_reduce(mx[:, b, 0:2], sc[:, 0:2, 0:CHUNK], AX_X, ALU.max))
                        steps.mark(dve.tensor_reduce(mx[:, b, 2:4], sc[:, 2:4, :], AX_X, ALU.max))
                    else:
                        steps.mark(dve.tensor_reduce(mx[:, b, :], sc, AX_X, ALU.max))
                    steps.wait()
                    sinks = sinkv[:, bass.ds(g, 1), :, :].rearrange("p a c r -> p (a c r)")
                    steps.link(dve.scalar_tensor_tensor(out=mx[:, b, :], in0=mx[:, b, :], scalar=SCALE, in1=sinks,
                                                        op0=ALU.mult, op1=ALU.max))
                    steps.link(dve.tensor_tensor(sdiff[:, b, :], sinks, mx[:, b, :], ALU.subtract))
                    dve.tensor_scalar(nmx[:, b, :], mx[:, b, :], -1.0, None, ALU.mult).then_inc(max_made, 1)
                for b in range(2):
                    dve.wait_ge(exp_made, 2 * g + b + 1)
                    dve.wait_ge(a_att, 8 * g + 4 * b + 4)
                    steps.link(dve.tensor_tensor(rden[:, b, :], rsum[:, b, :], esink[:, b, :], ALU.add))
                    steps.link(dve.reciprocal(rden[:, b, :], rden[:, b, :]))
                    for tile in range(4):
                        w = CHUNK if b == 0 and tile < 2 else P
                        ins = dve.tensor_scalar(prob[b][:, tile, 0:w], prob[b][:, tile, 0:w],
                                                rden[:, b, tile:tile + 1], None, ALU.mult)
                        if tile < 3:
                            steps.mark(ins)
                        else:
                            ins.then_inc(prob_made, 1)
                assert steps.n <= ATT_LINKS, steps.n
                while steps.n < ATT_LINKS:
                    steps.mark(dve.memset(credit[:, 13:14], 0.0))
                    steps.wait()
                dense_lo(r, 3)

            attention_v(0, A1, True)
            with dve.Fori(1, NKV) as g:
                attention_v(g, A1 + g, False)

            def merge_b(n):
                dve.wait_ge(gb_sig, n + 1)
                for t in range(TT):
                    await_chunk(dve, t, yb_full, n, ROUND * (3 * n + C_ROUND0 + 2) + 3)
                    dve.tensor_tensor(gyb[:, t, :], bank[6 + t][:], sgb[:, t, :], ALU.mult).then_inc(yb_free, 1)
                dve.wait_ge(yb_free, 2 * n + 4)
                for t in range(TT):
                    mg = merged[:, t, bass.ds(n * COLS, COLS)]
                    dve.tensor_tensor(mg, mg, gyb[:, t, :], ALU.add).then_inc(gyb_made, 1)

            def rounds_v(n, r, first):
                dense_lo(r, 0)
                if first:
                    evac_proj(A1 + A2 - 1)
                    heads_lo(NKV - 1)
                else:
                    merge_b(n - 1)
                dense_lo(r, 1)
                dense_lo(r, 2)
                if first:
                    inverse_mean(1, SGU_W)
                    dve.wait_ge(gv_in, 16)
                    for t in range(TT):
                        dve.wait_ge(rstd_made, TT + t + 1)
                        v = proj[:, t, VS_OFF:VS_OFF + SGU_W]
                        dve.scalar_tensor_tensor(out=v, in0=v, scalar=rstd[:, TT + t:TT + t + 1], in1=gv[:],
                                                 op0=ALU.mult, op1=ALU.mult).then_inc(vn_made, 1)
                dense_lo(r, 3)
                dense_lo(r + 1, 0)
                dve.wait_ge(bias_a_in, 16 * (A1 + A2) + 16 * n + 16)
                for t in range(TT):
                    await_chunk(dve, t, acc_full, n + (A1 + A2), ROUND * r + 3)
                    if first:
                        dve.wait_ge(mix_full, 4)
                    dve.scalar_tensor_tensor(out=sga[:, t, :], in0=bank[t][:], scalar=rstd[:, t:t + 1], in1=bias_a[:],
                                             op0=ALU.mult, op1=ALU.add).then_inc(acc_free, 1)
                if first:
                    gate_u(0)
                dense_lo(r + 1, 1)
                if first:
                    gate_u(1)
                dense_lo(r + 1, 2)
                if first:
                    for u in range(4):
                        dve.wait_ge(ybT_hi_made, u + 1)
                        t, k4 = divmod(u, 2)
                        hi = ybT_hi[:, 4 * k4:4 * k4 + 4, t * P:(t + 1) * P]
                        dve.tensor_tensor(ybT_lo[:, 4 * k4:4 * k4 + 4, t * P:(t + 1) * P],
                                          bank[4 + u][:].rearrange("p (k t) -> p k t", k=4), hi,
                                          ALU.subtract).then_inc(ybT_lo_made, 1)
                dense_lo(r + 1, 3)
                dense_lo(r + 2, 0)
                dve.wait_ge(bias_b_in, 16 * n + 16)
                for t in range(TT):
                    await_chunk(dve, t, gb_full, n, ROUND * r + (ROUND + 3))
                    dve.scalar_tensor_tensor(out=sgb[:, t, :], in0=bank[2 + t][:], scalar=rstd[:, t:t + 1],
                                             in1=bias_b[:], op0=ALU.mult, op1=ALU.add).then_inc(gb_free, 1)
                dense_lo(r + 2, 1)
                dense_lo(r + 2, 2)
                dve.wait_ge(ga_sig, n + 1)
                for t in range(TT):
                    await_chunk(dve, t, ya_full, n, ROUND * r + (2 * ROUND + 1))
                    dve.tensor_tensor(merged[:, t, bass.ds(n * COLS, COLS)], bank[4 + t][:], sga[:, t, :],
                                      ALU.mult).then_inc(ya_free, 1)
                dense_lo(r + 2, 3)

            def gate_u(t):
                dve.wait_ge(gelu_u, t + 1)
                for g in range(SG):
                    u = proj[:, t, U_OFF + g * P:U_OFF + (g + 1) * P]
                    dve.wait_ge(mix_full, 2 * t + g // 4 + 1)
                    dve.scalar_tensor_tensor(out=u, in0=bank[4 + 2 * t + g // 4][:, (g % 4) * P:(g % 4 + 1) * P],
                                             scalar=bsT[:, g:g + 1], in1=u,
                                             op0=ALU.add, op1=ALU.mult).then_inc(yb_made, 1)

            rounds_v(0, C_ROUND0, True)
            with dve.Fori(1, NC) as n:
                rounds_v(n, 3 * n + C_ROUND0, False)

            dense_lo(D_ROUND0, 0)
            merge_b(NC - 1)
            dense_lo(D_ROUND0, 1)
            for u in range(2 * NC):
                dve.wait_ge(mT_hi_made, u + 1)
                n, t = divmod(u, TT)
                hi = actT_hi[:, 4 * n:4 * n + 4, t * P:(t + 1) * P]
                dve.tensor_tensor(actT_lo[:, 4 * n:4 * n + 4, t * P:(t + 1) * P],
                                  bank[u][:].rearrange("p (k t) -> p k t", k=4), hi, ALU.subtract).then_inc(mT_lo_made, 1)
            dense_lo(D_ROUND0, 2)
            dense_lo(D_ROUND0, 3)

            def evac_out(n):
                dve.wait_ge(resid_in, 16 * TT)
                for t in range(TT):
                    await_chunk(dve, t, acc_full, n + (A1 + A2 + NC), ROUND * n + (ROUND * D_ROUND0 + 3))
                    h = resid[:, t, bass.ds(n * COLS, COLS)]
                    dve.tensor_tensor(h, bank[t][:], h, ALU.add).then_inc(acc_free, 1)

            dve.wait_ge(wr_in, 32)
            dve.tensor_tensor(wr[:], wr[:], gT[:, KT:2 * KT].to_broadcast([P, KT, NR]), ALU.mult).then_inc(wr_made, 1)
            dve.wait_ge(gb_free, 2 * NC + 2)
            dve.wait_ge(acc_free, 2 * (A1 + A2 + NC) + 2)
            for t in range(TT):
                dve.memset(lgs[:, t, :], 0.0).then_inc(lgs_made, 1)
            order.link(dve.memset(gl8[:], LOWEST))

            def add_logits(n):
                dve.wait_ge(lg_full, n + 1)
                for t in range(TT):
                    dve.wait_ge(lgs_made, 2 * n + t + 1)
                    dve.tensor_tensor(lgs[:, t, :], bank[4][:, t * NR:(t + 1) * NR], lgs[:, t, :],
                                      ALU.add).then_inc(lgs_made, 1)

            dense_lo(D_ROUND0 + 1, 0)
            evac_out(0)
            for k in range(1, ROUND):
                dense_lo(D_ROUND0 + 1, k)
            with dve.Fori(2, NC) as n:
                dense_lo(n + D_ROUND0, 0)
                evac_out(n - 1)
                add_logits(n - 2)
                for k in range(1, ROUND):
                    dense_lo(n + D_ROUND0, k)
            evac_out(NC - 1)

            add_logits(NC - 2)
            dve.wait_ge(sq_h_made, TT * NC + 1)
            dve.tensor_reduce(ssq[:, 2 * TT:3 * TT], ssq_h[:], AX_X, ALU.add).then_inc(ssq_made, TT)
            inverse_mean(2, D)
            add_logits(NC - 1)
            dve.wait_ge(br_in, 32)
            dve.wait_ge(lgs_made, TT * NC + TT)
            for t in range(TT):
                dve.wait_ge(rstd_made, 2 * TT + t + 1)
                order.mark(dve.scalar_tensor_tensor(out=lg[:, t, :], in0=lgs[:, t, :],
                                                    scalar=rstd[:, 2 * TT + t:2 * TT + t + 1], in1=br[:],
                                                    op0=ALU.mult, op1=ALU.add))
            order.wait()
            order.link(dve.tensor_copy(gl8[:, :, 0:NG], lg[:, :, 0:NG]))
            for t in range(TT):
                order.mark(dve.max(gm8[:, t, :], gl8[:, t, :]))
            order.wait()
            dve.tensor_scalar(ngm[:], gm8[:, :, 0], -1.0, None, ALU.mult).then_inc(gmax_made, 1)
            for t in range(TT):
                order.mark(dve.max_index(gi8[:, t, :], gm8[:, t, :], gl8[:, t, :]))
            order.wait()
            order.link(dve.tensor_copy(gif[:], gi8[:]))
            for t in range(TT):
                dve.tensor_scalar(goh[:, t, :], slot_no[:, 0:NG], gif[:, t, 0:1], None,
                                  ALU.is_equal).then_inc(goh_made, 1)
            dve.wait_ge(goh_made, TT)
            def pick(i):
                for t in range(TT):
                    dve.tensor_scalar(sel[:, t, :], slot_no[:], pos[:, t, bass.ds(i, 1)], None,
                                      ALU.is_equal).then_inc(sel_made, 1)

            for t in range(TT):
                order.mark(dve.tensor_tensor(own[:, t, :, :], lg[:, t, NG:NR].rearrange("p (g e) -> p g e", g=NG),
                                             goh[:, t, :].to_broadcast([P, NG, EPG]), ALU.mult))
            order.wait()
            for t in range(TT):
                order.mark(dve.tensor_reduce(inl[:, t, :], own[:, t, :, :].rearrange("p g e -> p e g"), AX_X, ALU.add))
            order.wait()
            for t in range(TT):
                order.mark(dve.max(em8[:, t, :], inl[:, t, :]))
            order.wait()
            dve.tensor_tensor(ed[:], em8[:, :, 1], em8[:, :, 0], ALU.subtract).then_inc(ed_made, 1)
            for t in range(TT):
                order.mark(dve.max_index(ei8[:, t, :], em8[:, t, :], inl[:, t, :]))
            order.wait()
            order.link(dve.tensor_copy(eif[:], ei8[:]))
            dve.wait_ge(rank_full, 3)
            for t in range(TT):
                order.mark(dve.tensor_tensor(rkp[:, t, :], bank[2 + t][:, 0:NG], goh[:, t, :], ALU.mult))
            order.wait()
            order.link(dve.tensor_reduce(rank[:], rkp[:], AX_X, ALU.add))
            order.mark(dve.tensor_scalar(fits[:], rank[:], float(P), None, ALU.is_lt))
            order.mark(dve.tensor_scalar(over[:], rank[:], float(P), None, ALU.is_ge))
            order.wait()
            order.mark(dve.scalar_tensor_tensor(out=rk1[:], in0=rank[:], scalar=1.0, in1=fits[:], op0=ALU.add, op1=ALU.mult))
            order.mark(dve.scalar_tensor_tensor(out=rk2[:], in0=rank[:], scalar=1.0 - P, in1=over[:], op0=ALU.add, op1=ALU.mult))
            order.wait()
            for t in range(TT):
                order.mark(dve.tensor_scalar(pos[:, t, 0:NG], goh[:, t, :], rk1[:, t:t + 1], -1.0, ALU.mult, ALU.add))
            order.mark(dve.tensor_scalar(pos[:, :, NG], rk2[:], -1.0, None, ALU.add))
            order.wait()
            pick(0)
            dve.wait_ge(gexp_made, TT)
            order.link(dve.reciprocal(gval[:], gsum[:]))
            dve.wait_ge(ee_made, 1)
            order.link(dve.tensor_scalar(es1[:], ee[:], 1.0, None, ALU.add))
            order.link(dve.reciprocal(es1[:], es1[:]))
            order.link(dve.tensor_tensor(ew0[:], es1[:], gval[:], ALU.mult))
            order.link(dve.tensor_tensor(ew1[:], ew0[:], ee[:], ALU.mult))
            for t in range(TT):
                order.mark(dve.tensor_scalar(ca[:, t, 0:EPG], slot_no[:, 0:EPG], eif[:, t, 0:1], ew0[:, t:t + 1],
                                             ALU.is_equal, ALU.mult))
                order.mark(dve.tensor_scalar(cb[:, t, :], slot_no[:, 0:EPG], eif[:, t, 1:2], ew1[:, t:t + 1],
                                             ALU.is_equal, ALU.mult))
            order.wait()
            order.link(dve.tensor_tensor(ca[:, :, 0:EPG], ca[:, :, 0:EPG], cb[:], ALU.add))
            for t in range(TT):
                n = 2 * TT + t
                order.mark(dve.tensor_scalar(ca[:, t, 0:EPG], ca[:, t, 0:EPG], rstd[:, n:n + 1], None, ALU.mult))
                order.mark(dve.tensor_copy(ca[:, t, EPG:EPG + 2], rstd[:, n:n + 1].to_broadcast([P, 2])))
            order.wait()
            order.link(dve.tensor_copy(cw_hi[:], ca[:]))
            dve.tensor_tensor(cw_lo[:], ca[:], cw_hi[:], ALU.subtract).then_inc(cwparts_made, 1)
            order.link(dve.tensor_scalar(ovg[:], bank[4][:, 0:NG], float(P), None, ALU.is_gt))
            order.link(dve.tensor_tensor(ovn[:], ovg[:], slot_no[:, 0:NG], ALU.mult))
            order.mark(dve.tensor_reduce(ctlf[:, 0:1], ovg[:], AX_X, ALU.add))
            order.mark(dve.tensor_reduce(ctlf[:, 1:2], ovn[:], AX_X, ALU.add))
            order.wait()
            dve.tensor_copy(ctl[:], ctlf[:]).then_inc(ctl_made, 1)

            def expert_lo(i, j, q):
                m = 6 * j - 2 + q
                s, sp_ = (4 + q) % EXP_RAW, (4 + q) % EXP_PARTS
                dve.wait_ge(hi_made, DENSE + PER_G * i + m + 1)
                dve.tensor_tensor(wlo[:, sp_, :], xraw[:, s, :], whi[:, sp_, :], ALU.subtract).then_inc(lo_made, 1)

            def hidden_lo(i, j):
                dve.wait_ge(hT_hi_made, EPG * i + j + 1)
                dve.tensor_tensor(hT_lo[:], bank[1][:, 0:T].rearrange("p (a b) -> p a b", a=2), hT_hi[:],
                                  ALU.subtract).then_inc(hT_lo_made, 1)

            def hidden(i, j):
                dve.wait_ge(silu_made, EPG * i + j + 1)
                dve.scalar_tensor_tensor(out=hid[:], in0=bank[0][:, FF:2 * FF], scalar=cw[:, bass.ds(j, 1)],
                                         in1=s_act[:], op0=ALU.mult, op1=ALU.mult).then_inc(hid_made, 1)

            def gathered_lo(i, chunks):
                for k4 in chunks:
                    b = GATHER_BANKS[k4]
                    dve.wait_ge(xg_hi_made, 4 * i + k4 + 1)
                    dve.tensor_tensor(xg_lo[:, 4 * k4:4 * k4 + 4, :], bank[b][:].rearrange("p (k t) -> p k t", k=4),
                                      xg_hi[:, 4 * k4:4 * k4 + 4, :], ALU.subtract).then_inc(xg_lo_made, 1)

            def weights(i):
                dve.wait_ge(cw_full, i + 1)
                if not (isinstance(i, int) and i == 0):
                    dve.wait_ge(hid_made, EPG * i)
                dve.tensor_copy(cw[:], bank[7][:, 0:EPG + 2]).then_inc(cw_made, 1)

            def output_lo(i, chunks):
                for b in chunks:
                    dve.wait_ge(o_hi_made, 4 * i + b + 1)
                    cols = slice(b * COLS, (b + 1) * COLS)
                    dve.tensor_tensor(o_lo[:, cols], bank[2 + b][:], o_hi[:, cols], ALU.subtract).then_inc(o_lo_made, 1)

            def add(i, units, order):
                for u in units:
                    dst, b, t = order[u]
                    dve.wait_ge(scat_full, 8 * i + u + 1)
                    h = resid[:, t, b * COLS:(b + 1) * COLS]
                    dve.tensor_tensor(h, bank[dst][:], h, ALU.add).then_inc(added, 1)

            def group_v(i, after_another, another_follows):
                if not after_another:
                    if isinstance(i, int) and i == NG:
                        pick(i)
                    expert_lo(i, 0, 2)
                    gathered_lo(i, range(4))
                    weights(i)
                expert_lo(i, 0, 3)
                expert_lo(i, 0, 4)
                if after_another:
                    output_lo(i - 1, range(0, 2))
                expert_lo(i, 0, 5)
                if after_another:
                    output_lo(i - 1, range(2, 4))
                expert_lo(i, 1, 0)
                expert_lo(i, 1, 1)
                dve.wait_ge(cw_made, i + 1)
                hidden(i, 0)
                if after_another:
                    add(i - 1, range(0, 4), SCATTER)
                expert_lo(i, 1, 2)
                hidden_lo(i, 0)
                if after_another:
                    add(i - 1, range(4, 6), SCATTER)
                for q in range(3, 6):
                    expert_lo(i, 1, q)
                if after_another:
                    add(i - 1, range(6, 8), SCATTER)
                hidden(i, 1)
                expert_lo(i, 2, 0)
                expert_lo(i, 2, 1)
                hidden_lo(i, 1)
                if another_follows:
                    dve.wait_ge(selT_full, i + 1)
                    pick(i + 1)
                for q in range(2, 6):
                    expert_lo(i, 2, q)
                hidden(i, 2)
                with dve.Fori(3, EPG) as j:
                    expert_lo(i, j, 0)
                    expert_lo(i, j, 1)
                    hidden_lo(i, j - 1)
                    for q in range(2, 6):
                        expert_lo(i, j, q)
                    hidden(i, j)
                expert_lo(i, EPG, 0)
                expert_lo(i, EPG, 1)
                if another_follows:
                    expert_lo(i + 1, 0, 2)
                    gathered_lo(i + 1, range(0, 2))
                hidden_lo(i, EPG - 1)
                if another_follows:
                    gathered_lo(i + 1, range(2, 4))
                    weights(i + 1)
                else:
                    output_lo(i, range(4))
                    add(i, range(8), SCATTER_LAST)

            dve.wait_ge(v_order, order.n)
            group_v(0, False, True)
            with dve.Fori(1, NG - 1) as i:
                group_v(i, True, True)
            group_v(NG - 1, True, False)
            dve.wait_ge(ctl_made, 1)
            more = dve.value_load(ctl[0:1, 0:1], min_val=0, max_val=1)
            with dve.If(more == 1):
                group_v(NG, False, False)
            dve.wait_ge(added, 8 * NG)
            dve.memset(credit[:, 14:15], 0.0).then_inc(small_made, 1)
            inverse_mean(3, D)
            dve.wait_ge(gf_in, 16)
            for t in range(TT):
                dve.wait_ge(rstd_made, 3 * TT + t + 1)
                dve.scalar_tensor_tensor(out=y_out[:, t, :], in0=resid[:, t, :], scalar=rstd[:, 3 * TT + t:3 * TT + t + 1], in1=gbig[:],
                                         op0=ALU.mult, op1=ALU.mult).then_inc(y_made, 1)

        @block.tensor
        def _(pe):
            def three(o, x_hi, x_lo, w_hi, w_lo, start, stop):
                pe.matmul(o, x_hi, w_hi, start=start, stop=False)
                pe.matmul(o, x_lo, w_hi, start=False, stop=False)
                return pe.matmul(o, x_hi, w_lo, start=False, stop=stop)

            pe.wait_ge(consts, 1)
            pe.wait_ge(g_in, 32)
            pe.transpose(bank[7][:, 0:2 * KT], g_rows[:], ident[0:2 * KT, 0:2 * KT]).then_inc(gT_full, 1)

            def turn_x(t):
                for k4 in range(4):
                    if k4 % 2 == 0:
                        pe.wait_ge(x_in[2 * t + k4 // 2], 16)
                    if t == 1 and k4 == 3:
                        pe.wait_ge(gT_made, 1)
                    for k in range(4):
                        d0 = (4 * k4 + k) * P
                        mm = pe.transpose(bank[4 * t + k4][:, k * P:(k + 1) * P], x0[:, t, d0:d0 + P], ident[:])
                        if t == 0 and k4 == 0 and k < DENSE_PARTS:
                            mm.then_inc(piece_used, 1)
                    mm.then_inc(xT_full, 1)

            def proj_piece(c, k, mid=None):
                dense_piece(c, k, 0, actT_hi, actT_lo, 4 * k, k == 0, k == ROUND - 1, (acc_free, 2 * c), acc_full, mid)

            def dense_piece(r, k, banks, x_hi, x_lo, kt, first, last, free, full, mid=None):
                pe.wait_ge(lo_made, DENSE_RAW + ROUND * r + k + 1)
                s = k % DENSE_PARTS
                for t in range(TT):
                    if t and mid:
                        mid()
                    if first:
                        pe.wait_ge(free[0], free[1] + t + 1)
                    for q in range(4):
                        cols = slice(q * COLS, (q + 1) * COLS)
                        tok = slice(t * P, (t + 1) * P)
                        mm = three(bank[banks + t][:], x_hi[:, kt + q, tok], x_lo[:, kt + q, tok],
                                   whi[:, s, cols], wlo[:, s, cols], first and q == 0, last and q == 3)
                    if last and t == 0:
                        mm.then_inc(full, 1)
                mm.then_inc(piece_used, 1)

            def second_tile():
                turn_x(1)
                pe.wait_ge(xT_lo_made, 8)

            def turn_spatial():
                pe.wait_ge(wsp_in, 16)
                for b in range(2):
                    for g in range(4):
                        mm = pe.transpose(bank[4 + b][:, g * P:(g + 1) * P], wsp[:, 4 * b + g, :], ident[:])
                    mm.then_inc(wspT_full, 1)
                pe.wait_ge(bs_in, 16)
                pe.transpose(bank[6][:, 0:SG], bs8[:], ident[0:SG, 0:SG]).then_inc(wspT_full, 1)

            turn_x(0)
            pe.wait_ge(xT_lo_made, 4)
            proj_piece(0, 0, second_tile)
            for k in range(1, ROUND):
                proj_piece(0, k)
            turn_spatial()
            with pe.Fori(1, A1) as c:
                for k in range(ROUND):
                    proj_piece(c, k)
            pe.wait_ge(wspT_made, 5)

            def attention_t(g, r):
                proj_piece(r, 0)
                pe.wait_ge(qkv_made, 3 * g + 3)
                for t in range(TT):
                    for h, w in enumerate((P, HEAD, HEAD, HEAD)):
                        mm = pe.transpose(bank[2 + t][0:w, h * P:(h + 1) * P],
                                          qkv[:, t, h * HEAD:h * HEAD + w], ident[:])
                    mm.then_inc(qkT_full, 1)
                for t in range(TT):
                    mm = pe.transpose(bank[4][0:HEAD, t * P:(t + 1) * P], qkv[:, t, 4 * HEAD:5 * HEAD], ident[:])
                mm.then_inc(qkT_full, 1)
                proj_piece(r, 1)
                pe.wait_ge(qkT_made, 3 * g + 3)
                for b in range(2):
                    for c2 in range(2):
                        c = 2 * b + c2
                        for rr in range(2):
                            o = (c2 * 2 + rr) * P
                            q = qT[:, c, 2 * rr:2 * rr + 2, :].rearrange("p h q -> p (h q)")
                            spans = {0: [(0, 0, CHUNK)], 1: [(0, 0, P)], 3: [(0, P, 2 * P)],
                                     2: [(0, P, P + CHUNK), (CHUNK, CHUNK, P)]}[c]
                            for off, k0, k1 in spans:
                                mm = pe.matmul(bank[5 + b][:, o + off:o + off + k1 - k0], q, kT[:, k0:k1],
                                               start=True, stop=True)
                    mm.then_inc(sc_full, 1)
                proj_piece(r, 2)
                for b in range(2):
                    pe.wait_ge(prob_made, 2 * g + b + 1)
                    dst = bank[7 if b == 0 else 2]
                    for tile in (2, 3, 0, 1):
                        w = CHUNK if b == 0 and tile < 2 else P
                        mm = pe.transpose(dst[0:w, tile * P:(tile + 1) * P], prob[b][:, tile, 0:w], ident[:])
                    mm.then_inc(pT_full, 1)
                proj_piece(r, 3)
                pe.wait_ge(vmid_made, 2 * g + 2)
                for b in range(2):
                    pe.wait_ge(pT_made, 3 * g + 2 + b)
                    for tile in (2, 3, 0, 1):
                        c = 2 * b + tile // 2
                        w = CHUNK if c == 0 else P
                        v = {0: qkv[0:CHUNK, 0, 5 * HEAD:6 * HEAD], 1: qkv[:, 0, 5 * HEAD:6 * HEAD],
                             2: vmid[:], 3: qkv[:, 1, 5 * HEAD:6 * HEAD]}[c]
                        mm = pe.matmul(bank[3 + b][0:HEAD, tile * P:(tile + 1) * P], v, probT[b][0:w, tile, :],
                                       start=True, stop=True)
                    mm.then_inc(ya_t_full, 1)

            with pe.Fori(0, NKV) as g:
                attention_t(g, A1 + g)

            def rounds_t(n, r, first):
                for k in range(ROUND):
                    dense_piece(r, k, 0, actT_hi, actT_lo, 4 * k, k == 0, k == 3,
                                     (acc_free, 2 * (A1 + A2) + 2 * n), acc_full)
                    if first and k == 2:
                        pe.wait_ge(yaT_hi_made, NKV)
                        for t in range(TT):
                            pe.wait_ge(vn_made, t + 1)
                            for gg in range(2):
                                for g in range(4):
                                    ch = 4 * gg + g
                                    mm = pe.matmul(bank[4 + 2 * t + gg][:, g * P:(g + 1) * P], wspT[:, ch, :],
                                                   proj[:, t, VS_OFF + ch * P:VS_OFF + (ch + 1) * P],
                                                   start=True, stop=True)
                                mm.then_inc(mix_full, 1)
                for k in range(ROUND):
                    dense_piece(r + 1, k, 2, actT_hi, actT_lo, 4 * k, k == 0, k == 3,
                                     (gb_free, 2 * n), gb_full)
                    if first and k == 1:
                        for t in range(TT):
                            pe.wait_ge(yb_made, SG * (t + 1) if t == 0 else TT * SG)
                            for k4 in range(2):
                                for q in range(4):
                                    c0 = U_OFF + (4 * k4 + q) * P
                                    mm = pe.transpose(bank[4 + 2 * t + k4][:, q * P:(q + 1) * P],
                                                      proj[:, t, c0:c0 + P], ident[:])
                                mm.then_inc(ybT_full, 1)
                if first:
                    pe.wait_ge(yaT_lo_made, NKV)
                    pe.wait_ge(ybT_lo_made, 4)
                for k in range(2):
                    dense_piece(r + 2, k, 4, yaT_hi, yaT_lo, 4 * k, k == 0, k == 1, (ya_free, 2 * n), ya_full)
                for k in range(2):
                    dense_piece(r + 2, 2 + k, 6, ybT_hi, ybT_lo, 4 * k, k == 0, k == 1, (yb_free, 2 * n), yb_full)

            rounds_t(0, C_ROUND0, True)
            with pe.Fori(1, NC) as n:
                rounds_t(n, 3 * n + C_ROUND0, False)

            pe.wait_ge(acc_free, 2 * (A1 + A2 + NC) + 2)
            pe.wait_ge(gb_free, 2 * NC + 2)
            pe.wait_ge(ya_free, 2 * NC + 2)
            for n in range(NC):
                pe.wait_ge(gyb_made, 2 * n + 2)
                for t in range(TT):
                    for q in range(4):
                        c0 = (4 * n + q) * P
                        mm = pe.transpose(bank[2 * n + t][:, q * P:(q + 1) * P], merged[:, t, c0:c0 + P], ident[:])
                    mm.then_inc(mT_full, 1)
            pe.wait_ge(mT_lo_made, 2 * NC)

            def out_piece(n, k):
                dense_piece(n + D_ROUND0, k, 0, actT_hi, actT_lo, 4 * k, k == 0, k == 3,
                            (acc_free, 2 * (A1 + A2 + NC) + 2 * n), acc_full)

            def turn_residual(t, src, c0):
                for q in range(4):
                    mm = pe.transpose(bank[2 + t][:, q * P:(q + 1) * P], src[:, t, c0 + q * P:c0 + (q + 1) * P], ident[:])
                mm.then_inc(hT_h_full, 1)

            def route(n):
                for t in range(TT):
                    pe.wait_ge(hT_h_made, 2 * n + 2 + t + 1)
                    for q in range(4):
                        mm = pe.matmul(bank[4][:, t * NR:(t + 1) * NR], hT[:, q, t * P:(t + 1) * P],
                                       wr[:, bass.ds(4 * n + q, 1), :].rearrange("p a n -> p (a n)"),
                                       start=(q == 0), stop=(q == 3))
                mm.then_inc(lg_full, 1)

            for k in range(ROUND):
                out_piece(0, k)
            pe.wait_ge(wr_made, 1)
            with pe.Fori(1, NC) as n:
                out_piece(n, 0)
                out_piece(n, 1)
                for t in range(TT):
                    pe.wait_ge(h_chunk_made, 2 * n - 1 + t)
                    turn_residual(t, h_chunk, 0)
                out_piece(n, 2)
                pe.wait_ge(lgs_made, 2 * n)
                route(n - 1)
                out_piece(n, 3)

            for t in range(TT):
                pe.wait_ge(acc_free, 2 * (A1 + A2 + NC) + 2 + 2 * (NC - 1) + t + 1)
                turn_residual(t, resid, (NC - 1) * COLS)
            pe.wait_ge(lgs_made, 2 * NC)
            route(NC - 1)
            pe.wait_ge(goh_made, TT)
            pe.matmul(bank[2][:, 0:NG], before[:], goh[:, 0, :], start=True, stop=True).then_inc(rank_full, 1)
            pe.matmul(bank[3][:, 0:NG], before[:], goh[:, 1, :], start=True, stop=False)
            pe.matmul(bank[3][:, 0:NG], ones[:], goh[:, 0, :], start=False, stop=True).then_inc(rank_full, 1)
            pe.matmul(bank[4][:, 0:NG], ones[:], goh[:, 0, :], start=True, stop=False)
            pe.matmul(bank[4][:, 0:NG], ones[:], goh[:, 1, :], start=False, stop=True).then_inc(rank_full, 1)
            pe.wait_ge(x2_lo_made, TT)
            pe.wait_ge(ident_r_made, 1)

            def gu_piece(i, j, q):
                m = 6 * j - 2 + q
                s = (4 + q) % EXP_PARTS
                pe.wait_ge(lo_made, DENSE_RAW + DENSE + PER_G * i + m + 1)
                w_hi = whi[:, s, :].rearrange("p (u k f) -> p u k f", u=2, k=4)
                w_lo = wlo[:, s, :].rearrange("p (u k f) -> p u k f", u=2, k=4)
                return w_hi, w_lo

            def gate_up(i, j, q0):
                if q0 == 0:
                    pe.wait_ge(hid_made, EPG * i + j)
                for k4 in range(4):
                    w_hi, w_lo = gu_piece(i, j, q0 + k4)
                    for k in range(4):
                        kt = 4 * k4 + k
                        mm = three(bank[0][:], xg_hi[:, kt, :], xg_lo[:, kt, :], w_hi[:, :, k, :], w_lo[:, :, k, :],
                                   kt == 0, kt == KT - 1)
                    mm.then_inc(piece_used, 1)

            def down(i, j, start, stop):
                pe.wait_ge(hT_lo_made, EPG * i + j)
                for f in range(2):
                    m = 6 * j + 2 + f
                    q = 4 + f if not stop else f
                    if stop:
                        m = 6 * j - 2 + f
                    s = (4 + q) % EXP_PARTS
                    pe.wait_ge(lo_made, DENSE_RAW + DENSE + PER_G * i + m + 1)
                    for b in range(4):
                        cols = slice(b * COLS, (b + 1) * COLS)
                        mm = three(bank[2 + b][:], hT_hi[:, f, :], hT_lo[:, f, :], whi[:, s, cols], wlo[:, s, cols],
                                   start and f == 0, stop and f == 1)
                        if stop and f == 1 and b < 3:
                            mm.then_inc(o_full, 1)
                    mm.then_inc(piece_used, 1)

            def turn_hidden(i, j):
                pe.wait_ge(hid_made, EPG * i + j + 1)
                for f in range(2):
                    mm = pe.transpose(bank[1][:, f * P:(f + 1) * P], hid[:, f * P:(f + 1) * P], ident[:])
                mm.then_inc(hT_full, 1)

            def gather(i, chunks):
                pe.wait_ge(sel_made, TT * i + 2)
                for k4 in chunks:
                    b = GATHER_BANKS[k4]
                    if k4 == 3:
                        pe.wait_ge(xg_lo_made, 4 * i + 1)
                    for q in range(4):
                        kt = 4 * k4 + q
                        n = 0
                        for part in (x2_hi, x2_lo):
                            for t in range(TT):
                                mm = pe.matmul(bank[b][:, q * P:(q + 1) * P], part[:, t, kt * P:(kt + 1) * P],
                                               sel[:, t, :], start=(n == 0), stop=(n == 3))
                                n += 1
                    mm.then_inc(xg_full, 1)

            def gather_weights(i):
                pe.wait_ge(xg_lo_made, 4 * i + 2)
                pe.wait_ge(cwparts_made, 1)
                n = 0
                for t in range(TT):
                    for part in (cw_hi, cw_lo):
                        mm = pe.matmul(bank[7][:, 0:EPG + 2], sel[:, t, :], part[:, t, :], start=(n == 0), stop=(n == 3))
                        n += 1
                mm.then_inc(cw_full, 1)

            def scatter(i, units, order):
                for u in units:
                    dst, b, t = order[u]
                    cols, tok = slice(b * COLS, (b + 1) * COLS), slice(t * P, (t + 1) * P)
                    pe.wait_ge(o_lo_made, 4 * i + max(b, dst - 2 if dst in OUT_BANKS else 0) + 1)
                    pe.matmul(bank[dst][:], selT[:, tok], o_hi[:, cols], start=True, stop=False)
                    pe.matmul(bank[dst][:], selT[:, tok], o_lo[:, cols], start=False, stop=True).then_inc(scat_full, 1)

            def group_t(i, after_another, another_follows):
                if not after_another:
                    gather(i, range(4))
                    gather_weights(i)
                pe.wait_ge(xg_lo_made, 4 * i + 4)
                gate_up(i, 0, 2)
                if after_another:
                    pe.wait_ge(selT_made, i)
                    pe.wait_ge(cw_made, i + 1)
                    scatter(i - 1, range(0, 6), SCATTER)
                turn_hidden(i, 0)
                gate_up(i, 1, 0)
                if after_another:
                    pe.wait_ge(added, 8 * (i - 1) + 6)
                    scatter(i - 1, range(6, 8), SCATTER)
                down(i, 1, True, False)
                turn_hidden(i, 1)
                if after_another:
                    pe.wait_ge(added, 8 * (i - 1) + 7)
                for t in range(TT):
                    mm = pe.matmul(bank[6][:, t * P:(t + 1) * P], sel[:, t, :], ident_r[:], start=True, stop=True)
                mm.then_inc(selT_full, 1)
                with pe.Fori(2, EPG - 1) as j:
                    gate_up(i, j, 0)
                    down(i, j, False, False)
                    turn_hidden(i, j)
                gate_up(i, EPG - 1, 0)
                down(i, EPG - 1, False, False)
                if another_follows:
                    pe.wait_ge(selT_made, i + 1)
                    if after_another:
                        pe.wait_ge(added, 8 * i)
                    gather(i + 1, range(0, 2))
                turn_hidden(i, EPG - 1)
                if another_follows:
                    gather(i + 1, range(2, 4))
                    gather_weights(i + 1)
                down(i, EPG, False, True)
                if not another_follows:
                    pe.wait_ge(selT_made, i + 1)
                    scatter(i, range(8), SCATTER_LAST)

            group_t(0, False, True)
            with pe.Fori(1, NG - 1) as i:
                group_t(i, True, True)
            group_t(NG - 1, True, False)
            pe.wait_ge(ctl_made, 1)
            more = pe.value_load(ctl[0:1, 0:1], min_val=0, max_val=1)
            with pe.If(more == 1):
                group_t(NG, False, False)


_INS = ["x", "norm_mix_g", "w_in", "b_in", "attn_sinks", "norm_v_g", "w_spatial", "b_spatial", "w_gate", "b_gate",
        "w_branch_a", "w_branch_b", "w_out", "norm_ffn_g", "w_router_group", "b_router_group", "w_router_expert",
        "b_router_expert", "w_e_gate", "w_e_up", "w_e_down", "norm_final_g"]


def kernel(**inputs):
    import numpy as _np
    import concourse.bacc as _bacc
    from concourse import mybir as _mybir
    from concourse.bass_utils import run_bass_kernel_spmd as _run

    nc = _bacc.Bacc("TRN2", target_bir_lowering=False, num_devices=1)
    arrays, views = {}, {}
    for name in _INS:
        v = _np.ascontiguousarray(inputs[name])
        arrays[f"in_{name}"] = v
        views[name] = nc.dram_tensor(f"in_{name}", v.shape, _mybir.dt.from_np(v.dtype), kind="ExternalInput").ap()
    x = arrays["in_x"]
    out = nc.dram_tensor("out_y", x.shape, _mybir.dt.from_np(x.dtype), kind="ExternalOutput").ap()
    build_trunk(nc, views, out)
    r = _run(nc, [arrays], core_ids=[0])
    return r.results[0]["out_y"]
```

```python
from contextlib import ExitStack

import concourse.bass as bass
from concourse import mybir

F32 = mybir.dt.float32
F32R = mybir.dt.float32r
I32 = mybir.dt.int32
U32 = mybir.dt.uint32
ALU = mybir.AluOpType
ACT = mybir.ActivationFunctionType
AX_X = mybir.AxisListType.X

P = 128
KB = 1024
CHUNK, HEAD, Q_PER_KV = 64, 64, 4
COLS = 512
PIECE = 2048
ROUND = 4
EPS = 1e-6
DENSE_RAW, DENSE_PARTS = 4, 2
EXP_RAW, EXP_PARTS = 6, 3
LOWEST = -3.0e38


class Chain:

    def __init__(self, eng, sem, base=0):
        self.eng, self.sem, self.base, self.n = eng, sem, base, 0

    def mark(self, ins):
        self.n += 1
        return ins.then_inc(self.sem, 1)

    def wait(self):
        self.eng.wait_ge(self.sem, self.base + self.n)

    def link(self, ins):
        self.mark(ins)
        self.wait()


def build_trunk(nc, a, out):
    T, D = a["x"].shape[1], a["x"].shape[2]
    TT, KT = T // P, D // P
    IN_W = a["w_in"].shape[2]
    SGU_W = a["norm_v_g"].shape[1]
    NH = a["attn_sinks"].shape[1]
    NKV = NH // Q_PER_KV
    ATT_W, KV_W = NH * HEAD, NKV * HEAD
    K_OFF, V_OFF = ATT_W, ATT_W + KV_W
    U_OFF, VS_OFF = ATT_W + 2 * KV_W, ATT_W + 2 * KV_W + SGU_W
    SG = a["w_spatial"].shape[1]
    KB2 = SGU_W // P
    NG = a["w_router_group"].shape[2]
    NE = a["w_router_expert"].shape[2]
    EPG = NE // NG
    FF = a["w_e_gate"].shape[3]
    NR = NG + NE
    A1, A2 = 3, IN_W // COLS - 3
    NC = D // COLS
    C_ROUND0 = A1 + A2
    D_ROUND0 = C_ROUND0 + 3 * NC
    DENSE = ROUND * (D_ROUND0 + NC)
    PER_G = 6 * EPG
    assert TT == 2 and KT == 16 and A2 == NKV == 4 and NC == 4 and KB2 == 8 and SG == 8 and FF == 256
    SCALE = float(HEAD) ** -0.5

    with ExitStack() as ctx:
        base = (nc.sbuf_base + 31) // 32 * 32
        room = (nc.sbuf_usable_end - base) // 32 * 32
        ctx.enter_context(nc.sbuf_tensor("arena", [P, room // 4], F32))

        def at(name, kb, shape, dt=F32):
            nbytes = 4
            for n in shape[1:]:
                nbytes *= n
            assert kb * KB + nbytes <= room, name
            return nc.alloc_sbuf_tensor_at(name, shape, dt, offset=base + int(kb * KB))

        def sem(name):
            return ctx.enter_context(nc.semaphore(name))

        bank = [ctx.enter_context(nc.psum_tensor(f"bank{i}", [P, COLS], F32)) for i in range(8)]

        resid = at("resid", 0, [P, TT, D])
        wsp = at("wsp", 0, [P, SG, P])
        yat = at("yat", 0, [P, 2, T])
        wspT = at("wspT", 4, [P, SG, P])
        gv = at("gv", 8, [P, SGU_W])
        probT = [at(f"probT{b}", 12 + 2 * b, [P, 4, P]) for b in range(2)]
        whi = [at(f"whi{s}", kb, [P, PIECE], F32R) for s, kb in enumerate((16, 24, 64))]
        wlo = [at(f"wlo{s}", kb, [P, PIECE], F32R) for s, kb in enumerate((40, 48, 72))]
        actT_hi = at("actT_hi", 64, [P, KT, T], F32R)
        actT_lo = at("actT_lo", 80, [P, KT, T], F32R)
        raw = at("raw", 96, [P, DENSE_RAW, PIECE])
        xg_hi = at("xg_hi", 96, [P, KT, P], F32R)
        xg_lo = at("xg_lo", 104, [P, KT, P], F32R)
        o_hi = at("o_hi", 112, [P, D], F32R)
        o_lo = at("o_lo", 120, [P, D], F32R)
        y_out = at("y_out", 96, [P, TT, D])
        xraw = at("xraw", 128, [P, EXP_RAW, PIECE])
        extra = [at(f"extra{n}", kb, [P, PIECE]) for n, kb in enumerate((112, 120, 80, 88))]
        x0 = at("x0", 128, [P, TT, D])
        xs0 = at("xs0", 144, [P, 4 * TT, KT // 4, P])
        g_rows = at("g_rows", 160, [2 * KT, P])
        sq0 = at("sq0", 168, [P, D])
        proj = at("proj", 128, [P, TT, IN_W])
        merged = at("merged", 128, [P, TT, D])
        sga = at("sga", 144, [P, TT, COLS])
        sgb = at("sgb", 148, [P, TT, COLS])
        gyb = at("gyb", 152, [P, TT, COLS])
        yaT_hi = at("yaT_hi", 156, [P, KB2, T], F32R)
        yaT_lo = at("yaT_lo", 164, [P, KB2, T], F32R)
        ybT_hi = at("ybT_hi", 172, [P, KB2, T], F32R)
        ybT_lo = at("ybT_lo", 180, [P, KB2, T], F32R)
        sq_v = at("sq_v", 172, [P, SGU_W])
        s_act = at("s_act", 176, [P, FF])
        hid = at("hid", 177, [P, FF])
        hT_hi = at("hT_hi", 178, [P, 2, P], F32R)
        hT_lo = at("hT_lo", 179, [P, 2, P], F32R)
        sel = at("sel", 180, [P, TT, P])
        selT = at("selT", 181, [P, T], F32R)
        sq2 = at("sq2", 128, [P, D])
        hg = [at("hg0", 32, [P, D]), at("hg1", 56, [P, D])]
        h_chunk = at("h_chunk", 176, [P, TT, COLS])
        hT = at("hT", 182, [P, COLS // P, T])
        sq_h = at("sq_h", 186, [P, COLS])
        bias_a = at("bias_a", 188, [P, COLS])
        bias_b = at("bias_b", 190, [P, COLS])
        ident = at("ident", 192, [P, P])
        before = at("before", 193, [P, P])
        ones = at("ones", 193.5, [P, P])
        slot_no = at("slot_no", 194, [P, P])
        slot_one = at("slot_one", 192.5, [P, P])
        qkv = at("qkv", 194.5, [P, TT, (Q_PER_KV + 2) * HEAD])
        qT = at("qT", 197.5, [HEAD, T // CHUNK, Q_PER_KV, CHUNK])
        kT = at("kT", 201.5, [HEAD, T])
        prob = [at(f"prob{b}", 202.5 + 2 * b, [P, 4, P]) for b in range(2)]
        gbig = at("gbig", 196.875, [P, D])
        wr = at("wr", 194.5, [P, KT, NR])
        small_at = [206.5]

        def small(name, shape, dt=F32):
            n = 4
            for s in shape[1:]:
                n *= s
            t = at(name, small_at[0], shape, dt)
            small_at[0] += (n + 31) // 32 * 32 / KB
            return t

        ssq = small("ssq", [P, 4 * TT])
        ms = small("ms", [P, 4 * TT])
        rstd = small("rstd", [P, 4 * TT])
        gT = small("gT", [P, 2 * KT])
        credit = small("credit", [P, 16])
        table_junk = small("table_junk", [P, 1])
        bsT = small("bsT", [P, SG])
        sink_row = small("sink_row", [P, NH])
        sinkv = small("sinkv", [P, NKV, 2, 2])
        mx = small("mx", [P, 2, 4])
        nmx = small("nmx", [P, 2, 4])
        sdiff = small("sdiff", [P, 2, 4])
        rsum = small("rsum", [P, 2, 4])
        esink = small("esink", [P, 2, 4])
        rden = small("rden", [P, 2, 4])
        vmid = small("vmid", [P, HEAD])
        bs8 = at("bs8", 202.5, [SG, P])
        br = at("br", 188, [P, NR])

        def rsmall(name, shape, dt=F32):
            t = small(name, shape, dt)
            assert small_at[0] <= 192, name
            return t

        small_at[0] = 188.25
        lg = rsmall("lg", [P, TT, NE])
        lgs = rsmall("lgs", [P, TT, NR])
        ssq_h = rsmall("ssq_h", [P, TT, NC])
        ssq_f = rsmall("ssq_f", [P, TT, NC])
        gl8 = rsmall("gl8", [P, TT, 8])
        gm8 = rsmall("gm8", [P, TT, 8])
        gi8 = rsmall("gi8", [P, TT, 8], U32)
        gif = rsmall("gif", [P, TT, 8])
        ngm = rsmall("ngm", [P, TT])
        gexp = rsmall("gexp", [P, TT, NG])
        gsum = rsmall("gsum", [P, TT])
        gval = rsmall("gval", [P, TT])
        goh = rsmall("goh", [P, TT, NG])
        own = rsmall("own", [P, TT, NG, EPG])
        inl = rsmall("inl", [P, TT, EPG])
        em8 = rsmall("em8", [P, TT, 8])
        ei8 = rsmall("ei8", [P, TT, 8], U32)
        eif = rsmall("eif", [P, TT, 8])
        ed = rsmall("ed", [P, TT])
        ee = rsmall("ee", [P, TT])
        es1 = rsmall("es1", [P, TT])
        ew0 = rsmall("ew0", [P, TT])
        ew1 = rsmall("ew1", [P, TT])
        ca = rsmall("ca", [P, TT, EPG + 2])
        cb = rsmall("cb", [P, TT, EPG])
        rest = rsmall("rest", [P, TT, NG])
        pos = rsmall("pos", [P, TT, NG + 1])
        ovg = rsmall("ovg", [P, NG])
        ovn = rsmall("ovn", [P, NG])
        ctlf = rsmall("ctlf", [P, 2])
        ctl = rsmall("ctl", [P, 2], I32)
        cw = rsmall("cw", [P, EPG + 2])

        x_in = [sem(f"x_in{n}") for n in range(2 * TT)]
        g_in, gv_in, wsp_in, bs_in, sink_in = (sem(n) for n in ("g_in", "gv_in", "wsp_in", "bs_in", "sink_in"))
        raw_in = [sem(f"raw_in{s}") for s in range(DENSE_RAW)]
        xraw_in = [sem(f"xraw_in{s}") for s in range(EXP_RAW)]
        extra_in = [sem(f"extra_in{n}") for n in range(4)]
        bias_a_in, bias_b_in = sem("bias_a_in"), sem("bias_b_in")
        resid_in, g2_in, wr_in, br_in, gf_in = (sem(n) for n in ("resid_in", "g2_in", "wr_in", "br_in", "gf_in"))
        out_done = sem("out_done")
        hi_made, lo_made, piece_used = sem("hi_made"), sem("lo_made"), sem("piece_used")
        consts, ident_made = sem("consts"), sem("ident_made")
        ssq_made, mean_made, ms_made, rstd_made = (sem(n) for n in ("ssq_made", "mean_made", "ms_made", "rstd_made"))
        gT_full, gT_made = sem("gT_full"), sem("gT_made")
        xs_made, xT_full, xT_hi_made, xT_lo_made = sem("xs_made"), sem("xT_full"), sem("xT_hi_made"), sem("xT_lo_made")
        wspT_full, wspT_made = sem("wspT_full"), sem("wspT_made")
        acc_full, acc_free = sem("acc_full"), sem("acc_free")
        gb_full, gb_free = sem("gb_full"), sem("gb_free")
        ya_full, ya_free = sem("ya_full"), sem("ya_free")
        yb_full, yb_free = sem("yb_full"), sem("yb_free")
        ga_sig, gb_sig, gyb_made = sem("ga_sig"), sem("gb_sig"), sem("gyb_made")
        qkv_made, qkT_full, qkT_made, vmid_made = sem("qkv_made"), sem("qkT_full"), sem("qkT_made"), sem("vmid_made")
        sc_full, max_made, exp_made, prob_made = sem("sc_full"), sem("max_made"), sem("exp_made"), sem("prob_made")
        pT_full, pT_made, ya_t_full, yat_made = sem("pT_full"), sem("pT_made"), sem("ya_t_full"), sem("yat_made")
        yaT_hi_made, yaT_lo_made = sem("yaT_hi_made"), sem("yaT_lo_made")
        gelu_v, gelu_u, vn_made, mix_full, yb_made = (sem(n) for n in ("gelu_v", "gelu_u", "vn_made", "mix_full", "yb_made"))
        ybT_full, ybT_hi_made, ybT_lo_made = sem("ybT_full"), sem("ybT_hi_made"), sem("ybT_lo_made")
        mT_full, mT_hi_made, mT_lo_made = sem("mT_full"), sem("mT_hi_made"), sem("mT_lo_made")
        wr_made, hg_made, hT_h_full, hT_h_made = sem("wr_made"), sem("hg_made"), sem("hT_h_full"), sem("hT_h_made")
        sq_h_made, lgs_made = sem("sq_h_made"), sem("lgs_made")
        h_chunk_made = sem("h_chunk_made")
        lg_full = sem("lg_full")
        gmax_made, gexp_made, goh_made, rank_full = sem("gmax_made"), sem("gexp_made"), sem("goh_made"), sem("rank_full")
        ed_made, ee_made, ca_made, ctl_made = sem("ed_made"), sem("ee_made"), sem("ca_made"), sem("ctl_made")
        sel_made, selT_full, selT_made, cw_made = sem("sel_made"), sem("selT_full"), sem("selT_made"), sem("cw_made")
        cw_full = sem("cw_full")
        xg_full, xg_hi_made, xg_lo_made = sem("xg_full"), sem("xg_hi_made"), sem("xg_lo_made")
        silu_made, hid_made = sem("silu_made"), sem("hid_made")
        hT_full, hT_hi_made, hT_lo_made = sem("hT_full"), sem("hT_hi_made"), sem("hT_lo_made")
        o_full, o_hi_made, o_lo_made = sem("o_full"), sem("o_hi_made"), sem("o_lo_made")
        scat_full, added = sem("scat_full"), sem("added")
        sq_f_made, y_made = sem("sq_f_made"), sem("y_made")
        v_order, v_att, pool_order, table_order = (sem(n) for n in ("v_order", "v_att", "pool_order", "table_order"))
        a_att = sem("a_att")

        block = ctx.enter_context(nc.Block())

        def await_used(eng, n):
            eng.wait_ge(piece_used, n + (DENSE_PARTS + 1))

        def await_chunk(eng, t, full, n, last_piece):
            if t == 0:
                eng.wait_ge(full, n + 1)
            else:
                await_used(eng, last_piece)

        OUT_BANKS = (2, 3, 4, 5)
        GATHER_BANKS = (6, 7, 0, 6)
        SCATTER = [(2, 0, 0), (3, 0, 1), (4, 1, 0), (5, 1, 1), (6, 2, 0), (7, 2, 1), (6, 3, 0), (7, 3, 1)]
        SCATTER_LAST = [(6, 0, 0), (7, 1, 0), (0, 2, 0), (1, 3, 0), (2, 0, 1), (3, 1, 1), (4, 2, 1), (5, 3, 1)]

        def place(i, j, q):
            if isinstance(i, int) and i == 0 and isinstance(j, int) and j <= 1:
                m = 6 * j - 2 + q
                if m < EXP_RAW:
                    return xraw[:, m, :], xraw_in[m], 0
                return extra[m - EXP_RAW][:], extra_in[m - EXP_RAW], 0
            return xraw[:, q, :], xraw_in[q], PER_G // EXP_RAW * i + j - 1

        x_v = a["x"].rearrange("b (t p) d -> p (b t) d", p=P)
        out_v = out.rearrange("b (t p) d -> p (b t) d", p=P)

        def chunked(w):
            return w[0].rearrange("(k p) (c n) -> p k c n", p=P, n=COLS)

        w_in_v, w_gate_v, w_out_v = chunked(a["w_in"]), chunked(a["w_gate"]), chunked(a["w_out"])
        w_a_v, w_b_v = chunked(a["w_branch_a"]), chunked(a["w_branch_b"])
        b_in_v = a["b_in"].rearrange("a (c n) -> a c n", n=COLS)
        b_gate_v = a["b_gate"].rearrange("a (c n) -> a c n", n=COLS)
        wg_v = a["w_e_gate"][0].rearrange("e (p k) f -> e p k f", p=P)
        wu_v = a["w_e_up"][0].rearrange("e (p k) f -> e p k f", p=P)
        wd_v = a["w_e_down"][0].rearrange("e (k p) d -> e p k d", p=P)

        def wide(row):
            return row.partition_broadcast(P).rearrange("p a n -> p (a n)")

        @block.sync
        def _(sp):
            def load_piece(r, k, view, kt, c):
                sp.wait_ge(lo_made, ROUND * r + k + 1)
                for h in range(2):
                    sp.dma_start(raw[:, k, h * KB:(h + 1) * KB].rearrange("p (k n) -> p k n", n=COLS),
                                 view[:, kt + 2 * h:kt + 2 * h + 2, c, :]).then_inc(raw_in[k], 16)

            def load_round(r, views):
                for k, (view, kt, c) in enumerate(views):
                    load_piece(r, k, view, kt, c)

            def full(view, c):
                return [(view, 4 * k, c) for k in range(4)]

            def load_bias(tile, row, arrived, freed, n):
                sp.wait_ge(freed, 2 * n + 2)
                sp.dma_start(tile[:], wide(row)).then_inc(arrived, 16)

            for n, gain in enumerate(("norm_mix_g", "norm_ffn_g")):
                sp.dma_start(g_rows[n * KT:(n + 1) * KT, :],
                             a[gain].rearrange("a (k p) -> (a k) p", p=P)).then_inc(g_in, 16)
            for t in range(TT):
                for h in range(2):
                    cols = slice(h * D // 2, (h + 1) * D // 2)
                    sp.dma_start(x0[:, t, cols], x_v[:, t, cols]).then_inc(x_in[2 * t + h], 16)
                if t == 0:
                    load_piece(0, 0, w_in_v, 0, 0)
            for k in range(1, ROUND):
                load_piece(0, k, w_in_v, 4 * k, 0)
            load_bias(bias_a, b_in_v[:, 0, :], bias_a_in, acc_free, 0)
            sp.dma_start(wsp[:], a["w_spatial"][0].rearrange("g i j -> i g j")).then_inc(wsp_in, 16)
            sp.dma_start(bs8[:], a["b_spatial"][0]).then_inc(bs_in, 16)
            sp.dma_start(sink_row[:], wide(a["attn_sinks"])).then_inc(sink_in, 16)
            with sp.Fori(1, A1 + A2) as c:
                load_round(c, full(w_in_v, c))
                load_bias(bias_a, b_in_v[:, c, :], bias_a_in, acc_free, c)
            sp.dma_start(gv[:], wide(a["norm_v_g"])).then_inc(gv_in, 16)

            def load_c(n):
                r = C_ROUND0 + 3 * n
                load_round(r, full(w_gate_v, n))
                load_bias(bias_a, b_gate_v[:, n, :], bias_a_in, acc_free, A1 + A2 + n)
                load_round(r + 1, full(w_gate_v, NC + n))
                load_bias(bias_b, b_gate_v[:, NC + n, :], bias_b_in, gb_free, n)
                load_round(r + 2, [(w_a_v, 0, n), (w_a_v, 4, n), (w_b_v, 0, n), (w_b_v, 4, n)])

            load_c(0)
            sp.wait_ge(ybT_lo_made, 4)
            for t in range(TT):
                sp.dma_start(resid[:, t, :], x_v[:, t, :]).then_inc(resid_in, 16)
            sp.wait_ge(yaT_lo_made, NKV)
            sp.dma_start(gbig[:], wide(a["norm_ffn_g"])).then_inc(g2_in, 16)
            sp.dma_start(wr[:, :, 0:NG], a["w_router_group"][0].rearrange("(k p) n -> p k n", p=P)).then_inc(wr_in, 16)
            sp.dma_start(wr[:, :, NG:NR], a["w_router_expert"][0].rearrange("(k p) n -> p k n", p=P)).then_inc(wr_in, 16)
            with sp.Fori(1, NC) as n:
                load_c(n)
            def load_expert(i, j, q, e):
                dst, arrived, _ = place(i, j, q)
                for h in range(2):
                    half = dst[:, h * KB:(h + 1) * KB]
                    if isinstance(j, int) and j == 0:
                        src = (wg_v, wu_v)[h][e, :, 4 * (q - 2):4 * (q - 2) + 4, :]
                    elif isinstance(j, int) and j == EPG:
                        src = wd_v[e + EPG - 1, :, q, h * KB:(h + 1) * KB]
                    elif q < 4:
                        src = (wg_v, wu_v)[h][e + j, :, 4 * q:4 * q + 4, :]
                    else:
                        src = wd_v[e + j - 1, :, q - 4, h * KB:(h + 1) * KB]
                    if len(src.shape) == 3:
                        half = half.rearrange("p (k f) -> p k f", f=FF)
                    sp.dma_start(half, src).then_inc(arrived, 16)

            def await_place(i, j, q):
                sp.wait_ge(lo_made, DENSE_RAW + DENSE + PER_G * i + 6 * j - 2 + q - EXP_RAW + 1)

            load_round(D_ROUND0, full(w_out_v, 0))
            for n in range(1, NC):
                load_round(D_ROUND0 + n, full(w_out_v, n))
                if n == 1:
                    sp.wait_ge(mT_lo_made, 2 * NC)
                    sp.wait_ge(acc_free, 2 * (A1 + A2 + NC) + 2)
                    sp.wait_ge(gb_free, 2 * NC + 2)
                    sp.dma_start(br[:, 0:NG], wide(a["b_router_group"])).then_inc(br_in, 16)
                    sp.dma_start(br[:, NG:NR], wide(a["b_router_expert"])).then_inc(br_in, 16)
                for m in range(2 * n - 2, 2 * n):
                    load_expert(0, (m + 2) // 6, (m + 2) % 6, 0)
            sp.wait_ge(lo_made, DENSE_RAW + DENSE)
            load_expert(0, 1, 2, 0)
            load_expert(0, 1, 3, 0)
            await_used(sp, DENSE - 1)
            load_expert(0, 1, 4, 0)
            load_expert(0, 1, 5, 0)
            sp.wait_ge(hg_made, TT * NC)
            sp.dma_start(gbig[:], wide(a["norm_final_g"].rearrange("(a n) -> a n", a=1))).then_inc(gf_in, 16)

            def load_group(i, e):
                for q in range(2, 6):
                    await_place(i, 0, q)
                    load_expert(i, 0, q, e)
                with sp.Fori(1, EPG) as j:
                    for q in range(6):
                        await_place(i, j, q)
                        load_expert(i, j, q, e)
                for q in range(2):
                    await_place(i, EPG, q)
                    load_expert(i, EPG, q, e)

            for q in range(6):
                sp.wait_ge(lo_made, DENSE_RAW + DENSE + q + 1)
                load_expert(0, 2, q, 0)
            with sp.Fori(3, EPG) as j:
                for q in range(6):
                    await_place(0, j, q)
                    load_expert(0, j, q, 0)
            for q in range(2):
                await_place(0, EPG, q)
                load_expert(0, EPG, q, 0)
            with sp.Fori(1, NG) as i:
                load_group(i, i * EPG)
            sp.wait_ge(ctl_made, 1)
            more = sp.value_load(ctl[0:1, 0:1], min_val=0, max_val=1)
            group = sp.value_load(ctl[0:1, 1:2], min_val=0, max_val=NG - 1)
            with sp.If(more == 1):
                load_group(NG, group * EPG)
            for u in range(2 * TT):
                t, h = divmod(u, 2)
                cols = slice(h * D // 2, (h + 1) * D // 2)
                sp.wait_ge(y_made, u + 1)
                sp.dma_start(out_v[:, t, cols], y_out[:, t, cols]).then_inc(out_done, 16)
            sp.wait_ge(out_done, 32 * TT)

        @block.gpsimd
        def _(pool):
            order = Chain(pool, pool_order)
            pool.memset(ident[:], 0.0).then_inc(pool_order, 1)
            pool.wait_ge(pool_order, 1)
            pool.affine_select(out=ident[:], in_=ident[:], compare_op=ALU.not_equal, fill=1.0,
                               base=0, pattern=[[-1, P]], channel_multiplier=1).then_inc(ident_made, 1)
            pool.memset(before[:], 1.0).then_inc(pool_order, 1)
            pool.memset(ones[:], 1.0).then_inc(pool_order, 1)
            pool.iota(slot_no[:], [[1, P]], base=0, channel_multiplier=0,
                      allow_small_or_imprecise_dtypes=True).then_inc(pool_order, 1)
            pool.iota(slot_one[:], [[1, P]], base=1, channel_multiplier=0,
                      allow_small_or_imprecise_dtypes=True).then_inc(pool_order, 1)
            pool.memset(wspT[:], 0.0).then_inc(pool_order, 1)
            order.n = 6
            order.wait()
            order.link(pool.affine_select(out=before[:], in_=before[:], compare_op=ALU.is_gt, fill=0.0,
                                          base=0, pattern=[[1, P]], channel_multiplier=-1))
            pool.memset(credit[:, 15:16], 0.0).then_inc(consts, 1)

            def permuted(tile, chunk):
                return tile.rearrange("t (k p) -> t k p", p=P)[:, :, bass.ds(chunk * (COLS // KT), COLS // KT)]

            pool.wait_ge(g2_in, 16)
            with pool.Fori(0, NC) as n:
                for t in range(TT):
                    pool.wait_ge(acc_free, 2 * (A1 + A2 + NC) + 2 + 2 * n + t + 1)
                    cols = bass.ds(n * COLS, COLS)
                    pool.tensor_tensor(permuted(hg[t][:], n),
                                       resid[:, t, cols].rearrange("t (p k) -> t k p", k=KT),
                                       gbig[:, cols].rearrange("t (p k) -> t k p", k=KT), ALU.mult).then_inc(hg_made, 1)

        @block.scalar
        def _(act):
            table_loads = [0]

            def make_hi(slot, arrived, use, src):
                act.wait_ge(arrived, 32 * use + 32)
                return act.activation(whi[slot][:], src, ACT.Copy)

            def dense_hi(r, k):
                act.wait_ge(piece_used, ROUND * r + k + 1)
                make_hi(k % DENSE_PARTS, raw_in[k], r, raw[:, k, :]).then_inc(hi_made, 1)

            def sum_squares(n, src, junk):
                act.activation(junk, src, ACT.Square, accum_out=ssq[:, n:n + 1]).then_inc(ssq_made, 1)

            def root(k, tiles=range(TT)):
                cols = slice(TT * k + tiles.start, TT * k + tiles.stop)
                act.wait_ge(ms_made, cols.stop)
                act.activation(rstd[:, cols], ms[:, cols], ACT.Sqrt).then_inc(rstd_made, len(tiles))

            for u in range(8):
                if u == 4:
                    dense_hi(0, 0)
                act.wait_ge(xs_made, u + 1)
                t, k4 = divmod(u, 4)
                act.activation(actT_hi[:, 4 * k4:4 * k4 + 4, t * P:(t + 1) * P], xs0[:, u, :, :],
                               ACT.Copy).then_inc(xT_hi_made, 1)
            dense_hi(0, 1)
            for t in range(TT):
                if t:
                    act.wait_ge(ssq_made, t)
                sum_squares(t, x0[:, t, :], sq0[:])
            dense_hi(0, 2)
            root(0)
            dense_hi(0, 3)

            with act.Fori(1, A1) as c:
                for k in range(ROUND):
                    dense_hi(c, k)

            def evac_heads(g):
                act.wait_ge(ya_t_full, 2 * g + 2)
                for b in range(2):
                    for h2 in range(2):
                        ins = act.activation(
                            yat[h2 * HEAD:(h2 + 1) * HEAD, :, b * P:(b + 1) * P].rearrange("p r (c q) -> p c r q", c=2),
                            bank[3 + b][0:HEAD, :].rearrange("p (c r h q) -> p c r h q", c=2, r=2, h=2)[:, :, :, h2, :],
                            ACT.Copy)
                        ins.then_inc(yat_made, 1)
                act.wait_ge(yat_made, 4 * g + 4)
                act.activation(yaT_hi[:, bass.ds(2 * g, 2), :], yat[:], ACT.Copy).then_inc(yaT_hi_made, 1)

            def attention_a(g, r, first):
                dense_hi(r, 0)
                dense_hi(r, 1)
                if not first:
                    evac_heads(g - 1)
                else:
                    act.wait_ge(acc_free, 2 + 2 * A1)
                act.activation(qkv[:, :, 0:4 * HEAD], proj[:, :, bass.ds(4 * HEAD * g, 4 * HEAD)],
                               ACT.Copy).then_inc(qkv_made, 1)
                act.activation(qkv[:, :, 4 * HEAD:5 * HEAD], proj[:, :, bass.ds(HEAD * g + K_OFF, HEAD)],
                               ACT.Copy).then_inc(qkv_made, 1)
                act.activation(qkv[:, :, 5 * HEAD:6 * HEAD], proj[:, :, bass.ds(HEAD * g + V_OFF, HEAD)],
                               ACT.Copy).then_inc(qkv_made, 1)
                act.wait_ge(qkT_full, 3 * g + 3)
                for t in range(TT):
                    act.activation(qT[:, 2 * t:2 * t + 2, :, :].rearrange("p c h q -> p h c q"),
                                   bank[2 + t][0:HEAD, :].rearrange("p (h c q) -> p h c q", h=4, c=2),
                                   ACT.Copy).then_inc(qkT_made, 1)
                act.activation(kT[:], bank[4][0:HEAD, 0:T], ACT.Copy).then_inc(qkT_made, 1)
                dense_hi(r, 2)
                dense_hi(r, 3)
                for b in range(2):
                    act.wait_ge(max_made, 2 * g + b + 1)
                    for tile in range(4):
                        w = CHUNK if b == 0 and tile < 2 else P
                        act.activation(prob[b][:, tile, 0:w], bank[5 + b][:, tile * P:tile * P + w], ACT.Exp,
                                       bias=nmx[:, b, tile:tile + 1], scale=SCALE,
                                       accum_out=rsum[:, b, tile:tile + 1]).then_inc(a_att, 1)
                    act.activation(esink[:, b, :], sdiff[:, b, :], ACT.Exp).then_inc(exp_made, 1)

            attention_a(0, A1, True)
            with act.Fori(1, NKV) as g:
                attention_a(g, A1 + g, False)

            def merged_hi(chunks):
                for u in range(2 * chunks.start, 2 * chunks.stop):
                    act.wait_ge(mT_full, u + 1)
                    n, t = divmod(u, TT)
                    act.activation(actT_hi[:, 4 * n:4 * n + 4, t * P:(t + 1) * P],
                                   bank[u][:].rearrange("p (k t) -> p k t", k=4), ACT.Copy).then_inc(mT_hi_made, 1)

            def rounds_c(n, r, first, last=False):
                dense_hi(r, 0)
                dense_hi(r, 1)
                if first:
                    evac_heads(NKV - 1)
                if first:
                    act.wait_ge(acc_free, 2 + 2 * (A1 + A2))
                    for t in range(TT):
                        act.activation(proj[:, t, VS_OFF:VS_OFF + SGU_W], proj[:, t, VS_OFF:VS_OFF + SGU_W],
                                       ACT.Gelu_apprx_tanh).then_inc(gelu_v, 1)
                    for t in range(TT):
                        act.wait_ge(gelu_v, t + 1)
                        act.wait_ge(ssq_made, TT + t)
                        sum_squares(TT + t, proj[:, t, VS_OFF:VS_OFF + SGU_W], sq_v[:])
                dense_hi(r, 2)
                if first:
                    root(1)
                    for t in range(TT):
                        act.activation(proj[:, t, U_OFF:U_OFF + SGU_W], proj[:, t, U_OFF:U_OFF + SGU_W],
                                       ACT.Gelu_apprx_tanh).then_inc(gelu_u, 1)
                dense_hi(r, 3)
                dense_hi(r + 1, 0)
                dense_hi(r + 1, 1)
                act.wait_ge(acc_free, 2 * (A1 + A2) + 2 * n + 4)
                act.activation(sga[:], sga[:], ACT.Sigmoid).then_inc(ga_sig, 1)
                dense_hi(r + 1, 2)
                if first:
                    for u in range(4):
                        act.wait_ge(ybT_full, u + 1)
                        t, k4 = divmod(u, 2)
                        act.activation(ybT_hi[:, 4 * k4:4 * k4 + 4, t * P:(t + 1) * P],
                                       bank[4 + u][:].rearrange("p (k t) -> p k t", k=4),
                                       ACT.Copy).then_inc(ybT_hi_made, 1)
                dense_hi(r + 1, 3)
                dense_hi(r + 2, 0)
                dense_hi(r + 2, 1)
                act.wait_ge(gb_free, 2 * n + 4)
                act.activation(sgb[:], sgb[:], ACT.Sigmoid).then_inc(gb_sig, 1)
                dense_hi(r + 2, 2)
                if last:
                    merged_hi(range(0, 2))
                dense_hi(r + 2, 3)

            rounds_c(0, C_ROUND0, True)
            with act.Fori(1, NC - 1) as n:
                rounds_c(n, 3 * n + C_ROUND0, False)
            rounds_c(NC - 1, D_ROUND0 - 3, False, last=True)

            dense_hi(D_ROUND0, 0)
            dense_hi(D_ROUND0, 1)
            merged_hi(range(2, 3))
            dense_hi(D_ROUND0, 2)
            merged_hi(range(3, 4))
            dense_hi(D_ROUND0, 3)

            def bring_table(func):
                act.activation(table_junk[:, 0:1], ones[:, 0:1], func).then_inc(table_order, 1)
                table_loads[0] += 1
                act.wait_ge(table_order, table_loads[0])

            def residual_squares(n):
                for t in range(TT):
                    act.wait_ge(acc_free, 2 * (A1 + A2 + NC) + 2 + 2 * n + t + 1)
                    act.wait_ge(sq_h_made, 2 * n + t + 1)
                    act.activation(sq_h[:], resid[:, t, bass.ds(n * COLS, COLS)], ACT.Square,
                                   accum_out=ssq_h[:, t, bass.ds(n, 1)]).then_inc(sq_h_made, 1)

            def residual_turned(n):
                for t in range(TT):
                    act.wait_ge(hT_h_full, 2 * n + t + 1)
                    act.activation(hT[:, :, t * P:(t + 1) * P], bank[2 + t][:].rearrange("p (k t) -> p k t", k=4),
                                   ACT.Copy).then_inc(hT_h_made, 1)

            with act.Fori(1, NC) as n:
                dense_hi(n + D_ROUND0, 0)
                dense_hi(n + D_ROUND0, 1)
                for t in range(TT):
                    act.wait_ge(acc_free, 2 * (A1 + A2 + NC) + 2 * n + t + 1)
                    act.wait_ge(hT_h_made, 2 * n)
                    act.activation(h_chunk[:, t, :], resid[:, t, bass.ds(n * COLS - COLS, COLS)],
                                   ACT.Copy).then_inc(h_chunk_made, 1)
                residual_squares(n - 1)
                dense_hi(n + D_ROUND0, 2)
                residual_turned(n - 1)
                dense_hi(n + D_ROUND0, 3)

            await_used(act, DENSE - 2)
            make_hi(0, xraw_in[0], 0, xraw[:, 0, :]).then_inc(hi_made, 1)
            bring_table(ACT.Sqrt)
            residual_turned(NC - 1)
            residual_squares(NC - 1)
            await_used(act, DENSE - 1)
            root(2)
            make_hi(1, xraw_in[1], 0, xraw[:, 1, :]).then_inc(hi_made, 1)
            act.wait_ge(gmax_made, 1)
            for t in range(TT):
                act.activation(gexp[:, t, :], gl8[:, t, 0:NG], ACT.Exp, bias=ngm[:, t:t + 1],
                               accum_out=gsum[:, t:t + 1]).then_inc(gexp_made, 1)
            make_hi(2, xraw_in[2], 0, xraw[:, 2, :]).then_inc(hi_made, 1)
            act.wait_ge(ed_made, 1)
            act.activation(ee[:], ed[:], ACT.Exp).then_inc(ee_made, 1)

            def expert_hi(i, j, q):
                m = 6 * j - 2 + q
                act.wait_ge(piece_used, DENSE + PER_G * i + m)
                src, arrived, use = place(i, j, q)
                make_hi((4 + q) % EXP_PARTS, arrived, use, src).then_inc(hi_made, 1)

            def hidden_hi(i, j):
                act.wait_ge(hT_full, EPG * i + j + 1)
                act.activation(hT_hi[:], bank[1][:, 0:T].rearrange("p (a b) -> p a b", a=2),
                               ACT.Copy).then_inc(hT_hi_made, 1)

            def silu(i, j):
                await_used(act, PER_G * i + (DENSE + 3) if isinstance(j, int) and j == 0 else
                           PER_G * i + 6 * j + (DENSE + 1))
                act.activation(s_act[:], bank[0][:, 0:FF], ACT.Silu, scale=cw[:, EPG:EPG + 1]).then_inc(silu_made, 1)

            def gathered_hi(i, chunks):
                for k4 in chunks:
                    b = GATHER_BANKS[k4]
                    act.wait_ge(xg_full, 4 * i + k4 + 1)
                    act.activation(xg_hi[:, 4 * k4:4 * k4 + 4, :], bank[b][:].rearrange("p (k t) -> p k t", k=4),
                                   ACT.Copy).then_inc(xg_hi_made, 1)

            def output_hi(i, chunks):
                for b in chunks:
                    if b < 3:
                        act.wait_ge(o_full, 3 * i + b + 1)
                    else:
                        await_used(act, PER_G * i + (DENSE + PER_G - 1))
                    act.activation(o_hi[:, b * COLS:(b + 1) * COLS], bank[2 + b][:], ACT.Copy).then_inc(o_hi_made, 1)

            def group_a(i, after_another, another_follows):
                if after_another:
                    expert_hi(i, 0, 3)
                elif i == 0:
                    gathered_hi(i, range(4))
                    bring_table(ACT.Silu)
                else:
                    expert_hi(i, 0, 2)
                    expert_hi(i, 0, 3)
                    gathered_hi(i, range(4))
                if after_another or i != 0:
                    expert_hi(i, 0, 4)
                if after_another:
                    output_hi(i - 1, range(0, 2))
                expert_hi(i, 0, 5)
                if after_another:
                    output_hi(i - 1, range(2, 4))
                expert_hi(i, 1, 0)
                if after_another:
                    expert_hi(i, 1, 1)
                act.wait_ge(cw_made, i + 1)
                silu(i, 0)
                if not after_another:
                    expert_hi(i, 1, 1)
                expert_hi(i, 1, 2)
                hidden_hi(i, 0)
                for q in range(3, 6):
                    expert_hi(i, 1, q)
                silu(i, 1)
                expert_hi(i, 2, 0)
                expert_hi(i, 2, 1)
                hidden_hi(i, 1)
                act.wait_ge(selT_full, i + 1)
                act.activation(selT[:], bank[6][:, 0:T], ACT.Copy).then_inc(selT_made, 1)
                for q in range(2, 6):
                    expert_hi(i, 2, q)
                silu(i, 2)
                with act.Fori(3, EPG) as j:
                    expert_hi(i, j, 0)
                    expert_hi(i, j, 1)
                    hidden_hi(i, j - 1)
                    for q in range(2, 6):
                        expert_hi(i, j, q)
                    silu(i, j)
                expert_hi(i, EPG, 0)
                expert_hi(i, EPG, 1)
                if another_follows:
                    gathered_hi(i + 1, range(0, 1))
                    expert_hi(i + 1, 0, 2)
                    gathered_hi(i + 1, range(1, 2))
                hidden_hi(i, EPG - 1)
                if another_follows:
                    gathered_hi(i + 1, range(2, 4))
                else:
                    output_hi(i, range(4))

            group_a(0, False, True)
            with act.Fori(1, NG - 1) as i:
                group_a(i, True, True)
            group_a(NG - 1, True, False)
            act.wait_ge(ctl_made, 1)
            more = act.value_load(ctl[0:1, 0:1], min_val=0, max_val=1)
            with act.If(more == 1):
                group_a(NG, False, False)
                act.wait_ge(added, 8 * NG + 8)
            bring_table(ACT.Sqrt)
            for t in range(TT):
                for b in range(NC):
                    act.wait_ge(added, 8 * (NG - 1) + 4 * t + b + 1)
                    if t:
                        act.wait_ge(sq_f_made, b + 1)
                    cols = slice(b * COLS, (b + 1) * COLS)
                    act.activation(sq2[:, cols], resid[:, t, cols], ACT.Square,
                                   accum_out=ssq_f[:, t, b:b + 1]).then_inc(sq_f_made, 1)
                root(3, range(t, t + 1))

        @block.vector
        def _(dve):
            order = Chain(dve, v_order)

            def dense_lo(r, k):
                dve.wait_ge(hi_made, ROUND * r + k + 1)
                s = k % DENSE_PARTS
                dve.tensor_tensor(wlo[s][:], raw[:, k, :], whi[s][:], ALU.subtract).then_inc(lo_made, 1)

            for n, (s, count) in enumerate(((lo_made, DENSE_RAW), (acc_free, 2), (gb_free, 2), (ya_free, 2),
                                            (yb_free, 2), (hT_h_made, 2), (sq_h_made, 1))):
                dve.memset(credit[:, n:n + 1], 0.0).then_inc(s, count)

            def inverse_mean(k, width, tiles=range(TT)):
                cols = slice(TT * k + tiles.start, TT * k + tiles.stop)
                dve.wait_ge(ssq_made, cols.stop)
                dve.tensor_scalar(ms[:, cols], ssq[:, cols], 1.0 / width, EPS,
                                  ALU.mult, ALU.add).then_inc(mean_made, len(tiles))
                dve.wait_ge(mean_made, cols.stop)
                dve.reciprocal(ms[:, cols], ms[:, cols]).then_inc(ms_made, len(tiles))

            dve.wait_ge(gT_full, 1)
            dve.tensor_copy(gT[:], bank[7][:, 0:2 * KT]).then_inc(gT_made, 1)
            dve.wait_ge(gT_made, 1)

            def gain(u):
                dve.wait_ge(xT_full, u + 1)
                k4 = u % 4
                dve.tensor_tensor(xs0[:, u, :, :], bank[u][:].rearrange("p (k t) -> p k t", k=4),
                                  gT[:, 4 * k4:4 * k4 + 4].to_broadcast([P, 4, P]), ALU.mult).then_inc(xs_made, 1)

            def xT_low(u):
                dve.wait_ge(xT_hi_made, u + 1)
                t, k4 = divmod(u, 4)
                part = (slice(None), slice(4 * k4, 4 * k4 + 4), slice(t * P, (t + 1) * P))
                dve.tensor_tensor(actT_lo[part], xs0[:, u, :, :], actT_hi[part], ALU.subtract).then_inc(xT_lo_made, 1)

            gain(0)
            for u in range(1, 4):
                gain(u)
                xT_low(u - 1)
            xT_low(3)
            dense_lo(0, 0)
            gain(4)
            for u in range(5, 8):
                gain(u)
                xT_low(u - 1)
            xT_low(7)
            dense_lo(0, 1)
            inverse_mean(0, D)
            dense_lo(0, 2)
            dense_lo(0, 3)
            def evac_proj(c):
                dve.wait_ge(bias_a_in, 16 * c + 16)
                dve.wait_ge(rstd_made, TT)
                for t in range(TT):
                    await_chunk(dve, t, acc_full, c, ROUND * c + 3)
                    dve.scalar_tensor_tensor(out=proj[:, t, bass.ds(c * COLS, COLS)], in0=bank[t][:],
                                             scalar=rstd[:, t:t + 1], in1=bias_a[:],
                                             op0=ALU.mult, op1=ALU.add).then_inc(acc_free, 1)

            dense_lo(1, 0)
            evac_proj(0)
            dense_lo(1, 1)
            dve.wait_ge(wspT_full, 3)
            dve.wait_ge(consts, 1)
            for b in range(2):
                src = bank[4 + b][:].rearrange("p (g i) -> p g i", g=4)
                dve.tensor_copy(wspT[0:CHUNK, 4 * b:4 * b + 4, :], src[0:CHUNK]).then_inc(wspT_made, 1)
                dve.tensor_copy(wspT[CHUNK:P, 4 * b:4 * b + 4, CHUNK:P], src[CHUNK:P, :, CHUNK:P]).then_inc(wspT_made, 1)
            dve.tensor_copy(bsT[:], bank[6][:, 0:SG]).then_inc(wspT_made, 1)
            dve.wait_ge(sink_in, 16)
            for h2 in range(2):
                rows = slice(h2 * CHUNK, (h2 + 1) * CHUNK)
                src = sink_row[rows, :].rearrange("p (g r h) -> p g r h", g=NKV, r=2)[:, :, :, h2]
                for c2 in range(2):
                    order.mark(dve.tensor_copy(sinkv[rows, :, c2, :], src))
            order.wait()

            dense_lo(1, 2)
            dense_lo(1, 3)
            with dve.Fori(2, A1) as c:
                dense_lo(c, 0)
                evac_proj(c - 1)
                for k in range(1, ROUND):
                    dense_lo(c, k)

            ATT_LINKS = 18

            def heads_lo(g):
                dve.wait_ge(yaT_hi_made, g + 1)
                dve.tensor_tensor(yaT_lo[:, bass.ds(2 * g, 2), :], yat[:], yaT_hi[:, bass.ds(2 * g, 2), :],
                                  ALU.subtract).then_inc(yaT_lo_made, 1)

            def attention_v(g, r, first):
                steps = Chain(dve, v_att, ATT_LINKS * g)
                dense_lo(r, 0)
                evac_proj(r - 1)
                dense_lo(r, 1)
                if not first:
                    heads_lo(g - 1)
                dve.wait_ge(qkv_made, 3 * g + 3)
                dve.tensor_copy(vmid[0:CHUNK, :], qkv[0:CHUNK, 1, 5 * HEAD:6 * HEAD]).then_inc(vmid_made, 1)
                dve.tensor_copy(vmid[CHUNK:P, :], qkv[CHUNK:P, 0, 5 * HEAD:6 * HEAD]).then_inc(vmid_made, 1)
                dense_lo(r, 2)
                for b in range(2):
                    dve.wait_ge(sc_full, 2 * g + b + 1)
                    sc = bank[5 + b][:].rearrange("p (a k) -> p a k", a=4)
                    if b == 0:
                        steps.mark(dve.tensor_reduce(mx[:, b, 0:2], sc[:, 0:2, 0:CHUNK], AX_X, ALU.max))
                        steps.mark(dve.tensor_reduce(mx[:, b, 2:4], sc[:, 2:4, :], AX_X, ALU.max))
                    else:
                        steps.mark(dve.tensor_reduce(mx[:, b, :], sc, AX_X, ALU.max))
                    steps.wait()
                    sinks = sinkv[:, bass.ds(g, 1), :, :].rearrange("p a c r -> p (a c r)")
                    steps.link(dve.scalar_tensor_tensor(out=mx[:, b, :], in0=mx[:, b, :], scalar=SCALE, in1=sinks,
                                                        op0=ALU.mult, op1=ALU.max))
                    steps.link(dve.tensor_tensor(sdiff[:, b, :], sinks, mx[:, b, :], ALU.subtract))
                    dve.tensor_scalar(nmx[:, b, :], mx[:, b, :], -1.0, None, ALU.mult).then_inc(max_made, 1)
                dense_lo(r, 3)
                for b in range(2):
                    dve.wait_ge(exp_made, 2 * g + b + 1)
                    dve.wait_ge(a_att, 8 * g + 4 * b + 4)
                    steps.link(dve.tensor_tensor(rden[:, b, :], rsum[:, b, :], esink[:, b, :], ALU.add))
                    steps.link(dve.reciprocal(rden[:, b, :], rden[:, b, :]))
                    for tile in range(4):
                        w = CHUNK if b == 0 and tile < 2 else P
                        ins = dve.tensor_scalar(prob[b][:, tile, 0:w], prob[b][:, tile, 0:w],
                                                rden[:, b, tile:tile + 1], None, ALU.mult)
                        if tile < 3:
                            steps.mark(ins)
                        else:
                            ins.then_inc(prob_made, 1)
                assert steps.n <= ATT_LINKS, steps.n
                while steps.n < ATT_LINKS:
                    steps.mark(dve.memset(credit[:, 13:14], 0.0))
                    steps.wait()
                for b in range(2):
                    dve.wait_ge(pT_full, 2 * g + b + 1)
                    src = bank[7 if b == 0 else 2][:].rearrange("p (a b) -> p a b", a=4)
                    if b == 0:
                        dve.tensor_copy(probT[0][0:CHUNK, 0:2, :], src[0:CHUNK, 0:2, :]).then_inc(pT_made, 1)
                        dve.tensor_copy(probT[0][:, 2:4, :], src[:, 2:4, :]).then_inc(pT_made, 1)
                    else:
                        dve.tensor_copy(probT[1][:], src).then_inc(pT_made, 1)

            attention_v(0, A1, True)
            with dve.Fori(1, NKV) as g:
                attention_v(g, A1 + g, False)

            def merge_b(n):
                dve.wait_ge(gb_sig, n + 1)
                for t in range(TT):
                    await_chunk(dve, t, yb_full, n, ROUND * (3 * n + C_ROUND0 + 2) + 3)
                    dve.tensor_tensor(gyb[:, t, :], bank[6 + t][:], sgb[:, t, :], ALU.mult).then_inc(yb_free, 1)
                dve.wait_ge(yb_free, 2 * n + 4)
                for t in range(TT):
                    mg = merged[:, t, bass.ds(n * COLS, COLS)]
                    dve.tensor_tensor(mg, mg, gyb[:, t, :], ALU.add).then_inc(gyb_made, 1)

            def merged_lo(chunks):
                for u in range(2 * chunks.start, 2 * chunks.stop):
                    dve.wait_ge(mT_hi_made, u + 1)
                    n, t = divmod(u, TT)
                    part = (slice(None), slice(4 * n, 4 * n + 4), slice(t * P, (t + 1) * P))
                    dve.tensor_tensor(actT_lo[part], bank[u][:].rearrange("p (k t) -> p k t", k=4), actT_hi[part],
                                      ALU.subtract).then_inc(mT_lo_made, 1)

            def rounds_v(n, r, first, last=False):
                dense_lo(r, 0)
                if first:
                    evac_proj(A1 + A2 - 1)
                else:
                    merge_b(n - 1)
                dense_lo(r, 1)
                if first:
                    heads_lo(NKV - 1)
                dense_lo(r, 2)
                if first:
                    inverse_mean(1, SGU_W)
                    dve.wait_ge(gv_in, 16)
                    for t in range(TT):
                        dve.wait_ge(rstd_made, TT + t + 1)
                        v = proj[:, t, VS_OFF:VS_OFF + SGU_W]
                        dve.scalar_tensor_tensor(out=v, in0=v, scalar=rstd[:, TT + t:TT + t + 1], in1=gv[:],
                                                 op0=ALU.mult, op1=ALU.mult).then_inc(vn_made, 1)
                dense_lo(r, 3)
                dense_lo(r + 1, 0)
                dve.wait_ge(bias_a_in, 16 * (A1 + A2) + 16 * n + 16)
                for t in range(TT):
                    await_chunk(dve, t, acc_full, n + (A1 + A2), ROUND * r + 3)
                    if first:
                        dve.wait_ge(mix_full, 4)
                    dve.scalar_tensor_tensor(out=sga[:, t, :], in0=bank[t][:], scalar=rstd[:, t:t + 1], in1=bias_a[:],
                                             op0=ALU.mult, op1=ALU.add).then_inc(acc_free, 1)
                if first:
                    gate_u(0)
                dense_lo(r + 1, 1)
                if first:
                    gate_u(1)
                dense_lo(r + 1, 2)
                if first:
                    for u in range(4):
                        dve.wait_ge(ybT_hi_made, u + 1)
                        t, k4 = divmod(u, 2)
                        hi = ybT_hi[:, 4 * k4:4 * k4 + 4, t * P:(t + 1) * P]
                        dve.tensor_tensor(ybT_lo[:, 4 * k4:4 * k4 + 4, t * P:(t + 1) * P],
                                          bank[4 + u][:].rearrange("p (k t) -> p k t", k=4), hi,
                                          ALU.subtract).then_inc(ybT_lo_made, 1)
                dense_lo(r + 1, 3)
                dense_lo(r + 2, 0)
                dve.wait_ge(bias_b_in, 16 * n + 16)
                for t in range(TT):
                    await_chunk(dve, t, gb_full, n, ROUND * r + (ROUND + 3))
                    dve.scalar_tensor_tensor(out=sgb[:, t, :], in0=bank[2 + t][:], scalar=rstd[:, t:t + 1],
                                             in1=bias_b[:], op0=ALU.mult, op1=ALU.add).then_inc(gb_free, 1)
                dense_lo(r + 2, 1)
                dense_lo(r + 2, 2)
                dve.wait_ge(ga_sig, n + 1)
                for t in range(TT):
                    await_chunk(dve, t, ya_full, n, ROUND * r + (2 * ROUND + 1))
                    dve.tensor_tensor(merged[:, t, bass.ds(n * COLS, COLS)], bank[4 + t][:], sga[:, t, :],
                                      ALU.mult).then_inc(ya_free, 1)
                dense_lo(r + 2, 3)
                if last:
                    merged_lo(range(0, 2))

            def gate_u(t):
                dve.wait_ge(gelu_u, t + 1)
                for g in range(SG):
                    u = proj[:, t, U_OFF + g * P:U_OFF + (g + 1) * P]
                    dve.wait_ge(mix_full, 2 * t + g // 4 + 1)
                    dve.scalar_tensor_tensor(out=u, in0=bank[4 + 2 * t + g // 4][:, (g % 4) * P:(g % 4 + 1) * P],
                                             scalar=bsT[:, g:g + 1], in1=u,
                                             op0=ALU.add, op1=ALU.mult).then_inc(yb_made, 1)

            rounds_v(0, C_ROUND0, True)
            with dve.Fori(1, NC - 1) as n:
                rounds_v(n, 3 * n + C_ROUND0, False)
            rounds_v(NC - 1, D_ROUND0 - 3, False, last=True)

            dense_lo(D_ROUND0, 0)
            merge_b(NC - 1)
            dense_lo(D_ROUND0, 1)
            merged_lo(range(2, 3))
            dense_lo(D_ROUND0, 2)
            merged_lo(range(3, 4))
            dense_lo(D_ROUND0, 3)

            def first_lo(m):
                dve.wait_ge(hi_made, DENSE + m + 1)
                dve.tensor_tensor(wlo[m][:], xraw[:, m, :], whi[m][:], ALU.subtract).then_inc(lo_made, 1)

            def evac_out(n):
                dve.wait_ge(resid_in, 16 * TT)
                for t in range(TT):
                    await_chunk(dve, t, acc_full, n + (A1 + A2 + NC), ROUND * n + (ROUND * D_ROUND0 + 3))
                    h = resid[:, t, bass.ds(n * COLS, COLS)]
                    dve.tensor_tensor(h, bank[t][:], h, ALU.add).then_inc(acc_free, 1)

            dve.wait_ge(wr_in, 32)
            dve.tensor_tensor(wr[:], wr[:], gT[:, KT:2 * KT].to_broadcast([P, KT, NR]), ALU.mult).then_inc(wr_made, 1)
            dve.wait_ge(gb_free, 2 * NC + 2)
            dve.wait_ge(acc_free, 2 * (A1 + A2 + NC) + 2)
            for t in range(TT):
                dve.memset(lgs[:, t, :], 0.0).then_inc(lgs_made, 1)
            order.link(dve.memset(gl8[:], LOWEST))

            def add_logits(n):
                dve.wait_ge(lg_full, n + 1)
                for t in range(TT):
                    dve.wait_ge(lgs_made, 2 * n + t + 1)
                    dve.tensor_tensor(lgs[:, t, :], bank[4][:, t * NR:(t + 1) * NR], lgs[:, t, :],
                                      ALU.add).then_inc(lgs_made, 1)

            dense_lo(D_ROUND0 + 1, 0)
            evac_out(0)
            for k in range(1, ROUND):
                dense_lo(D_ROUND0 + 1, k)
            with dve.Fori(2, NC) as n:
                dense_lo(n + D_ROUND0, 0)
                evac_out(n - 1)
                add_logits(n - 2)
                for k in range(1, ROUND):
                    dense_lo(n + D_ROUND0, k)
            first_lo(0)
            evac_out(NC - 1)

            add_logits(NC - 2)
            dve.wait_ge(sq_h_made, TT * NC + 1)
            dve.tensor_reduce(ssq[:, 2 * TT:3 * TT], ssq_h[:], AX_X, ALU.add).then_inc(ssq_made, TT)
            inverse_mean(2, D)
            add_logits(NC - 1)
            dve.wait_ge(br_in, 32)
            dve.wait_ge(lgs_made, TT * NC + TT)
            for t in range(TT):
                dve.wait_ge(rstd_made, 2 * TT + t + 1)
                order.mark(dve.scalar_tensor_tensor(out=gl8[:, t, 0:NG], in0=lgs[:, t, 0:NG],
                                                    scalar=rstd[:, 2 * TT + t:2 * TT + t + 1], in1=br[:, 0:NG],
                                                    op0=ALU.mult, op1=ALU.add))
            order.wait()
            for t in range(TT):
                order.mark(dve.max(gm8[:, t, :], gl8[:, t, :]))
            order.wait()
            for t in range(TT):
                order.mark(dve.max_index(gi8[:, t, :], gm8[:, t, :], gl8[:, t, :]))
            order.wait()
            order.link(dve.tensor_copy(gif[:], gi8[:]))
            for t in range(TT):
                dve.tensor_scalar(goh[:, t, :], slot_no[:, 0:NG], gif[:, t, 0:1], None,
                                  ALU.is_equal).then_inc(goh_made, 1)
            dve.tensor_scalar(ngm[:], gm8[:, :, 0], -1.0, None, ALU.mult).then_inc(gmax_made, 1)

            def pick(i):
                for t in range(TT):
                    dve.tensor_scalar(sel[:, t, :], slot_one[:], pos[:, t, bass.ds(i, 1)], None,
                                      ALU.is_equal).then_inc(sel_made, 1)

            for t in range(TT):
                order.mark(dve.scalar_tensor_tensor(out=lg[:, t, :], in0=lgs[:, t, NG:NR],
                                                    scalar=rstd[:, 2 * TT + t:2 * TT + t + 1], in1=br[:, NG:NR],
                                                    op0=ALU.mult, op1=ALU.add))
            order.wait()
            dve.wait_ge(goh_made, TT)
            for t in range(TT):
                order.mark(dve.tensor_tensor(own[:, t, :, :], lg[:, t, :].rearrange("p (g e) -> p g e", g=NG),
                                             goh[:, t, :].to_broadcast([P, NG, EPG]), ALU.mult))
            order.wait()
            dve.wait_ge(rank_full, 2)
            for t in range(TT):
                order.mark(dve.scalar_tensor_tensor(out=pos[:, t, 0:NG], in0=bank[2 + t][:, 0:NG], scalar=1.0,
                                                    in1=goh[:, t, :], op0=ALU.add, op1=ALU.mult))
            order.wait()
            pick(0)
            for t in range(TT):
                order.mark(dve.tensor_scalar(rest[:, t, :], pos[:, t, 0:NG], -float(P), 0.0, ALU.add, ALU.max))
            order.wait()
            for t in range(TT):
                order.mark(dve.tensor_reduce(pos[:, t, NG:NG + 1], rest[:, t, :], AX_X, ALU.add))
            for t in range(TT):
                order.mark(dve.tensor_reduce(inl[:, t, :], own[:, t, :, :].rearrange("p g e -> p e g"), AX_X, ALU.add))
            order.wait()
            for t in range(TT):
                order.mark(dve.max(em8[:, t, :], inl[:, t, :]))
            order.wait()
            dve.tensor_tensor(ed[:], em8[:, :, 1], em8[:, :, 0], ALU.subtract).then_inc(ed_made, 1)
            for t in range(TT):
                order.mark(dve.max_index(ei8[:, t, :], em8[:, t, :], inl[:, t, :]))
            order.wait()
            order.link(dve.tensor_copy(eif[:], ei8[:]))
            dve.wait_ge(gexp_made, TT)
            order.link(dve.reciprocal(gval[:], gsum[:]))
            dve.wait_ge(ee_made, 1)
            order.link(dve.tensor_scalar(es1[:], ee[:], 1.0, None, ALU.add))
            order.link(dve.reciprocal(es1[:], es1[:]))
            order.link(dve.tensor_tensor(ew0[:], es1[:], gval[:], ALU.mult))
            order.link(dve.tensor_tensor(ew1[:], ew0[:], ee[:], ALU.mult))
            for t in range(TT):
                order.mark(dve.tensor_scalar(ca[:, t, 0:EPG], slot_no[:, 0:EPG], eif[:, t, 0:1], ew0[:, t:t + 1],
                                             ALU.is_equal, ALU.mult))
                order.mark(dve.tensor_scalar(cb[:, t, :], slot_no[:, 0:EPG], eif[:, t, 1:2], ew1[:, t:t + 1],
                                             ALU.is_equal, ALU.mult))
            order.wait()
            order.link(dve.tensor_tensor(ca[:, :, 0:EPG], ca[:, :, 0:EPG], cb[:], ALU.add))
            for t in range(TT):
                n = 2 * TT + t
                dve.tensor_scalar(ca[:, t, 0:EPG], ca[:, t, 0:EPG], rstd[:, n:n + 1], None, ALU.mult).then_inc(ca_made, 1)
                dve.tensor_copy(ca[:, t, EPG:EPG + 2], rstd[:, n:n + 1].to_broadcast([P, 2])).then_inc(ca_made, 1)
            def expert_lo(i, j, q):
                m = 6 * j - 2 + q
                s = (4 + q) % EXP_PARTS
                dve.wait_ge(hi_made, DENSE + PER_G * i + m + 1)
                dve.tensor_tensor(wlo[s][:], place(i, j, q)[0], whi[s][:], ALU.subtract).then_inc(lo_made, 1)

            def hidden_lo(i, j):
                dve.wait_ge(hT_hi_made, EPG * i + j + 1)
                dve.tensor_tensor(hT_lo[:], bank[1][:, 0:T].rearrange("p (a b) -> p a b", a=2), hT_hi[:],
                                  ALU.subtract).then_inc(hT_lo_made, 1)

            def hidden(i, j):
                dve.wait_ge(silu_made, EPG * i + j + 1)
                dve.scalar_tensor_tensor(out=hid[:], in0=bank[0][:, FF:2 * FF], scalar=cw[:, bass.ds(j, 1)],
                                         in1=s_act[:], op0=ALU.mult, op1=ALU.mult).then_inc(hid_made, 1)

            def find_overflow():
                dve.wait_ge(rank_full, 3)
                order.link(dve.tensor_scalar(ovg[:], bank[4][:, 0:NG], float(P), None, ALU.is_gt))
                order.link(dve.tensor_tensor(ovn[:], ovg[:], slot_no[:, 0:NG], ALU.mult))
                order.mark(dve.tensor_reduce(ctlf[:, 0:1], ovg[:], AX_X, ALU.add))
                order.mark(dve.tensor_reduce(ctlf[:, 1:2], ovn[:], AX_X, ALU.add))
                order.wait()
                dve.tensor_copy(ctl[:], ctlf[:]).then_inc(ctl_made, 1)

            def gathered_lo(i, chunks):
                for k4 in chunks:
                    b = GATHER_BANKS[k4]
                    dve.wait_ge(xg_hi_made, 4 * i + k4 + 1)
                    dve.tensor_tensor(xg_lo[:, 4 * k4:4 * k4 + 4, :], bank[b][:].rearrange("p (k t) -> p k t", k=4),
                                      xg_hi[:, 4 * k4:4 * k4 + 4, :], ALU.subtract).then_inc(xg_lo_made, 1)

            def weights(i):
                dve.wait_ge(cw_full, i + 1)
                if not (isinstance(i, int) and i == 0):
                    dve.wait_ge(hid_made, EPG * i)
                dve.tensor_copy(cw[:], bank[7][:, 0:EPG + 2]).then_inc(cw_made, 1)

            def output_lo(i, chunks):
                for b in chunks:
                    dve.wait_ge(o_hi_made, 4 * i + b + 1)
                    cols = slice(b * COLS, (b + 1) * COLS)
                    dve.tensor_tensor(o_lo[:, cols], bank[2 + b][:], o_hi[:, cols], ALU.subtract).then_inc(o_lo_made, 1)

            def add(i, units, order):
                for u in units:
                    dst, b, t = order[u]
                    dve.wait_ge(scat_full, 8 * i + u + 1)
                    h = resid[:, t, b * COLS:(b + 1) * COLS]
                    dve.tensor_tensor(h, bank[dst][:], h, ALU.add).then_inc(added, 1)

            def group_v(i, after_another, another_follows):
                if after_another:
                    expert_lo(i, 0, 3)
                elif i == 0:
                    gathered_lo(i, range(0, 1))
                    first_lo(1)
                    gathered_lo(i, range(1, 4))
                    weights(i)
                else:
                    pick(i)
                    expert_lo(i, 0, 2)
                    expert_lo(i, 0, 3)
                    gathered_lo(i, range(4))
                    weights(i)
                expert_lo(i, 0, 4)
                if not after_another and i == 0:
                    find_overflow()
                if after_another:
                    output_lo(i - 1, range(0, 2))
                expert_lo(i, 0, 5)
                if after_another:
                    output_lo(i - 1, range(2, 4))
                expert_lo(i, 1, 0)
                if after_another:
                    expert_lo(i, 1, 1)
                dve.wait_ge(cw_made, i + 1)
                hidden(i, 0)
                if not after_another:
                    expert_lo(i, 1, 1)
                if after_another:
                    add(i - 1, range(0, 4), SCATTER)
                expert_lo(i, 1, 2)
                hidden_lo(i, 0)
                if after_another:
                    add(i - 1, range(4, 6), SCATTER)
                for q in range(3, 6):
                    expert_lo(i, 1, q)
                if after_another:
                    add(i - 1, range(6, 8), SCATTER)
                hidden(i, 1)
                expert_lo(i, 2, 0)
                expert_lo(i, 2, 1)
                hidden_lo(i, 1)
                if another_follows:
                    dve.wait_ge(selT_full, i + 1)
                    pick(i + 1)
                for q in range(2, 6):
                    expert_lo(i, 2, q)
                hidden(i, 2)
                with dve.Fori(3, EPG) as j:
                    expert_lo(i, j, 0)
                    expert_lo(i, j, 1)
                    hidden_lo(i, j - 1)
                    for q in range(2, 6):
                        expert_lo(i, j, q)
                    hidden(i, j)
                expert_lo(i, EPG, 0)
                if another_follows:
                    expert_lo(i, EPG, 1)
                    gathered_lo(i + 1, range(0, 1))
                    expert_lo(i + 1, 0, 2)
                    gathered_lo(i + 1, range(1, 2))
                hidden_lo(i, EPG - 1)
                if not another_follows:
                    expert_lo(i, EPG, 1)
                if another_follows:
                    gathered_lo(i + 1, range(2, 4))
                    weights(i + 1)
                else:
                    output_lo(i, range(4))
                    add(i, range(8), SCATTER_LAST)

            def output_rows(t):
                n = 3 * TT + t
                dve.wait_ge(rstd_made, n + 1)
                for h in range(2):
                    cols = slice(h * D // 2, (h + 1) * D // 2)
                    dve.scalar_tensor_tensor(out=y_out[:, t, cols], in0=resid[:, t, cols], scalar=rstd[:, n:n + 1],
                                             in1=gbig[:, cols], op0=ALU.mult, op1=ALU.mult).then_inc(y_made, 1)

            group_v(0, False, True)
            with dve.Fori(1, NG - 1) as i:
                group_v(i, True, True)
            group_v(NG - 1, True, False)
            dve.wait_ge(ctl_made, 1)
            more = dve.value_load(ctl[0:1, 0:1], min_val=0, max_val=1)
            with dve.If(more == 1):
                group_v(NG, False, False)
            dve.wait_ge(gf_in, 16)
            for t in range(TT):
                dve.wait_ge(sq_f_made, NC * (t + 1))
                n = 3 * TT + t
                dve.tensor_reduce(ssq[:, n:n + 1], ssq_f[:, t, :], AX_X, ALU.add).then_inc(ssq_made, 1)
                inverse_mean(3, D, range(t, t + 1))
                if t == 0:
                    output_rows(0)
            output_rows(1)

        @block.tensor
        def _(pe):
            def three(o, x_hi, x_lo, w_hi, w_lo, start, stop):
                pe.matmul(o, x_hi, w_hi, start=start, stop=False)
                pe.matmul(o, x_lo, w_hi, start=False, stop=False)
                return pe.matmul(o, x_hi, w_lo, start=False, stop=stop)

            def keep_clock(n, operand, dst):
                for _ in range(n):
                    pe.matmul(dst, operand[:, 0:P], operand, start=True, stop=True)

            pe.wait_ge(ident_made, 1)
            keep_clock(8, ident[:], bank[1][:, 0:P])
            pe.wait_ge(g_in, 32)
            pe.transpose(bank[7][:, 0:2 * KT], g_rows[:], ident[0:2 * KT, 0:2 * KT]).then_inc(gT_full, 1)

            def turn_x(t):
                for k4 in range(4):
                    if k4 % 2 == 0:
                        pe.wait_ge(x_in[2 * t + k4 // 2], 16)
                    if t == 1 and k4 == 3:
                        pe.wait_ge(gT_made, 1)
                    for k in range(4):
                        d0 = (4 * k4 + k) * P
                        mm = pe.transpose(bank[4 * t + k4][:, k * P:(k + 1) * P], x0[:, t, d0:d0 + P], ident[:])
                        if t == 0 and k4 == 0 and k < DENSE_PARTS:
                            mm.then_inc(piece_used, 1)
                    mm.then_inc(xT_full, 1)

            def proj_piece(c, k, mid=None):
                dense_piece(c, k, 0, actT_hi, actT_lo, 4 * k, k == 0, k == ROUND - 1, (acc_free, 2 * c), acc_full, mid)

            def dense_piece(r, k, banks, x_hi, x_lo, kt, first, last, free, full, mid=None):
                pe.wait_ge(lo_made, DENSE_RAW + ROUND * r + k + 1)
                s = k % DENSE_PARTS
                for t in range(TT):
                    if t and mid:
                        mid()
                    if first:
                        pe.wait_ge(free[0], free[1] + t + 1)
                    for q in range(4):
                        cols = slice(q * COLS, (q + 1) * COLS)
                        tok = slice(t * P, (t + 1) * P)
                        mm = three(bank[banks + t][:], x_hi[:, kt + q, tok], x_lo[:, kt + q, tok],
                                   whi[s][:, cols], wlo[s][:, cols], first and q == 0, last and q == 3)
                    if last and t == 0:
                        mm.then_inc(full, 1)
                mm.then_inc(piece_used, 1)

            def second_tile():
                pe.wait_ge(xT_lo_made, 8)
            def turn_spatial():
                pe.wait_ge(wsp_in, 16)
                for b in range(2):
                    for g in range(4):
                        mm = pe.transpose(bank[4 + b][:, g * P:(g + 1) * P], wsp[:, 4 * b + g, :], ident[:])
                    mm.then_inc(wspT_full, 1)
                pe.wait_ge(bs_in, 16)
                pe.transpose(bank[6][:, 0:SG], bs8[:], ident[0:SG, 0:SG]).then_inc(wspT_full, 1)

            turn_x(0)
            turn_x(1)
            pe.wait_ge(xT_lo_made, 4)
            proj_piece(0, 0, second_tile)
            for k in range(1, ROUND):
                proj_piece(0, k)
            turn_spatial()
            with pe.Fori(1, A1) as c:
                for k in range(ROUND):
                    proj_piece(c, k)
            pe.wait_ge(wspT_made, 5)

            def attention_t(g, r):
                proj_piece(r, 0)
                pe.wait_ge(qkv_made, 3 * g + 3)
                for t in range(TT):
                    for h, w in enumerate((P, HEAD, HEAD, HEAD)):
                        mm = pe.transpose(bank[2 + t][0:w, h * P:(h + 1) * P],
                                          qkv[:, t, h * HEAD:h * HEAD + w], ident[:])
                    mm.then_inc(qkT_full, 1)
                for t in range(TT):
                    mm = pe.transpose(bank[4][0:HEAD, t * P:(t + 1) * P], qkv[:, t, 4 * HEAD:5 * HEAD], ident[:])
                mm.then_inc(qkT_full, 1)

                def scores():
                    pe.wait_ge(qkT_made, 3 * g + 3)
                    for b in range(2):
                        for c2 in range(2):
                            c = 2 * b + c2
                            for rr in range(2):
                                o = (c2 * 2 + rr) * P
                                q = qT[:, c, 2 * rr:2 * rr + 2, :].rearrange("p h q -> p (h q)")
                                spans = {0: [(0, 0, CHUNK)], 1: [(0, 0, P)], 3: [(0, P, 2 * P)],
                                         2: [(0, P, P + CHUNK), (CHUNK, CHUNK, P)]}[c]
                                for off, k0, k1 in spans:
                                    mm = pe.matmul(bank[5 + b][:, o + off:o + off + k1 - k0], q, kT[:, k0:k1],
                                                   start=True, stop=True)
                        mm.then_inc(sc_full, 1)

                def turn_probs():
                    for b in range(2):
                        pe.wait_ge(prob_made, 2 * g + b + 1)
                        dst = bank[7 if b == 0 else 2]
                        for tile in (2, 3, 0, 1):
                            w = CHUNK if b == 0 and tile < 2 else P
                            mm = pe.transpose(dst[0:w, tile * P:(tile + 1) * P], prob[b][:, tile, 0:w], ident[:])
                        mm.then_inc(pT_full, 1)

                proj_piece(r, 1, scores)
                proj_piece(r, 2)
                proj_piece(r, 3, turn_probs)
                pe.wait_ge(vmid_made, 2 * g + 2)
                for b in range(2):
                    pe.wait_ge(pT_made, 3 * g + 2 + b)
                    for tile in (2, 3, 0, 1):
                        c = 2 * b + tile // 2
                        w = CHUNK if c == 0 else P
                        v = {0: qkv[0:CHUNK, 0, 5 * HEAD:6 * HEAD], 1: qkv[:, 0, 5 * HEAD:6 * HEAD],
                             2: vmid[:], 3: qkv[:, 1, 5 * HEAD:6 * HEAD]}[c]
                        mm = pe.matmul(bank[3 + b][0:HEAD, tile * P:(tile + 1) * P], v, probT[b][0:w, tile, :],
                                       start=True, stop=True)
                    mm.then_inc(ya_t_full, 1)

            with pe.Fori(0, NKV) as g:
                attention_t(g, A1 + g)

            def turn_merged(n):
                pe.wait_ge(gyb_made, 2 * n + 2)
                for t in range(TT):
                    for q in range(4):
                        c0 = (4 * n + q) * P
                        mm = pe.transpose(bank[2 * n + t][:, q * P:(q + 1) * P], merged[:, t, c0:c0 + P], ident[:])
                    mm.then_inc(mT_full, 1)

            def rounds_t(n, r, first, last=False):
                for k in range(ROUND):
                    dense_piece(r, k, 0, actT_hi, actT_lo, 4 * k, k == 0, k == 3,
                                     (acc_free, 2 * (A1 + A2) + 2 * n), acc_full)
                    if first and k == 2:
                        pe.wait_ge(yaT_hi_made, NKV)
                        for t in range(TT):
                            pe.wait_ge(vn_made, t + 1)
                            for gg in range(2):
                                for g in range(4):
                                    ch = 4 * gg + g
                                    mm = pe.matmul(bank[4 + 2 * t + gg][:, g * P:(g + 1) * P], wspT[:, ch, :],
                                                   proj[:, t, VS_OFF + ch * P:VS_OFF + (ch + 1) * P],
                                                   start=True, stop=True)
                                mm.then_inc(mix_full, 1)
                for k in range(ROUND):
                    dense_piece(r + 1, k, 2, actT_hi, actT_lo, 4 * k, k == 0, k == 3,
                                     (gb_free, 2 * n), gb_full)
                    if first and k == 1:
                        for t in range(TT):
                            pe.wait_ge(yb_made, SG * (t + 1) if t == 0 else TT * SG)
                            for k4 in range(2):
                                for q in range(4):
                                    c0 = U_OFF + (4 * k4 + q) * P
                                    mm = pe.transpose(bank[4 + 2 * t + k4][:, q * P:(q + 1) * P],
                                                      proj[:, t, c0:c0 + P], ident[:])
                                mm.then_inc(ybT_full, 1)
                if first:
                    pe.wait_ge(yaT_lo_made, NKV)
                    pe.wait_ge(ybT_lo_made, 4)
                for k in range(2):
                    dense_piece(r + 2, k, 4, yaT_hi, yaT_lo, 4 * k, k == 0, k == 1, (ya_free, 2 * n), ya_full)
                if last:
                    pe.wait_ge(acc_free, 2 * (A1 + A2 + NC) + 2)
                    turn_merged(0)
                    pe.wait_ge(gb_free, 2 * NC + 2)
                    turn_merged(1)
                for k in range(2):
                    dense_piece(r + 2, 2 + k, 6, ybT_hi, ybT_lo, 4 * k, k == 0, k == 1, (yb_free, 2 * n), yb_full)

            rounds_t(0, C_ROUND0, True)
            with pe.Fori(1, NC - 1) as n:
                rounds_t(n, 3 * n + C_ROUND0, False)
            rounds_t(NC - 1, D_ROUND0 - 3, False, last=True)

            def out_piece(n, k):
                dense_piece(n + D_ROUND0, k, 0, actT_hi, actT_lo, 4 * k, k == 0, k == 3,
                            (acc_free, 2 * (A1 + A2 + NC) + 2 * n), acc_full)

            def turn_residual(t, src, c0):
                for q in range(4):
                    mm = pe.transpose(bank[2 + t][:, q * P:(q + 1) * P], src[:, t, c0 + q * P:c0 + (q + 1) * P], ident[:])
                mm.then_inc(hT_h_full, 1)

            def route(n):
                for t in range(TT):
                    pe.wait_ge(hT_h_made, 2 * n + 2 + t + 1)
                    for q in range(4):
                        mm = pe.matmul(bank[4][:, t * NR:(t + 1) * NR], hT[:, q, t * P:(t + 1) * P],
                                       wr[:, bass.ds(4 * n + q, 1), :].rearrange("p a n -> p (a n)"),
                                       start=(q == 0), stop=(q == 3))
                mm.then_inc(lg_full, 1)

            pe.wait_ge(ya_free, 2 * NC + 2)
            turn_merged(2)
            pe.wait_ge(mT_lo_made, 4)
            out_piece(0, 0)
            pe.wait_ge(yb_free, 2 * NC + 2)
            turn_merged(3)
            out_piece(0, 1)
            pe.wait_ge(mT_lo_made, 6)
            out_piece(0, 2)
            pe.wait_ge(mT_lo_made, 8)
            out_piece(0, 3)
            pe.wait_ge(wr_made, 1)
            with pe.Fori(1, NC) as n:
                out_piece(n, 0)
                out_piece(n, 1)
                for t in range(TT):
                    pe.wait_ge(h_chunk_made, 2 * n - 1 + t)
                    turn_residual(t, h_chunk, 0)
                out_piece(n, 2)
                pe.wait_ge(lgs_made, 2 * n)
                route(n - 1)
                out_piece(n, 3)

            for t in range(TT):
                pe.wait_ge(acc_free, 2 * (A1 + A2 + NC) + 2 + 2 * (NC - 1) + t + 1)
                turn_residual(t, resid, (NC - 1) * COLS)
            pe.wait_ge(lgs_made, 2 * NC)
            route(NC - 1)
            pe.wait_ge(lo_made, DENSE_RAW + DENSE + 1)
            keep_clock(12, whi[0][:, 0:COLS], bank[5][:])
            pe.wait_ge(goh_made, TT)
            pe.matmul(bank[2][:, 0:NG], before[:], goh[:, 0, :], start=True, stop=True).then_inc(rank_full, 1)
            pe.matmul(bank[3][:, 0:NG], before[:], goh[:, 1, :], start=True, stop=False)
            pe.matmul(bank[3][:, 0:NG], ones[:], goh[:, 0, :], start=False, stop=True).then_inc(rank_full, 1)
            pe.matmul(bank[4][:, 0:NG], ones[:], goh[:, 0, :], start=True, stop=False)
            pe.matmul(bank[4][:, 0:NG], ones[:], goh[:, 1, :], start=False, stop=True).then_inc(rank_full, 1)

            keep_clock(6, whi[0][:, 0:COLS], bank[5][:])

            def gu_piece(i, j, q):
                m = 6 * j - 2 + q
                s = (4 + q) % EXP_PARTS
                pe.wait_ge(lo_made, DENSE_RAW + DENSE + PER_G * i + m + 1)
                w_hi = whi[s][:].rearrange("p (u k f) -> p u k f", u=2, k=4)
                w_lo = wlo[s][:].rearrange("p (u k f) -> p u k f", u=2, k=4)
                return w_hi, w_lo

            def gate_up(i, j, q0):
                if q0 == 0:
                    pe.wait_ge(hid_made, EPG * i + j)
                for k4 in range(4):
                    if q0:
                        pe.wait_ge(xg_lo_made, 4 * i + max(k4, 2) + 1)
                    w_hi, w_lo = gu_piece(i, j, q0 + k4)
                    for k in range(4):
                        kt = 4 * k4 + k
                        mm = three(bank[0][:], xg_hi[:, kt, :], xg_lo[:, kt, :], w_hi[:, :, k, :], w_lo[:, :, k, :],
                                   kt == 0, kt == KT - 1)
                    mm.then_inc(piece_used, 1)

            def down(i, j, start, stop):
                pe.wait_ge(hT_lo_made, EPG * i + j)
                for f in range(2):
                    m = 6 * j + 2 + f
                    q = 4 + f if not stop else f
                    if stop:
                        m = 6 * j - 2 + f
                    s = (4 + q) % EXP_PARTS
                    pe.wait_ge(lo_made, DENSE_RAW + DENSE + PER_G * i + m + 1)
                    for b in range(4):
                        cols = slice(b * COLS, (b + 1) * COLS)
                        mm = three(bank[2 + b][:], hT_hi[:, f, :], hT_lo[:, f, :], whi[s][:, cols], wlo[s][:, cols],
                                   start and f == 0, stop and f == 1)
                        if stop and f == 1 and b < 3:
                            mm.then_inc(o_full, 1)
                    mm.then_inc(piece_used, 1)

            def turn_hidden(i, j):
                pe.wait_ge(hid_made, EPG * i + j + 1)
                for f in range(2):
                    mm = pe.transpose(bank[1][:, f * P:(f + 1) * P], hid[:, f * P:(f + 1) * P], ident[:])
                mm.then_inc(hT_full, 1)

            def gather(i, chunks):
                pe.wait_ge(sel_made, TT * i + 2)
                for k4 in chunks:
                    b = GATHER_BANKS[k4]
                    if k4 == 3:
                        pe.wait_ge(xg_lo_made, 4 * i + 1)
                    for q in range(4):
                        kt = 4 * k4 + q
                        for t in range(TT):
                            mm = pe.matmul(bank[b][:, q * P:(q + 1) * P], hg[t][:, kt * P:(kt + 1) * P],
                                           sel[:, t, :], start=(t == 0), stop=(t == TT - 1))
                    mm.then_inc(xg_full, 1)

            def gather_weights(i):
                pe.wait_ge(xg_lo_made, 4 * i + 2)
                pe.wait_ge(ca_made, 2 * TT)
                for t in range(TT):
                    mm = pe.matmul(bank[7][:, 0:EPG + 2], sel[:, t, :], ca[:, t, :], start=(t == 0), stop=(t == TT - 1))
                mm.then_inc(cw_full, 1)

            def scatter(i, units, order):
                for u in units:
                    dst, b, t = order[u]
                    cols, tok = slice(b * COLS, (b + 1) * COLS), slice(t * P, (t + 1) * P)
                    pe.wait_ge(o_lo_made, 4 * i + max(b, dst - 2 if dst in OUT_BANKS else 0) + 1)
                    pe.matmul(bank[dst][:], selT[:, tok], o_hi[:, cols], start=True, stop=False)
                    pe.matmul(bank[dst][:], selT[:, tok], o_lo[:, cols], start=False, stop=True).then_inc(scat_full, 1)

            def group_t(i, after_another, another_follows):
                if not after_another:
                    if i == 0:
                        pe.wait_ge(hg_made, TT * NC)
                    gather(i, range(4))
                    gather_weights(i)
                gate_up(i, 0, 2)
                if after_another:
                    pe.wait_ge(selT_made, i)
                    pe.wait_ge(cw_made, i + 1)
                    scatter(i - 1, range(0, 6), SCATTER)
                turn_hidden(i, 0)
                gate_up(i, 1, 0)
                if after_another:
                    pe.wait_ge(added, 8 * (i - 1) + 6)
                    scatter(i - 1, range(6, 8), SCATTER)
                elif i == 0:
                    pe.wait_ge(ctl_made, 1)
                down(i, 1, True, False)
                turn_hidden(i, 1)
                if after_another:
                    pe.wait_ge(added, 8 * (i - 1) + 7)
                for t in range(TT):
                    mm = pe.transpose(bank[6][:, t * P:(t + 1) * P], sel[:, t, :], ident[:])
                mm.then_inc(selT_full, 1)
                with pe.Fori(2, EPG - 1) as j:
                    gate_up(i, j, 0)
                    down(i, j, False, False)
                    turn_hidden(i, j)
                gate_up(i, EPG - 1, 0)
                down(i, EPG - 1, False, False)
                if another_follows:
                    pe.wait_ge(selT_made, i + 1)
                    if after_another:
                        pe.wait_ge(added, 8 * i)
                    gather(i + 1, range(0, 2))
                turn_hidden(i, EPG - 1)
                if another_follows:
                    gather(i + 1, range(2, 4))
                    gather_weights(i + 1)
                down(i, EPG, False, True)
                if not another_follows:
                    pe.wait_ge(selT_made, i + 1)
                    scatter(i, range(8), SCATTER_LAST)

            group_t(0, False, True)
            with pe.Fori(1, NG - 1) as i:
                group_t(i, True, True)
            group_t(NG - 1, True, False)
            pe.wait_ge(ctl_made, 1)
            more = pe.value_load(ctl[0:1, 0:1], min_val=0, max_val=1)
            with pe.If(more == 1):
                group_t(NG, False, False)


_INS = ["x", "norm_mix_g", "w_in", "b_in", "attn_sinks", "norm_v_g", "w_spatial", "b_spatial", "w_gate", "b_gate",
        "w_branch_a", "w_branch_b", "w_out", "norm_ffn_g", "w_router_group", "b_router_group", "w_router_expert",
        "b_router_expert", "w_e_gate", "w_e_up", "w_e_down", "norm_final_g"]


def kernel(**inputs):
    import numpy as _np
    import concourse.bacc as _bacc
    from concourse import mybir as _mybir
    from concourse.bass_utils import run_bass_kernel_spmd as _run

    nc = _bacc.Bacc("TRN2", target_bir_lowering=False, num_devices=1)
    arrays, views = {}, {}
    for name in _INS:
        v = _np.ascontiguousarray(inputs[name])
        arrays[f"in_{name}"] = v
        views[name] = nc.dram_tensor(f"in_{name}", v.shape, _mybir.dt.from_np(v.dtype), kind="ExternalInput").ap()
    x = arrays["in_x"]
    out = nc.dram_tensor("out_y", x.shape, _mybir.dt.from_np(x.dtype), kind="ExternalOutput").ap()
    build_trunk(nc, views, out)
    r = _run(nc, [arrays], core_ids=[0])
    return r.results[0]["out_y"]
```
